# Optimizing a Trainium2 kernel written in Bass

```python
import jax, jax.numpy as jnp
from jax import lax
import numpy as np

D_MODEL = 1024
BATCH = 1
SEQ = 256
DEPTH = 1

POOL_WIDTH = D_MODEL // 2
POOL_WINDOWS = (2, 4, 8, 16)
N_POOL_GROUPS = len(POOL_WINDOWS)
POOL_GROUP = POOL_WIDTH // N_POOL_GROUPS
N_HEADS = 8
HEAD_DIM = 64
ATTN_WIDTH = N_HEADS * HEAD_DIM
MOBA_BLOCK = 256
MOBA_TOPK = 3
Q_CHUNK = 32
D_FF = 4 * D_MODEL
N_BRANCHES = 2
IN_WIDTH = POOL_WIDTH + 3 * ATTN_WIDTH + N_BRANCHES * D_MODEL
EPS = 1e-6
NEG = -1e30


def rmsnorm(x, g):
    xf = x.astype(jnp.float32)
    y = xf * lax.rsqrt(jnp.mean(xf * xf, axis=-1, keepdims=True) + EPS) * g.astype(jnp.float32)
    return y.astype(x.dtype)

def alibi_slopes(n_heads):
    return jnp.asarray(2.0 ** (-8.0 * np.arange(1, n_heads + 1) / n_heads), dtype=jnp.float32)

def pool_mixer(p, pool_w, pool_scale):
    pf = p.astype(jnp.float32)
    B, S, _ = pf.shape
    cs = jnp.concatenate([jnp.zeros_like(pf[:, :1]), jnp.cumsum(pf, axis=1)], axis=1)
    t = jnp.arange(S)
    outs = []
    for g, w in enumerate(POOL_WINDOWS):
        sl = slice(g * POOL_GROUP, (g + 1) * POOL_GROUP)
        lo = jnp.maximum(t + 1 - w, 0)
        win_sum = cs[:, 1:, sl] - cs[:, lo, sl]
        count = jnp.minimum(t + 1, w).astype(jnp.float32)[None, :, None]
        outs.append(win_sum / count - pf[:, :, sl])
    y = jnp.stack(outs, axis=2)
    y = jnp.einsum('bsgc,gcd->bsgd', y, pool_w.astype(jnp.float32))
    y = y.reshape(B, S, POOL_WIDTH) * pool_scale.astype(jnp.float32)
    return y.astype(p.dtype)

def moba_attention(q, k, v):
    B, S, H, Dh = q.shape
    nb = -(-S // MOBA_BLOCK)
    s_pad = nb * MOBA_BLOCK
    qf = q.transpose(0, 2, 1, 3).astype(jnp.float32) * (HEAD_DIM ** -0.5)
    pad = ((0, 0), (0, 0), (0, s_pad - S), (0, 0))
    kf = jnp.pad(k.transpose(0, 2, 1, 3).astype(jnp.float32), pad)
    vf = jnp.pad(v.transpose(0, 2, 1, 3).astype(jnp.float32), pad)
    kb = kf.reshape(B, H, nb, MOBA_BLOCK, Dh)
    vb = vf.reshape(B, H, nb, MOBA_BLOCK, Dh)
    slope = alibi_slopes(H)[None, :, None, None]
    t = jnp.arange(S)
    qblk = t // MOBA_BLOCK
    k_sel = min(MOBA_TOPK, nb - 1)
    if k_sel > 0:
        kmean = jnp.mean(kb, axis=3)
        gate = jnp.einsum('bhsd,bhnd->bhsn', qf, kmean)
        past = jnp.arange(nb)[None, :] < qblk[:, None]
        gate = jnp.where(past[None, None], gate, NEG)
        _, sel = lax.top_k(gate, k_sel)
    else:
        sel = jnp.zeros((B, H, S, 0), dtype=jnp.int32)
    n_chunks = S // Q_CHUNK
    q_c = qf.reshape(B, H, n_chunks, Q_CHUNK, Dh).transpose(2, 0, 1, 3, 4)
    sel_c = sel.reshape(B, H, n_chunks, Q_CHUNK, k_sel).transpose(2, 0, 1, 3, 4)
    bi = jnp.arange(B)[:, None, None]
    hi = jnp.arange(H)[None, :, None]
    kpos_in = jnp.arange(MOBA_BLOCK)

    def chunk_attn(args):
        c, qc, selc = args
        tq = c * Q_CHUNK + jnp.arange(Q_CHUNK)
        own = (c * Q_CHUNK) // MOBA_BLOCK
        k_own = lax.dynamic_slice_in_dim(kf, own * MOBA_BLOCK, MOBA_BLOCK, axis=2)
        v_own = lax.dynamic_slice_in_dim(vf, own * MOBA_BLOCK, MOBA_BLOCK, axis=2)
        ks = own * MOBA_BLOCK + kpos_in
        dist = (tq[:, None] - ks[None, :]).astype(jnp.float32)
        s_own = jnp.einsum('bhqd,bhkd->bhqk', qc, k_own) - slope * dist[None, None]
        s_own = jnp.where((ks[None, :] <= tq[:, None])[None, None], s_own, NEG)
        scores = [s_own]
        idxs = []
        for j in range(k_sel):
            idx = selc[..., j]
            kg = kb[bi, hi, idx]
            kpos = idx[..., None] * MOBA_BLOCK + kpos_in
            d = (tq[None, None, :, None] - kpos).astype(jnp.float32)
            s = jnp.einsum('bhqd,bhqkd->bhqk', qc, kg) - slope * d
            s = jnp.where((idx < own)[..., None], s, NEG)
            scores.append(s)
            idxs.append(idx)
        p = jax.nn.softmax(jnp.concatenate(scores, axis=-1), axis=-1)
        out = jnp.einsum('bhqk,bhkd->bhqd', p[..., :MOBA_BLOCK], v_own)
        for j, idx in enumerate(idxs):
            vg = vb[bi, hi, idx]
            pj = p[..., (j + 1) * MOBA_BLOCK:(j + 2) * MOBA_BLOCK]
            out = out + jnp.einsum('bhqk,bhqkd->bhqd', pj, vg)
        return out

    out = lax.map(chunk_attn, (jnp.arange(n_chunks), q_c, sel_c))
    out = out.transpose(1, 0, 3, 2, 4).reshape(B, S, H * Dh)
    return out.astype(q.dtype)

def first_inputs(seed: int = 0) -> dict:
    key = jax.random.key(seed)
    ks = jax.random.split(key, 16)
    f32 = jnp.float32

    def nrm(k, shape, fan_in):
        return jax.random.normal(k, shape, f32) * (fan_in ** -0.5)

    def gain(k, shape):
        return 1.0 + 0.02 * jax.random.normal(k, shape, f32)

    L = DEPTH
    return {
        "x": jax.random.normal(ks[0], (BATCH, SEQ, D_MODEL), f32),
        "norm_mix_pre": gain(ks[1], (L, D_MODEL)),
        "w_in": nrm(ks[2], (L, D_MODEL, IN_WIDTH), D_MODEL),
        "b_gate": 0.01 * jax.random.normal(ks[3], (L, N_BRANCHES * D_MODEL), f32),
        "pool_w": nrm(ks[4], (L, N_POOL_GROUPS, POOL_GROUP, POOL_GROUP), POOL_GROUP),
        "pool_scale": gain(ks[5], (L, POOL_WIDTH)),
        "w_branch_pool": nrm(ks[6], (L, POOL_WIDTH, D_MODEL), POOL_WIDTH),
        "w_branch_attn": nrm(ks[7], (L, ATTN_WIDTH, D_MODEL), ATTN_WIDTH),
        "w_out": nrm(ks[8], (L, D_MODEL, D_MODEL), D_MODEL),
        "norm_mix_post": gain(ks[9], (L, D_MODEL)),
        "norm_mlp_pre": gain(ks[10], (L, D_MODEL)),
        "w_up": nrm(ks[11], (L, D_MODEL, D_FF), D_MODEL),
        "w_down": nrm(ks[12], (L, D_FF, D_MODEL), D_FF),
        "norm_mlp_post": gain(ks[13], (L, D_MODEL)),
    }

def first_block(x, norm_mix_pre, w_in, b_gate, pool_w, pool_scale, w_branch_pool, w_branch_attn, w_out,
              norm_mix_post, norm_mlp_pre, w_up, w_down, norm_mlp_post):
    B, S, _ = x.shape
    h = x
    o_q = POOL_WIDTH
    o_k = o_q + ATTN_WIDTH
    o_v = o_k + ATTN_WIDTH
    o_g = o_v + ATTN_WIDTH
    for l in range(DEPTH):
        u = rmsnorm(h, norm_mix_pre[l])
        z = u @ w_in[l]
        p = z[..., :o_q]
        q = z[..., o_q:o_k].reshape(B, S, N_HEADS, HEAD_DIM)
        k = z[..., o_k:o_v].reshape(B, S, N_HEADS, HEAD_DIM)
        v = z[..., o_v:o_g].reshape(B, S, N_HEADS, HEAD_DIM)
        g = z[..., o_g:] + b_gate[l]
        g_pool, g_attn = g[..., :D_MODEL], g[..., D_MODEL:]
        y_pool = pool_mixer(p, pool_w[l], pool_scale[l]) @ w_branch_pool[l]
        y_attn = moba_attention(q, k, v) @ w_branch_attn[l]
        m = jax.nn.sigmoid(g_pool) * y_pool + jax.nn.sigmoid(g_attn) * y_attn
        h = h + rmsnorm(m @ w_out[l], norm_mix_post[l])
        u2 = rmsnorm(h, norm_mlp_pre[l])
        a = jnp.square(jax.nn.relu(u2 @ w_up[l]))
        h = h + rmsnorm(a @ w_down[l], norm_mlp_post[l])
    return h


DEPTH_2 = 2

MIX_WIDTH = D_MODEL
CONV_WIDTH = MIX_WIDTH // 2
ATT_WIDTH = MIX_WIDTH - CONV_WIDTH
N_ATT_HEADS = ATT_WIDTH // HEAD_DIM
N_CONV_GROUPS = CONV_WIDTH // HEAD_DIM
CONV_K = 3
N_MEM = 256
N_XHEADS = 4
XHEAD_DIM = D_MODEL // N_XHEADS
D_FF_2 = 2816
Q_BLOCK = 128
IN_COLS = 3 * CONV_WIDTH + 3 * ATT_WIDTH + N_ATT_HEADS
SPLITS = [CONV_WIDTH, 2 * CONV_WIDTH, 3 * CONV_WIDTH,
          3 * CONV_WIDTH + ATT_WIDTH, 3 * CONV_WIDTH + 2 * ATT_WIDTH,
          3 * CONV_WIDTH + 3 * ATT_WIDTH]


def rmsnorm_2(x, g):
    xf = x.astype(jnp.float32)
    y = xf * lax.rsqrt(jnp.mean(xf * xf, axis=-1, keepdims=True) + EPS)
    return (y * g.astype(jnp.float32)).astype(x.dtype)

def swiglu(h, w_gu, w_down):
    gate, up = jnp.split(h @ w_gu, 2, axis=-1)
    return (jax.nn.silu(gate) * up) @ w_down

def causal_depthwise_conv(u, w):
    kern = w[:, None, :].astype(u.dtype)
    return lax.conv_general_dilated(
        u, kern, window_strides=(1,), padding=[(CONV_K - 1, 0)],
        dimension_numbers=('NWC', 'WIO', 'NWC'), feature_group_count=u.shape[-1])

def forgetting_attention(q, k, v, log_f):
    B, S, H, Dh = q.shape
    nb = S // Q_BLOCK
    scale = Dh ** -0.5
    c = jnp.cumsum(log_f, axis=1).transpose(0, 2, 1)
    qb = q.reshape(B, nb, Q_BLOCK, H, Dh).transpose(1, 0, 3, 2, 4)
    cqb = c.reshape(B, H, nb, Q_BLOCK).transpose(2, 0, 1, 3)
    kpos = jnp.arange(S)

    def block(args):
        i, q_i, cq_i = args
        s = jnp.einsum('bhqd,bkhd->bhqk', q_i, k,
                       preferred_element_type=jnp.float32) * scale
        s = s + cq_i[..., None] - c[:, :, None, :]
        qpos = i * Q_BLOCK + jnp.arange(Q_BLOCK)
        mask = kpos[None, :] <= qpos[:, None]
        s = jnp.where(mask, s, -jnp.inf)
        p = jax.nn.softmax(s, axis=-1)
        return jnp.einsum('bhqk,bkhd->bqhd', p.astype(v.dtype), v)

    out = lax.map(block, (jnp.arange(nb), qb, cqb))
    return out.transpose(1, 0, 2, 3, 4).reshape(B, S, H * Dh)

def memory_cross_attention(h, m, w_q, w_kv, w_o):
    B, S, _ = h.shape
    M = m.shape[1]
    q = (h @ w_q).reshape(B, S, N_XHEADS, XHEAD_DIM)
    k, v = jnp.split(m @ w_kv, 2, axis=-1)
    k = k.reshape(B, M, N_XHEADS, XHEAD_DIM)
    v = v.reshape(B, M, N_XHEADS, XHEAD_DIM)
    s = jnp.einsum('bshd,bmhd->bhsm', q, k,
                   preferred_element_type=jnp.float32) * (XHEAD_DIM ** -0.5)
    p = jax.nn.softmax(s, axis=-1)
    o = jnp.einsum('bhsm,bmhd->bshd', p.astype(v.dtype), v).reshape(B, S, D_MODEL)
    return o @ w_o

def second_inputs(seed: int = 0) -> dict:
    key = jax.random.key(seed)
    ks = jax.random.split(key, 24)
    f32 = jnp.float32

    def w(k, shape, fan_in):
        return jax.random.normal(k, shape, f32) * (fan_in ** -0.5)

    def gain(k, shape):
        return 1.0 + 0.1 * jax.random.normal(k, shape, f32)

    return {
        "x": jax.random.normal(ks[0], (BATCH, SEQ, D_MODEL), f32),
        "mem": jax.random.normal(ks[1], (BATCH, N_MEM, D_MODEL), f32),
        "g_ffn1": gain(ks[2], (DEPTH_2, D_MODEL)),
        "w_ffn1_gu": w(ks[3], (DEPTH_2, D_MODEL, 2 * D_FF_2), D_MODEL),
        "w_ffn1_down": w(ks[4], (DEPTH_2, D_FF_2, D_MODEL), D_FF_2),
        "g_mix": gain(ks[5], (DEPTH_2, D_MODEL)),
        "w_mix_in": w(ks[6], (DEPTH_2, D_MODEL, IN_COLS), D_MODEL),
        "w_conv": w(ks[7], (DEPTH_2, CONV_K, CONV_WIDTH), CONV_K),
        "b_f": 2.0 + 0.5 * jax.random.normal(ks[8], (DEPTH_2, N_ATT_HEADS), f32),
        "g_conv_out": gain(ks[9], (DEPTH_2, CONV_WIDTH)),
        "g_att_out": gain(ks[10], (DEPTH_2, ATT_WIDTH)),
        "w_mix_out": w(ks[11], (DEPTH_2, MIX_WIDTH, D_MODEL), MIX_WIDTH),
        "g_xattn": gain(ks[12], (DEPTH_2, D_MODEL)),
        "g_mem": gain(ks[13], (DEPTH_2, D_MODEL)),
        "w_xq": w(ks[14], (DEPTH_2, D_MODEL, D_MODEL), D_MODEL),
        "w_xkv": w(ks[15], (DEPTH_2, D_MODEL, 2 * D_MODEL), D_MODEL),
        "w_xo": w(ks[16], (DEPTH_2, D_MODEL, D_MODEL), D_MODEL),
        "g_ffn2": gain(ks[17], (DEPTH_2, D_MODEL)),
        "w_ffn2_gu": w(ks[18], (DEPTH_2, D_MODEL, 2 * D_FF_2), D_MODEL),
        "w_ffn2_down": w(ks[19], (DEPTH_2, D_FF_2, D_MODEL), D_FF_2),
        "g_final": gain(ks[20], (D_MODEL,)),
    }

def second_block(x, mem, g_ffn1, w_ffn1_gu, w_ffn1_down, g_mix, w_mix_in, w_conv, b_f,
              g_conv_out, g_att_out, w_mix_out, g_xattn, g_mem, w_xq, w_xkv, w_xo,
              g_ffn2, w_ffn2_gu, w_ffn2_down, g_final):
    B, S, _ = x.shape
    for l in range(DEPTH_2):
        x = x + 0.5 * swiglu(rmsnorm_2(x, g_ffn1[l]), w_ffn1_gu[l], w_ffn1_down[l])

        h = rmsnorm_2(x, g_mix[l])
        z = h @ w_mix_in[l]
        zb, zc, zv, zq, zk, zval, zf = jnp.split(z, SPLITS, axis=-1)

        y_conv = zb * causal_depthwise_conv(zc * zv, w_conv[l])

        log_f = jax.nn.log_sigmoid((zf + b_f[l]).astype(jnp.float32))
        q = zq.reshape(B, S, N_ATT_HEADS, HEAD_DIM)
        k = zk.reshape(B, S, N_ATT_HEADS, HEAD_DIM)
        v = zval.reshape(B, S, N_ATT_HEADS, HEAD_DIM)
        y_att = forgetting_attention(q, k, v, log_f)

        y = jnp.concatenate([rmsnorm_2(y_conv, g_conv_out[l]),
                             rmsnorm_2(y_att, g_att_out[l])], axis=-1)
        x = x + y @ w_mix_out[l]

        x = x + memory_cross_attention(rmsnorm_2(x, g_xattn[l]), rmsnorm_2(mem, g_mem[l]),
                                       w_xq[l], w_xkv[l], w_xo[l])

        x = x + 0.5 * swiglu(rmsnorm_2(x, g_ffn2[l]), w_ffn2_gu[l], w_ffn2_down[l])
    return rmsnorm_2(x, g_final)


def setup_inputs(seed=0):
    out = dict(first_inputs(seed))
    for name, value in second_inputs(seed + 1).items():
        if name != "x":
            out[name + "_2"] = value
    return out


def reference(
    x, norm_mix_pre, w_in, b_gate, pool_w, pool_scale, w_branch_pool, w_branch_attn, w_out,
    norm_mix_post, norm_mlp_pre, w_up, w_down, norm_mlp_post, mem_2, g_ffn1_2, w_ffn1_gu_2,
    w_ffn1_down_2, g_mix_2, w_mix_in_2, w_conv_2, b_f_2, g_conv_out_2, g_att_out_2, w_mix_out_2,
    g_xattn_2, g_mem_2, w_xq_2, w_xkv_2, w_xo_2, g_ffn2_2, w_ffn2_gu_2, w_ffn2_down_2,
    g_final_2,
):
    x = first_block(
        x, norm_mix_pre, w_in, b_gate, pool_w, pool_scale, w_branch_pool, w_branch_attn, w_out,
        norm_mix_post, norm_mlp_pre, w_up, w_down, norm_mlp_post,
    )
    return second_block(
        x, mem_2, g_ffn1_2, w_ffn1_gu_2, w_ffn1_down_2, g_mix_2, w_mix_in_2, w_conv_2, b_f_2,
        g_conv_out_2, g_att_out_2, w_mix_out_2, g_xattn_2, g_mem_2, w_xq_2, w_xkv_2, w_xo_2,
        g_ffn2_2, w_ffn2_gu_2, w_ffn2_down_2, g_final_2,
    )


_drawn_inputs = setup_inputs


def setup_inputs(seed=0):
    import zlib

    import numpy as np

    out = dict(_drawn_inputs(seed))
    spreads = {}
    factors = {'b_gate': 8.0,
     'pool_scale': 2.986,
     'norm_mix_post': 2.843,
     'norm_mlp_pre': 3.272,
     'norm_mlp_post': 3.352,
     'g_xattn_2': 7.108,
     'g_mem_2': 4.807}
    for name, (base, spread) in spreads.items():
        noise = np.random.default_rng([zlib.crc32(name.encode()), seed]).standard_normal(out[name].shape)
        drawn = base * np.exp(spread * noise) if base else spread * noise
        out[name] = __import__('jax').numpy.asarray(drawn.astype(out[name].dtype))
    for name, factor in factors.items():
        out[name] = (out[name] * factor).astype(out[name].dtype)
    return out
```

```python
from contextlib import ExitStack

import numpy as np

import concourse.bass as bass
from concourse import mybir

F32 = mybir.dt.float32
F32R = mybir.dt.float32r
ALU = mybir.AluOpType
ACT = mybir.ActivationFunctionType
AX = mybir.AxisListType

P = 128
D = 1024
S = 256
TOK = S // P
KT = D // P
BT = KT // 2
HEADS, DH = 8, 64
PAIRS = HEADS // 2
XH, XDH = 4, 256
POOL_WINDOWS = (2, 4, 8, 16)
LAYERS = 2
EPS = 1e-6
NEG = -1e30
BIG = 3e38

UNIT = 2048
RING = 3
TRI = 3 * P

B1_IN, B1_BRANCH, B1_OUT = 16, 4, 8 // 2
B1_FB = 8
B1_MLP = 4 * B1_FB
B1_UNITS = B1_IN + B1_BRANCH + B1_OUT + B1_MLP
FB = 11
FFN = 3 * FB
MID = 33
LAYER = 2 * FFN + MID
TOTAL = B1_UNITS + LAYERS * LAYER
AHEAD = TOTAL + 2
assert LAYER % RING == 0 and MID % RING == 0 and FFN % RING == 0

C_MIXPRE, C_MLPPRE, C_PSCALE, C_B1 = 0, 8, 16, 20
L_FFN1, L_MIX, L_MEM, L_XAT, L_FFN2, L_CONV, L_ATT, L_WCONV, L_BF, L_COLS = 0, 8, 16, 24, 32, 40, 44, 48, 60, 68

B1_PE = ["pool_mean", "pool_mix", "Tq", "Tk", "S0", "PT0", "PV0", "S1", "PT1", "PV1", "S2", "PT2",
         "PV2", "S3", "PT3", "PV3", "To"]
B1_ACT = ["p", "q", "ypT_hi", "qT", "v", "exp0", "exp1", "exp2", "exp3",
          "sig0", "sig1", "sig2", "sig3", "oT_hi"]
B1_DVE = ["yT", "ypT_lo", "k", "kT", "soft0", "gate0", "rinv0", "PT0", "O0", "soft1", "gate1", "rinv1", "PT1",
          "O1", "soft2", "gate2", "rinv2", "PT2", "O2", "soft3", "gate3", "rinv3", "PT3", "O3", "oT_lo",
          "m1", "m2h0", "mh0", "m2h1", "mh1", "postmix_h0", "postmix_h1", "postmlp_h0", "postmlp_h1"]
L_PE = ["Tq", "Tk", "cT", "S0", "PT0", "PV0", "S1", "PT1", "Tu", "PV1", "S2", "PT2", "PV2", "S3", "PT3",
        "Tzb", "PV3", "To", "TK0", "TK1", "ssq", "TX0", "TX1", "SX0", "SX1", "SX2", "SX3",
        "PX0", "PX1", "PX2", "PX3", "OX0", "OX1"]
L_ACT = ["q", "qT", "fexp", "fln", "v", "zc", "exp0", "exp1", "uT", "zb", "exp2", "exp3", "yc_hi", "ysq", "K1",
         "oT_hi", "V1", "xq0", "xqT0", "xexp0", "xexp1", "xexp2", "xexp3", "PX0", "PX2"]
L_DVE = ["k", "f", "fabs", "logf", "kT", "cT", "pad", "soft0", "rinv0", "PT0", "u", "O0", "soft1", "rinv1", "PT1",
         "O1", "soft2", "cv0", "cv1", "cv2", "rinv2", "PT2", "K0", "O2", "soft3", "rinv3", "PT3", "y", "ycT_lo", "O3",
         "oT_lo", "V0", "KT0", "KT1", "ssq", "resconv", "xq1", "xqT1", "xm0", "xneg0", "xm1", "xneg1", "xm2", "xneg2",
         "xm3", "xneg3", "rinvx", "PX1", "PX3", "xo0", "xo1"]

class Steps:

    def __init__(self, sem, names):
        self.sem, self.names, self.at = sem, names, 0
        assert len(set(names)) == len(names), names

    def upto(self, name, layer=0):
        return layer * len(self.names) + self.names.index(name) + 1

    def one(self, name):
        assert self.names[self.at] == name, (self.names[self.at], name)
        self.at += 1
        return 1

    def closed(self):
        assert self.at == len(self.names), self.names[self.at:]


def program(nc, x, mem, stream, cols, consts, sel, poolmat, poolw, gate_bias, post_gain, final_gain, out):
    with ExitStack() as ctx:
        def sb(name, shape, dt=F32):
            return ctx.enter_context(nc.sbuf_tensor(name, shape, dt))

        def sem(name):
            return ctx.enter_context(nc.semaphore(name))

        res = sb("res", [P, TOK, D])
        xT_hi, xT_lo = sb("xT_hi", [P, KT, S], F32R), sb("xT_lo", [P, KT, S], F32R)
        raw = sb("raw", [P, RING, UNIT])
        w_hi, w_lo = sb("w_hi", [P, RING, UNIT], F32R), sb("w_lo", [P, RING, UNIT], F32R)
        sT_hi, sT_lo = sb("sT_hi", [P, 8, S], F32R), sb("sT_lo", [P, 8, S], F32R)
        cst = sb("cst", [P, P + TRI + TRI + S])
        ident = cst[:, 0:P]
        negdist = cst[:, P:P + TRI]
        mask = cst[:, P + TRI:P + 2 * TRI]
        upto = cst[:, P + 2 * TRI:P + 2 * TRI + S]
        selr = sb("selr", [HEADS, HEADS, P])
        ones = sb("ones", [P, 2])
        consts2 = sb("consts2", [P, 4, 2])
        colsA = sb("colsA", [P, C_B1 + LAYERS * L_COLS])
        colsL = sb("colsL", [P, L_COLS])
        gfin = sb("gfin", [P, D])
        scratch = sb("scratch", [P, D])
        stat = sb("stat", [P, 6, 6])
        soft = sb("soft", [P, 2, 16])
        xmax = sb("xmax", [P, 2, 8])
        rinv = sb("rinv", [P, 16])
        lf = sb("lf", [P, 5, 2, HEADS])
        cT = sb("cT", [HEADS, S])

        qk_tok = sb("qk_tok", [P, 2, TOK, 512])
        v_tok = sb("v_tok", [P, TOK, 512])
        qkT = sb("qkT", [P, 2, 4, S])
        Pb = sb("Pb", [P, 4, 512])
        PTb = sb("PTb", [P, 4, 512])
        cu = sb("cu", [P, 2, TOK, 512])
        zb_tok = sb("zb_tok", [P, TOK, 512])
        uT = sb("uT", [P, 4, 2 + S])
        accT = sb("accT", [P, 4, S])
        kTx = sb("kTx", [P, KT, S])
        Vx = sb("Vx", [P, TOK, D])

        q_tok, k_tok = qk_tok[:, 0], qk_tok[:, 1]
        qT, kT = qkT[:, 0], qkT[:, 1]
        zc_tok, u_tok = cu[:, 0], cu[:, 1]
        xq_tok = qk_tok[:, :, :, :].rearrange("p a t n -> p (a t n)").rearrange("p (t n) -> p t n", t=TOK)
        xqT = qkT[:, :, :, :].rearrange("p a k n -> p (a k) n")
        K_tok = cu[:, :, :, :].rearrange("p a t n -> p (a t n)").rearrange("p (t n) -> p t n", t=TOK)
        mem_tok = kTx[:, :, :].rearrange("p k n -> p (k n)").rearrange("p (t n) -> p t n", t=TOK)
        o_tok, ysq = q_tok, k_tok.rearrange("p t n -> p (t n)").rearrange("p (c n) -> p c n", c=4)
        gate_act, hid = (Pb[:, i, :].rearrange("p (t n) -> p t n", t=TOK) for i in range(2))
        gates = [None] * 4
        gates[0] = kTx[:, 0:4, :].rearrange("p k n -> p (k n)").rearrange("p (t n) -> p t n", t=TOK)
        gates[1] = kTx[:, 4:8, :].rearrange("p k n -> p (k n)").rearrange("p (t n) -> p t n", t=TOK)
        gates[2] = Vx[:, 0, :].rearrange("p (t n) -> p t n", t=TOK)
        gates[3] = Vx[:, 1, :].rearrange("p (t n) -> p t n", t=TOK)
        gbias = cu[:, :, :, :].rearrange("p a t n -> p (a t n)")
        p_tok = PTb[:, 0:2, :]
        yT = PTb[:, 2:4, :].rearrange("p a n -> p (a n)").rearrange("p (c n) -> p c n", c=4)
        pmat = zb_tok[:, :, :].rearrange("p t n -> p (t n)")
        pmat2 = uT[:, :, :].rearrange("p c n -> p (c n)")
        pw = Pb[:, 0, :].rearrange("p (g n) -> p g n", g=4)
        alibi = [accT[:, :, :].rearrange("p c n -> p (c n)"), pmat]
        m_tok = Pb[:, :, :].rearrange("p a n -> p (a n)").rearrange("p (t n) -> p t n", t=TOK)
        gpost = qk_tok[:, :, :, :].rearrange("p a t n -> p (a t n)")
        relu = Pb[:, 0:2, :]
        sq = Pb[:, 2:4, :]
        out_tok = Vx

        ps = ctx.enter_context(nc.psum_tensor("ps", [P, 8, 512], F32))

        unit_landed = [sem(f"unit_landed{s}") for s in range(RING)]
        unit_hi, unit_lo, unit_used = sem("unit_hi"), sem("unit_lo"), sem("unit_used")
        x_in, cst_in, cols_in, pool_in, gbias_in, mem_in, gpost_in, gfin_in, out_sem = (
            sem(n) for n in ("x_in", "cst_in", "cols_in", "pool_in", "gbias_in", "mem_in", "gpost_in", "gfin_in", "out_sem"))
        set_ready = sem("set_ready")
        fin_ready = sem("fin_ready")
        half_ready = sem("half_ready")
        res_ready = sem("res_ready")
        turn_T = sem("turn_T")
        turn_hi, turn_lo = sem("turn_hi"), sem("turn_lo")
        sums = sem("sums")
        rstd = sem("rstd")
        cols_ready = sem("cols_ready")
        gate_ready, hid_ready, hid_T, hidT_hi, hidT_lo = (
            sem(n) for n in ("gate_ready", "hid_ready", "hid_T", "hidT_hi", "hidT_lo"))
        up_relu, up_sq, up_T, upT_hi, upT_lo = (sem(n) for n in ("up_relu", "up_sq", "up_T", "upT_hi", "upT_lo"))
        alibi_ready = sem("alibi_ready")
        b_pe, b_act, b_dve = Steps(sem("b_pe"), B1_PE), Steps(sem("b_act"), B1_ACT), Steps(sem("b_dve"), B1_DVE)
        l_pe, l_act, l_dve = Steps(sem("l_pe"), L_PE), Steps(sem("l_act"), L_ACT), Steps(sem("l_dve"), L_DVE)

        ST_X, ST_MEM, ST_WOUT, ST_NORM1, ST_MLP, ST_LAYER = range(6)
        ST_FFN1, ST_MIX, ST_ATT, ST_CONV, ST_XAT, ST_FFN2, NST = range(7)
        T_FFN, T_MEM, T_MIX, T_CONV, T_ATT, T_XAT = range(6)
        PER_LAYER_RES, PER_LAYER_TURN, PER_LAYER_HALF, PER_LAYER_SUMS = 16, 6 * BT, 4, 10

        def rstd_done(i):
            return 3 * i + 3

        def in_layer(l, i):
            return l * NST + (ST_LAYER + i)

        def rs(tile, t):
            return stat[:, tile, 4 + t:5 + t]

        def res_of(l, i):
            return l * PER_LAYER_RES + (8 + 4 * i + 4)

        def turns_before(l, i):
            return l * PER_LAYER_TURN + (3 + i) * BT

        def half_of(l, i):
            return l * PER_LAYER_HALF + (3 + i + 1)

        def sums_of(l, i):
            return l * PER_LAYER_SUMS + (10 + 2 * i + 2)

        def tiles_of(bank):
            return ps[:, bank, :].rearrange("p (k n) -> p k n", k=2)

        block = ctx.enter_context(nc.Block())

        def slot(c):
            return c % RING

        def landed(r3, c):
            return r3 * 16 + (c // RING + 1) * 16

        def upto_unit(r3, c):
            return r3 * RING + c + 1

        @block.sync
        def _(sp):
            def load(r3, c):
                if not (isinstance(r3, int) and 3 * r3 + c < RING):
                    sp.wait_ge(unit_lo, upto_unit(r3, c - RING))
                if isinstance(r3, int):
                    src = stream[(3 * r3 + c) % TOTAL]
                else:
                    src = stream[bass.ds(r3 * RING + c, 1)].rearrange("a p n -> p (a n)")
                sp.dma_start(raw[:, slot(c), :], src).then_inc(unit_landed[slot(c)], 16)

            for c in range(RING):
                load(0, c)
            whole = (TOTAL - RING) // RING
            with sp.Fori(0, whole) as r:
                for s in range(RING):
                    load(r, RING + s)
            for c in range(RING + whole * RING, AHEAD):
                load(0, c)
            for t in range(TOK):
                sp.wait_ge(fin_ready, t + 1)
                sp.dma_start(out[t], out_tok[:, t, :]).then_inc(out_sem, 16)
            sp.wait_ge(out_sem, 16 * TOK)
            for s in range(RING):
                sp.wait_ge(unit_landed[s], 16 * len(range(s, AHEAD, RING)))

        @block.tensor
        def _(pe):
            def mm(bank_ap, lh, rh, start, stop):
                return nc.tensor.matmul(bank_ap, lh, rh, start=start, stop=stop)

            def three(o, hi, lo, wh, wl, start, stop):
                nc.tensor.matmul(o, hi, wh, start=start, stop=False)
                nc.tensor.matmul(o, lo, wh, start=False, stop=False)
                return nc.tensor.matmul(o, hi, wl, start=False, stop=stop)

            def wide(r3, c, part, banks, tiles=None, hi=xT_hi, lo=xT_lo):
                pe.wait_ge(unit_lo, upto_unit(r3, c))
                wh = w_hi[:, slot(c), :].rearrange("p (k n) -> p k n", k=4)
                wl = w_lo[:, slot(c), :].rearrange("p (k n) -> p k n", k=4)
                for k in range(4):
                    kk = 4 * part + k
                    if tiles is not None and kk % 2 == 0:
                        pe.wait_ge(turn_lo, tiles + kk // 2 + 1)
                    for t in range(TOK):
                        last = three(ps[:, banks[t], :], hi[:, kk, t * P:(t + 1) * P], lo[:, kk, t * P:(t + 1) * P],
                                     wh[:, k, :], wl[:, k, :], kk == 0, kk == 7)
                last.then_inc(unit_used, 1)

            def tall(r3, c, k0, base, start, stop, hi, lo, signal_half=False, tiles=None):
                pe.wait_ge(unit_lo, upto_unit(r3, c))
                wh = w_hi[:, slot(c), :].rearrange("p (k n) -> p k n", k=2)
                wl = w_lo[:, slot(c), :].rearrange("p (k n) -> p k n", k=2)
                for half in range(2):
                    for k in range(2):
                        if tiles is not None and half == 0 and k == 0:
                            pe.wait_ge(turn_lo, tiles + k0 // 2 + 1)
                        for t in range(TOK):
                            cols_ = slice(half * 512, half * 512 + 512)
                            last = three(ps[:, base + 2 * half + t, :], hi[:, k0 + k, t * P:(t + 1) * P],
                                         lo[:, k0 + k, t * P:(t + 1) * P], wh[:, k, cols_], wl[:, k, cols_],
                                         start and k == 0, stop and k == 1)
                    if half == 0 and signal_half:
                        last.then_inc(half_ready, 1)
                last.then_inc(unit_used, 1)

            def turn(src, banks, wait=None):
                for k in range(KT):
                    if wait is not None:
                        wait(k)
                    for t in range(TOK):
                        last = nc.tensor.transpose(ps[:, banks[k // 2], (k % 2) * S + t * P:(k % 2) * S + (t + 1) * P],
                                                   src[:, t, k * P:(k + 1) * P], ident)
                    if k % 2 == 1:
                        last.then_inc(turn_T, 1)

            def turn_half(src, banks, k0):
                for k in range(4):
                    for t in range(TOK):
                        last = nc.tensor.transpose(ps[:, banks[k // 2], (k % 2) * S + t * P:(k % 2) * S + (t + 1) * P],
                                                   src[:, t, (k0 + k) * P:(k0 + k + 1) * P], ident)
                return last

            def scores(hp, forget):
                for e in range(2):
                    rows = slice(e * DH, e * DH + DH)
                    for t, (o0, nk) in enumerate(((0, P), (P, S))):
                        o = ps[:, 4 + e, o0:o0 + nk]
                        last = mm(o, qT[rows, hp, t * P:(t + 1) * P], kT[rows, hp, 0:nk], True, not forget)
                        if forget:
                            last = mm(o, selr[:, 2 * hp + e, :], cT[:, 0:nk], False, True)
                return last

            def prob_turn(hp):
                for e in range(2):
                    for b in range(3):
                        last = nc.tensor.transpose(ps[:, 4 + e, b * P:(b + 1) * P],
                                                   Pb[:, 2 * (hp % 2) + e, b * P:(b + 1) * P], ident)
                return last

            def values(hp):
                for e in range(2):
                    h = 2 * hp + e
                    pt = PTb[:, 2 * (hp % 2) + e, :]
                    c0 = TRI + e * DH
                    mm(ps[:, 4, c0:c0 + DH], pt[:, 0:P], v_tok[:, 0, h * DH:(h + 1) * DH], True, True)
                    mm(ps[:, 5, c0:c0 + DH], pt[:, P:2 * P], v_tok[:, 0, h * DH:(h + 1) * DH], True, False)
                    last = mm(ps[:, 5, c0:c0 + DH], pt[:, 2 * P:3 * P], v_tok[:, 1, h * DH:(h + 1) * DH], False, True)
                return last

            A, B, N = (0, 1), (2, 3), (4, 5, 6, 7)
            BB = lambda n: b_dve.upto(n)

            pe.wait_ge(cst_in, 16)
            pe.wait_ge(x_in, 16)
            turn(res, N)
            wide(0, 0, 0, A, tiles=0)
            wide(0, 1, 1, A, tiles=0)
            wide(0, 2, 0, B)
            pe.wait_ge(b_act.sem, b_act.upto("p"))
            pe.wait_ge(pool_in, 48)
            for g in range(4):
                o = ps[:, 6 + g // 2, (g % 2) * S:(g % 2) * S + S]
                pm = pmat if g < 2 else pmat2
                o0 = (g % 2) * TRI
                mm(o, p_tok[:, 0, g * P:(g + 1) * P], pm[:, o0:o0 + S], True, False)
                last = mm(o[:, P:S], p_tok[:, 1, g * P:(g + 1) * P], pm[:, o0 + S:o0 + TRI], False, True)
            last.then_inc(b_pe.sem, b_pe.one("pool_mean"))
            wide(0, 3, 1, B)
            wide(0, 4, 0, A)
            pe.wait_ge(b_dve.sem, BB("yT"))
            for g in range(4):
                last = mm(ps[:, 4 + g // 2, (g % 2) * S:(g % 2) * S + S], pw[:, g, :], yT[:, g, :], True, True)
            last.then_inc(b_pe.sem, b_pe.one("pool_mix"))
            wide(0, 5, 1, A)
            pe.wait_ge(b_act.sem, b_act.upto("q"))
            wide(0, 6, 0, B)
            turn_half(q_tok, (6, 7), 0).then_inc(b_pe.sem, b_pe.one("Tq"))
            wide(0, 7, 1, B)
            pe.wait_ge(b_dve.sem, BB("k"))
            turn_half(k_tok, (4, 5), 0).then_inc(b_pe.sem, b_pe.one("Tk"))
            for i in range(8):
                hp = i // 2
                if i == 2:
                    pe.wait_ge(b_act.sem, b_act.upto("v"))
                if i in (4, 6):
                    pe.wait_ge(b_dve.sem, BB(f"gate{hp - 2}"))
                wide(0, 8 + i, i % 2, (A, B)[hp % 2])
                if i % 2 == 0:
                    if hp:
                        pe.wait_ge(b_dve.sem, BB(f"PT{hp - 1}"))
                        values(hp - 1).then_inc(b_pe.sem, b_pe.one(f"PV{hp - 1}"))
                    else:
                        pe.wait_ge(b_act.sem, b_act.upto("qT"))
                        pe.wait_ge(b_dve.sem, BB("kT"))
                    scores(hp, False).then_inc(b_pe.sem, b_pe.one(f"S{hp}"))
                else:
                    pe.wait_ge(b_act.sem, b_act.upto(f"exp{hp}"))
                    prob_turn(hp).then_inc(b_pe.sem, b_pe.one(f"PT{hp}"))
            pe.wait_ge(b_dve.sem, BB("gate3"))
            tall(0, 16, 0, 0, True, False, sT_hi, sT_lo)
            pe.wait_ge(b_dve.sem, BB("PT3"))
            values(3).then_inc(b_pe.sem, b_pe.one("PV3"))
            tall(0, 17, 2, 0, False, True, sT_hi, sT_lo)
            pe.wait_ge(b_dve.sem, BB("O3"))
            turn_half(o_tok, (6, 7), 0).then_inc(b_pe.sem, b_pe.one("To"))
            pe.wait_ge(b_dve.sem, BB("oT_lo"))
            tall(0, 18, 4, 4, True, False, sT_hi, sT_lo)
            tall(0, 19, 6, 4, False, True, sT_hi, sT_lo, signal_half=True)
            turn(m_tok, (0, 1, 2, 3), wait=lambda k: pe.wait_ge(b_dve.sem, BB("mh0" if k < 4 else "mh1")))
            for i in range(4):
                tall(0, 20 + i, 2 * i, 4, i == 0, i == 3, xT_hi, xT_lo, tiles=BT, signal_half=(i == 3))

            turn(res, N, wait=lambda k: pe.wait_ge(res_ready, 2 if k < 4 else 4))

            def up_turn(jr, j, banks=B):
                pe.wait_ge(up_sq, jr + j + 1)
                turn_half(sq, banks, 0).then_inc(up_T, 1)

            def down1(r3, c, jr, j, start=False, stop=False):
                pe.wait_ge(upT_lo, jr + j + 1)
                tall(r3, c, 0, 4, start, False, sT_hi, sT_lo)
                tall(r3, c + 1, 2, 4, False, stop, sT_hi, sT_lo, signal_half=stop)

            c0 = B1_UNITS - B1_MLP
            wide(0, c0, 0, A, tiles=2 * BT)
            wide(0, c0 + 1, 1, A, tiles=2 * BT)
            wide(0, c0 + 2, 0, B)
            up_turn(0, 0, (4, 5))
            wide(0, c0 + 3, 1, B)
            down1(0, c0 + 4, 0, 0, start=True)
            up_turn(0, 1)
            with pe.Fori(0, 2) as r:
                for b in range(3):
                    c = c0 + 6 + 4 * b
                    wide(r * 4, c, 0, A)
                    wide(r * 4, c + 1, 1, A)
                    down1(r * 4, c + 2, r * 3, b + 1)
                    up_turn(r * 3, b + 2)
            down1(0, c0 + 30, 0, 7, stop=True)

            with pe.Fori(0, LAYERS) as l:
                def ffn(which, base):
                    L3 = l * (LAYER // 3)
                    fb = l * (2 * FB)
                    f0 = which * FB
                    before = res_of(l, -1 if which == 0 else 2)
                    turn(res, N, wait=lambda k: pe.wait_ge(res_ready, before - 2 if k < 4 else before))
                    tl = turns_before(l, 0 if which == 0 else 5)

                    def hid_turn(jr, j, bank=2):
                        pe.wait_ge(hid_ready, fb + jr + (f0 + j + 1))
                        for k in range(2):
                            for t in range(TOK):
                                last = nc.tensor.transpose(ps[:, bank, k * S + t * P:k * S + (t + 1) * P],
                                                           hid[:, t, k * P:(k + 1) * P], ident)
                        last.then_inc(hid_T, 1)

                    def down(r3, c, jr, j, start=False, stop=False):
                        pe.wait_ge(hidT_lo, fb + jr + (f0 + j + 1))
                        tall(r3, c, 0, 4, start, stop, sT_hi, sT_lo, signal_half=stop)

                    wide(L3, base, 0, A, tiles=tl)
                    wide(L3, base + 1, 1, A, tiles=tl)
                    wide(L3, base + 2, 0, B)
                    hid_turn(0, 0, 4)
                    wide(L3, base + 3, 1, B)
                    down(L3, base + 4, 0, 0, start=True)
                    hid_turn(0, 1)
                    with pe.Fori(1, FB - 1) as j:
                        wide(L3 + j, base + 2, 0, A)
                        wide(L3 + j, base + 3, 1, A)
                        down(L3 + j, base + 4, j, 0)
                        hid_turn(j, 1)
                    down(L3, base + FFN - 1, 0, FB - 1, stop=True)

                def wait_act(n):
                    pe.wait_ge(l_act.sem, l_act.upto(n, l))

                def wait_dve(n):
                    pe.wait_ge(l_dve.sem, l_dve.upto(n, l))

                ffn(0, B1_UNITS)

                L3 = l * (LAYER // 3)
                m0 = B1_UNITS + FFN
                turn(res, N, wait=lambda k: pe.wait_ge(res_ready, res_of(l, 0) - (2 if k < 4 else 0)))
                tl = turns_before(l, 1)
                wide(L3, m0, 0, A, tiles=tl)
                wide(L3, m0 + 1, 1, A, tiles=tl)
                wide(L3, m0 + 2, 0, B)
                wide(L3, m0 + 3, 1, B)
                pe.wait_ge(unit_lo, upto_unit(L3, m0 + 4))
                fh = w_hi[:, slot(m0 + 4), 0:KT * HEADS].rearrange("p (k n) -> p k n", k=KT)
                fl = w_lo[:, slot(m0 + 4), 0:KT * HEADS].rearrange("p (k n) -> p k n", k=KT)
                for k in range(KT):
                    for t in range(TOK):
                        last = three(ps[:, 4 + t, 0:HEADS], xT_hi[:, k, t * P:(t + 1) * P], xT_lo[:, k, t * P:(t + 1) * P],
                                     fh[:, k, :], fl[:, k, :], k == 0, k == KT - 1)
                last.then_inc(unit_used, 1)
                wait_act("q")
                wide(L3, m0 + 5, 0, A)
                turn_half(q_tok, (6, 7), 0).then_inc(l_pe.sem, l_pe.one("Tq"))
                wide(L3, m0 + 6, 1, A)
                wait_dve("f")
                turn_half(k_tok, (4, 5), 0).then_inc(l_pe.sem, l_pe.one("Tk"))
                wide(L3, m0 + 7, 0, B)
                wait_act("qT")
                wait_dve("logf")
                mm(ps[0:HEADS, 6, 0:S], lf[:, 4, 0, :], upto, True, False)
                mm(ps[0:HEADS, 6, P:S], lf[:, 4, 1, :], upto[:, 0:P], False, True).then_inc(l_pe.sem, l_pe.one("cT"))
                wide(L3, m0 + 8, 1, B)
                wait_dve("cT")
                scores(0, True).then_inc(l_pe.sem, l_pe.one("S0"))
                wait_act("v")
                wide(L3, m0 + 9, 0, A)
                wait_act("exp0")
                prob_turn(0).then_inc(l_pe.sem, l_pe.one("PT0"))
                wide(L3, m0 + 10, 1, A)
                wait_dve("PT0")
                values(0).then_inc(l_pe.sem, l_pe.one("PV0"))
                scores(1, True).then_inc(l_pe.sem, l_pe.one("S1"))
                wait_act("zc")
                wide(L3, m0 + 11, 0, B)
                wait_act("exp1")
                prob_turn(1).then_inc(l_pe.sem, l_pe.one("PT1"))
                wait_dve("u")
                turn_half(u_tok, (6, 7), 0).then_inc(l_pe.sem, l_pe.one("Tu"))
                wide(L3, m0 + 12, 1, B)
                wait_dve("PT1")
                values(1).then_inc(l_pe.sem, l_pe.one("PV1"))
                scores(2, True).then_inc(l_pe.sem, l_pe.one("S2"))
                pe.wait_ge(mem_in, l * 16 + 32)

                def mem_wait(k):
                    if k == 0:
                        wait_act("uT")
                    if k == 4:
                        wait_act("zb")
                turn(mem_tok, (6, 7, 2, 3), wait=mem_wait)
                tl = turns_before(l, 2)
                wide(L3, m0 + 13, 0, A, tiles=tl)
                wait_act("exp2")
                prob_turn(2).then_inc(l_pe.sem, l_pe.one("PT2"))
                wide(L3, m0 + 14, 1, A, tiles=tl)
                wait_dve("PT2")
                values(2).then_inc(l_pe.sem, l_pe.one("PV2"))
                scores(3, True).then_inc(l_pe.sem, l_pe.one("S3"))
                wide(L3, m0 + 15, 0, B)
                wait_act("exp3")
                prob_turn(3).then_inc(l_pe.sem, l_pe.one("PT3"))
                turn_half(zb_tok, (6, 7), 0).then_inc(l_pe.sem, l_pe.one("Tzb"))
                wide(L3, m0 + 16, 1, B)
                wait_dve("PT3")
                values(3).then_inc(l_pe.sem, l_pe.one("PV3"))
                wait_dve("K0")
                wide(L3, m0 + 17, 0, A)
                wait_dve("O3")
                turn_half(o_tok, (4, 5), 0).then_inc(l_pe.sem, l_pe.one("To"))
                wide(L3, m0 + 18, 1, A)
                wait_dve("y")
                turn_half(K_tok, (6, 7), 0).then_inc(l_pe.sem, l_pe.one("TK0"))
                wait_act("K1")
                wide(L3, m0 + 19, 0, B)
                wait_dve("KT0")
                turn_half(K_tok, (6, 7), 4).then_inc(l_pe.sem, l_pe.one("TK1"))
                wide(L3, m0 + 20, 1, B)
                wait_act("ysq")
                wait_dve("V0")
                for t in range(TOK):
                    for k in range(4):
                        last = mm(ps[:, 0, 2 * t:2 * t + 2], ysq[:, k, t * P:(t + 1) * P], ones[:, 0:2], k == 0, k == 3)
                last.then_inc(l_pe.sem, l_pe.one("ssq"))
                wait_dve("ycT_lo")
                wait_dve("oT_lo")
                wait_dve("KT1")
                tall(L3, m0 + 21, 0, 4, True, False, sT_hi, sT_lo)
                tall(L3, m0 + 22, 2, 4, False, True, sT_hi, sT_lo)
                wait_dve("ssq")
                wait_act("V1")
                tall(L3, m0 + 23, 4, 0, True, False, sT_hi, sT_lo)
                tall(L3, m0 + 24, 6, 0, False, True, sT_hi, sT_lo, signal_half=True)

                turn(res, N, wait=lambda k: pe.wait_ge(res_ready, res_of(l, 1) - (2 if k < 4 else 0)))
                tl = turns_before(l, 3)
                wide(L3, m0 + 25, 0, A, tiles=tl)
                wide(L3, m0 + 26, 1, A, tiles=tl)
                wide(L3, m0 + 27, 0, B)
                wait_act("xq0")
                turn_half(xq_tok, (4, 5), 0).then_inc(l_pe.sem, l_pe.one("TX0"))
                wide(L3, m0 + 28, 1, B)
                wait_dve("xq1")
                turn_half(xq_tok, (6, 7), 4).then_inc(l_pe.sem, l_pe.one("TX1"))
                for h in range(XH):
                    if h == 0:
                        wait_act("xqT0")
                    if h == 2:
                        wait_dve("xqT1")
                    for t in range(TOK):
                        for k in range(2):
                            last = mm(ps[:, h, t * S:(t + 1) * S], xqT[:, 2 * h + k, t * P:(t + 1) * P],
                                      kTx[:, 2 * h + k, :], k == 0, k == 1)
                    last.then_inc(l_pe.sem, l_pe.one(f"SX{h}"))
                for h in range(XH):
                    wait_act(f"xexp{h}")
                    for m in range(2):
                        for t in range(TOK):
                            last = nc.tensor.transpose(ps[:, 4 + h, m * S + t * P:m * S + (t + 1) * P],
                                                       Pb[:, h, t * S + m * P:t * S + (m + 1) * P], ident)
                    last.then_inc(l_pe.sem, l_pe.one(f"PX{h}"))
                for half in range(2):
                    for e in range(2):
                        h = 2 * half + e
                        if h % 2 == 0:
                            wait_act(f"PX{h}")
                        else:
                            wait_dve(f"PX{h}")
                        for t in range(TOK):
                            for m in range(2):
                                last = mm(ps[:, 2 * half + t, e * XDH:(e + 1) * XDH],
                                          PTb[:, h, m * S + t * P:m * S + (t + 1) * P],
                                          Vx[:, m, h * XDH:(h + 1) * XDH], m == 0, m == 1)
                    last.then_inc(l_pe.sem, l_pe.one(f"OX{half}"))

                def o_wait(k):
                    if k % 4 == 0:
                        wait_dve(f"xo{k // 4}")
                turn(xq_tok, N, wait=o_wait)
                tl = turns_before(l, 4)
                for i in range(4):
                    tall(L3, m0 + 29 + i, 2 * i, 0, i == 0, i == 3, xT_hi, xT_lo, tiles=tl, signal_half=(i == 3))

                ffn(1, B1_UNITS + FFN + MID)
            b_pe.closed()
            l_pe.closed()

        @block.scalar
        def _(act):
            copy, square, exp = ACT.Copy, ACT.Square, ACT.Exp

            def round_unit(r3, c):
                act.wait_ge(unit_landed[slot(c)], landed(r3, c))
                if not (isinstance(r3, int) and c < RING):
                    act.wait_ge(unit_used, upto_unit(r3, c - RING))
                nc.scalar.activation(w_hi[:, slot(c), :], raw[:, slot(c), :], copy).then_inc(unit_hi, 1)

            def turn_round(before, banks, gain):
                for b in range(BT):
                    act.wait_ge(turn_T, before + b + 1)
                    if gain is None:
                        last = nc.scalar.activation(xT_hi[:, 2 * b:2 * b + 2, :], tiles_of(banks[b]), copy)
                    else:
                        for k in (2 * b, 2 * b + 1):
                            last = nc.scalar.activation(xT_hi[:, k, :], tiles_of(banks[b])[:, k % 2, :], copy,
                                                        scale=gain[:, k:k + 1])
                    last.then_inc(turn_hi, 1)

            def squares(src, tile, before):
                for t in range(TOK):
                    if t or not isinstance(before, int) or before:
                        act.wait_ge(sums, before + t)
                    ap = src(t)
                    out_ = scratch[:, 0:ap.free_size()]
                    if len(ap.shape) == 3:
                        out_ = out_.rearrange("p (a n) -> p a n", a=ap.shape[1])
                    nc.scalar.activation(out_, ap, square, accum_out=stat[:, tile, t:t + 1]).then_inc(sums, 1)

            def probs(hp):
                for e in range(2):
                    h = 2 * hp + e
                    for t, (o0, nk) in enumerate(((0, P), (P, S))):
                        pr = Pb[:, 2 * (hp % 2) + e, o0:o0 + nk]
                        last = nc.scalar.activation(pr, pr, exp, scale=-1.0, bias=soft[:, 0, 8 * t + h:8 * t + h + 1],
                                                    accum_out=soft[:, 1, 8 * t + h:8 * t + h + 1])
                return last

            A, B, N = (0, 1), (2, 3), (4, 5, 6, 7)
            res_t = lambda t: res[:, t, :]

            def used(r3, c):
                act.wait_ge(unit_used, upto_unit(r3, c))

            def projected(banks, dst, tile):
                for t in range(TOK):
                    last = nc.scalar.activation(dst(t), ps[:, banks[t], :], copy, scale=rs(tile, t))
                return last

            act.dma_start(cst[:], consts).then_inc(cst_in, 16)
            act.dma_start(res[:], x).then_inc(x_in, 16)
            act.dma_start(colsA[:], cols).then_inc(cols_in, 16)
            act.dma_start(pmat[:, 0:2 * TRI], poolmat[:, 0:2 * TRI]).then_inc(pool_in, 16)
            act.dma_start(pmat2[:, 0:2 * TRI], poolmat[:, 2 * TRI:4 * TRI]).then_inc(pool_in, 16)
            act.dma_start(pw, poolw).then_inc(pool_in, 16)
            act.dma_start(mem_tok, mem).then_inc(mem_in, 16)
            act.dma_start(gbias, gate_bias).then_inc(gbias_in, 16)
            act.dma_start(gfin[:], final_gain).then_inc(gfin_in, 16)
            act.dma_start(selr[:], sel).then_inc(gfin_in, 16)

            def wait_pe1(n):
                act.wait_ge(b_pe.sem, b_pe.upto(n))

            def wait_dve1(n):
                act.wait_ge(b_dve.sem, b_dve.upto(n))

            def did1(ins, n):
                ins.then_inc(b_act.sem, b_act.one(n))

            round_unit(0, 0)
            act.wait_ge(cols_in, 16)
            turn_round(0, N, colsA[:, C_MIXPRE:C_MIXPRE + KT])
            round_unit(0, 1)
            act.wait_ge(x_in, 16)
            squares(res_t, T_FFN, 0)
            round_unit(0, 2)
            act.wait_ge(mem_in, 16)
            squares(lambda t: mem_tok[:, t, :], T_MEM, 2)
            round_unit(0, 3)
            used(0, 1)
            act.wait_ge(rstd, rstd_done(ST_X))
            did1(projected(A, lambda t: p_tok[:, t, :], T_FFN), "p")
            round_unit(0, 4)
            round_unit(0, 5)
            used(0, 3)
            did1(projected(B, lambda t: q_tok[:, t, :], T_FFN), "q")
            round_unit(0, 6)
            wait_pe1("pool_mix")
            for g in range(4):
                last = nc.scalar.activation(sT_hi[:, g, :], ps[:, 4 + g // 2, (g % 2) * S:(g % 2) * S + S], copy,
                                            scale=colsA[:, C_PSCALE + g:C_PSCALE + g + 1])
            did1(last, "ypT_hi")
            round_unit(0, 7)
            round_unit(0, 8)
            wait_pe1("Tq")
            did1(nc.scalar.activation(qT, ps[:, 6:8, :].rearrange("p b (k n) -> p (b k) n", k=2), copy, scale=DH ** -0.5), "qT")
            round_unit(0, 9)
            used(0, 7)
            did1(projected(B, lambda t: v_tok[:, t, :], T_FFN), "v")
            round_unit(0, 10)
            for hp in range(PAIRS):
                round_unit(0, 11 + 2 * hp)
                wait_dve1(f"soft{hp}")
                did1(probs(hp), f"exp{hp}")
                round_unit(0, 12 + 2 * hp)
            for i in range(4):
                wait_dve1(f"gate{i}")
                did1(nc.scalar.activation(gates[i], gates[i], ACT.Sigmoid), f"sig{i}")
            round_unit(0, 19)
            wait_pe1("To")
            did1(nc.scalar.activation(sT_hi[:, 4:8, :], ps[:, 6:8, :].rearrange("p b (k n) -> p (b k) n", k=2), copy), "oT_hi")
            act.dma_start(gpost, post_gain).then_inc(gpost_in, 16)
            round_unit(0, 20)
            round_unit(0, 21)
            turn_round(BT, (0, 1, 2, 3), None)
            round_unit(0, 22)
            round_unit(0, 23)
            round_unit(0, 24)
            round_unit(0, 25)
            used(0, 23)
            squares(lambda t: ps[:, 4 + t:8:2, :], T_MIX, 4)
            turn_round(2 * BT, N, colsA[:, C_MLPPRE:C_MLPPRE + KT])
            c0 = B1_UNITS - B1_MLP
            round_unit(0, c0 + 2)
            squares(res_t, T_FFN, 6)

            def relus(r3, c, banks):
                used(r3, c)
                for t in range(TOK):
                    last = nc.scalar.activation(relu[:, t, :], ps[:, banks[t], :], ACT.Relu, scale=rs(T_FFN, t))
                last.then_inc(up_relu, 1)

            def up_round(jr, j, banks):
                act.wait_ge(up_T, jr + j + 1)
                nc.scalar.activation(sT_hi[:, 0:4, :], ps[:, banks[0]:banks[1] + 1, :].rearrange("p b (k n) -> p (b k) n", k=2),
                                     copy).then_inc(upT_hi, 1)

            round_unit(0, c0 + 3)
            act.wait_ge(rstd, rstd_done(ST_NORM1))
            relus(0, c0 + 1, A)
            round_unit(0, c0 + 4)
            up_round(0, 0, (4, 5))
            round_unit(0, c0 + 5)
            relus(0, c0 + 3, B)
            round_unit(0, c0 + 6)
            round_unit(0, c0 + 7)
            up_round(0, 1, B)
            round_unit(0, c0 + 8)
            with act.Fori(0, 2) as r:
                for b in range(3):
                    c = c0 + 6 + 4 * b
                    round_unit(r * 4, c + 3)
                    relus(r * 4, c + 1, A)
                    round_unit(r * 4, c + 4)
                    round_unit(r * 4, c + 5)
                    up_round(r * 3, b + 2, B)
                    round_unit(r * 4, c + 6)
            round_unit(0, c0 + 33)
            used(0, c0 + 31)
            squares(lambda t: ps[:, 4 + t:8:2, :], T_MIX, 8)
            b_act.closed()

            with act.Fori(0, LAYERS) as l:
                L3 = l * (LAYER // 3)

                def wait_pe(n):
                    act.wait_ge(l_pe.sem, l_pe.upto(n, l))

                def wait_dve(n):
                    act.wait_ge(l_dve.sem, l_dve.upto(n, l))

                def did(ins, n):
                    ins.then_inc(l_act.sem, l_act.one(n))

                def ffn(which, base):
                    fb = l * (2 * FB)
                    f0 = which * FB
                    if which == 0:
                        act.wait_ge(cols_ready, l + 1)
                    g = colsL[:, (L_FFN1, L_FFN2)[which]:][:, 0:KT]
                    turn_round(turns_before(l, 0 if which == 0 else 5), N, g)
                    round_unit(L3, base + 2)
                    squares(res_t, T_FFN, sums_of(l, (0, 4)[which]) - 2)

                    def gate(r3, c, banks):
                        used(r3, c)
                        for t in range(TOK):
                            last = nc.scalar.activation(gate_act[:, t, :], ps[:, banks[t], 0:S], ACT.Silu, scale=rs(T_FFN, t))
                        last.then_inc(gate_ready, 1)

                    def hid_round(jr, j, bank=2):
                        act.wait_ge(hid_T, fb + jr + (f0 + j + 1))
                        nc.scalar.activation(sT_hi[:, 0:2, :], ps[:, bank, :].rearrange("p (k n) -> p k n", k=2),
                                             copy).then_inc(hidT_hi, 1)

                    round_unit(L3, base + 3)
                    act.wait_ge(rstd, rstd_done(in_layer(l, (ST_FFN1, ST_FFN2)[which])))
                    gate(L3, base + 1, A)
                    round_unit(L3, base + 4)
                    hid_round(0, 0, 4)
                    round_unit(L3, base + 5)
                    gate(L3, base + 3, B)
                    round_unit(L3, base + 6)
                    hid_round(0, 1)
                    round_unit(L3, base + 7)
                    with act.Fori(1, FB - 1) as j:
                        round_unit(L3 + j, base + 5)
                        gate(L3 + j, base + 3, A)
                        round_unit(L3 + j, base + 6)
                        hid_round(j, 1)
                        round_unit(L3 + j, base + 7)

                act.wait_ge(b_dve.sem, b_dve.upto("postmlp_h1"))
                act.dma_start(mem_tok, mem).then_inc(mem_in, 16)
                ffn(0, B1_UNITS)

                m0 = B1_UNITS + FFN

                def unit(i):
                    round_unit(L3, m0 + i)

                turn_round(turns_before(l, 1), N, colsL[:, L_MIX:L_MIX + KT])
                unit(2)
                squares(res_t, T_MIX, sums_of(l, 1) - 2)
                unit(3)
                act.wait_ge(rstd, rstd_done(in_layer(l, ST_MIX)))
                used(L3, m0 + 1)
                did(projected(A, lambda t: q_tok[:, t, :], T_MIX), "q")
                unit(4)
                unit(5)
                unit(6)
                unit(7)
                wait_pe("Tq")
                did(nc.scalar.activation(qT, ps[:, 6:8, :].rearrange("p b (k n) -> p (b k) n", k=2), copy, scale=DH ** -0.5), "qT")
                wait_dve("fabs")
                did(nc.scalar.activation(lf[:, 2], lf[:, 1], exp, scale=-1.0), "fexp")
                act.wait_ge(l_act.sem, l_act.upto("fexp", l))
                did(nc.scalar.activation(lf[:, 3], lf[:, 2], ACT.Ln, bias=1.0), "fln")
                unit(8)
                used(L3, m0 + 6)
                did(projected(A, lambda t: v_tok[:, t, :], T_MIX), "v")
                unit(9)
                unit(10)
                used(L3, m0 + 8)
                did(projected(B, lambda t: zc_tok[:, t, :], T_MIX), "zc")
                unit(11)
                wait_dve("soft0")
                did(probs(0), "exp0")
                unit(12)
                unit(13)
                wait_dve("soft1")
                did(probs(1), "exp1")
                unit(14)
                wait_pe("Tu")
                did(nc.scalar.activation(uT[:, :, 2:2 + S], ps[:, 6:8, :].rearrange("p b (k n) -> p (b k) n", k=2), copy), "uT")
                used(L3, m0 + 12)
                did(projected(B, lambda t: zb_tok[:, t, :], T_MIX), "zb")
                turn_round(turns_before(l, 2), (6, 7, 2, 3), colsL[:, L_MEM:L_MEM + KT])
                wait_dve("soft2")
                did(probs(2), "exp2")
                unit(15)
                unit(16)
                unit(17)
                wait_dve("soft3")
                did(probs(3), "exp3")
                unit(18)
                wait_dve("y")
                for c in range(4):
                    last = nc.scalar.activation(sT_hi[:, c, :], accT[:, c, :], copy, scale=colsL[:, L_CONV + c:L_CONV + c + 1])
                did(last, "yc_hi")
                did(nc.scalar.activation(ysq, accT[:, :, :], square), "ysq")
                used(L3, m0 + 16)
                did(projected(B, lambda t: K_tok[:, t, 512:1024], T_MEM), "K1")
                unit(19)
                wait_pe("To")
                for c in range(4):
                    last = nc.scalar.activation(sT_hi[:, 4 + c, :], ps[:, 4 + c // 2, (c % 2) * S:(c % 2) * S + S], copy,
                                                scale=colsL[:, L_ATT + c:L_ATT + c + 1])
                did(last, "oT_hi")
                squares(lambda t: o_tok[:, t, :], T_ATT, sums_of(l, 2) - 2)
                unit(20)
                unit(21)
                unit(22)
                used(L3, m0 + 20)
                did(projected(B, lambda t: Vx[:, t, 512:1024], T_MEM), "V1")
                for i in range(23, 27):
                    unit(i)

                turn_round(turns_before(l, 3), N, colsL[:, L_XAT:L_XAT + KT])
                unit(27)
                squares(res_t, T_XAT, sums_of(l, 3) - 2)
                unit(28)
                act.wait_ge(rstd, rstd_done(in_layer(l, ST_XAT)))
                used(L3, m0 + 26)
                did(projected(A, lambda t: xq_tok[:, t, 0:512], T_XAT), "xq0")
                unit(29)
                wait_pe("TX0")
                did(nc.scalar.activation(xqT[:, 0:4, :], ps[:, 4:6, :].rearrange("p b (k n) -> p (b k) n", k=2), copy,
                                         scale=XDH ** -0.5), "xqT0")
                unit(30)
                for h in range(XH):
                    wait_dve(f"xneg{h}")
                    for t in range(TOK):
                        last = nc.scalar.activation(Pb[:, h, t * S:(t + 1) * S], ps[:, h, t * S:(t + 1) * S], exp,
                                                    bias=xmax[:, 1, 2 * h + t:2 * h + t + 1],
                                                    accum_out=soft[:, 1, 8 * t + h:8 * t + h + 1])
                    did(last, f"xexp{h}")
                for h in (0, 2):
                    wait_pe(f"PX{h}")
                    did(nc.scalar.activation(PTb[:, h, :], ps[:, 4 + h, :], copy), f"PX{h}")
                turn_round(turns_before(l, 4), N, None)
                for i in range(31, 35):
                    unit(i)

                ffn(1, B1_UNITS + FFN + MID)
            l_act.closed()
            act.wait_ge(res_ready, res_of(LAYERS, -1))
            squares(res_t, T_XAT, sums_of(LAYERS, 0) - 2)

        @block.vector
        def _(dve):
            sub, mul, add, mx = ALU.subtract, ALU.mult, ALU.add, ALU.max
            stt = nc.vector.scalar_tensor_tensor

            def rest_unit(r3, c):
                dve.wait_ge(unit_hi, upto_unit(r3, c))
                nc.vector.tensor_tensor(w_lo[:, slot(c), :], raw[:, slot(c), :], w_hi[:, slot(c), :].bitcast(F32),
                                        sub).then_inc(unit_lo, 1)

            def rest(dst, src, hi, gain=None):
                if gain is None:
                    return nc.vector.tensor_tensor(dst, src, hi.bitcast(F32), sub)
                return stt(out=dst, in0=src, scalar=gain, in1=hi.bitcast(F32), op0=mul, op1=sub)

            def turn_rest(before, banks, gain):
                for b in range(BT):
                    dve.wait_ge(turn_hi, before + b + 1)
                    if gain is None:
                        last = rest(xT_lo[:, 2 * b:2 * b + 2, :], tiles_of(banks[b]), xT_hi[:, 2 * b:2 * b + 2, :])
                    else:
                        for k in (2 * b, 2 * b + 1):
                            last = rest(xT_lo[:, k, :], tiles_of(banks[b])[:, k % 2, :], xT_hi[:, k, :], gain[:, k:k + 1])
                    last.then_inc(turn_lo, 1)

            def used(r3, c):
                dve.wait_ge(unit_used, upto_unit(r3, c))

            def projected(banks, dst, tile):
                for t in range(TOK):
                    last = nc.vector.tensor_scalar(dst(t), ps[:, banks[t], :], rs(tile, t), None, mul)
                return last

            def two_banks(b):
                return ps[:, b:b + 2, :].rearrange("p b (k n) -> p (b k) n", k=2)

            def maxima(hp, bias):
                for e in range(2):
                    h = 2 * hp + e
                    for t, (o0, nk) in enumerate(((0, P), (P, S))):
                        last = nc.vector.tensor_tensor_reduce(
                            out=Pb[:, 2 * (hp % 2) + e, o0:o0 + nk], in0=ps[:, 4 + e, o0:o0 + nk],
                            in1=bias(e)[:, o0:o0 + nk], scale=-1.0, scalar=BIG, op0=add, op1=ALU.min,
                            accum_out=soft[:, 0, 8 * t + h:8 * t + h + 1])
                return last

            def pair(ap, hp):
                return ap.rearrange("p (t h) -> p t h", t=2)[:, :, 2 * hp:2 * hp + 2]

            def inverse_sums(hp):
                return nc.vector.reciprocal(pair(rinv[:], hp), pair(soft[:, 1, :], hp))

            def probs_T(hp):
                a = 2 * (hp % 2)
                return nc.vector.tensor_copy(PTb[:, a:a + 2, 0:TRI], ps[:, 4:6, 0:TRI])

            def values_out(hp):
                for t in range(TOK):
                    o = o_tok[:, t, hp * P:(hp + 1) * P].rearrange("p (e d) -> p e d", e=2)
                    r = rinv[:, 8 * t + 2 * hp:8 * t + 2 * hp + 2].unsqueeze(2).to_broadcast([P, 2, DH])
                    last = nc.vector.tensor_tensor(o, ps[:, 4 + t, TRI:512].rearrange("p (e d) -> p e d", e=2), r, mul)
                return last

            A, B, N = (0, 1), (2, 3), (4, 5, 6, 7)

            def wait_pe1(n):
                dve.wait_ge(b_pe.sem, b_pe.upto(n))

            def wait_act1(n):
                dve.wait_ge(b_act.sem, b_act.upto(n))

            def wait_own1(n):
                dve.wait_ge(b_dve.sem, b_dve.upto(n))

            def did1(ins, n):
                ins.then_inc(b_dve.sem, b_dve.one(n))

            rest_unit(0, 0)
            turn_rest(0, N, colsA[:, C_MIXPRE:C_MIXPRE + KT])
            for c in range(1, 6):
                rest_unit(0, c)
            wait_pe1("pool_mean")
            did1(nc.vector.tensor_copy(yT, two_banks(6)), "yT")
            rest_unit(0, 6)
            wait_act1("ypT_hi")
            for g in range(4):
                last = rest(sT_lo[:, g, :], two_banks(4)[:, g, :], sT_hi[:, g, :], colsA[:, C_PSCALE + g:C_PSCALE + g + 1])
            did1(last, "ypT_lo")
            rest_unit(0, 7)
            used(0, 5)
            did1(projected(A, lambda t: k_tok[:, t, :], T_FFN), "k")
            rest_unit(0, 8)
            rest_unit(0, 9)
            wait_pe1("Tk")
            did1(nc.vector.tensor_copy(kT, two_banks(4)), "kT")
            rest_unit(0, 10)
            dve.wait_ge(gbias_in, 16)
            for hp in range(PAIRS):
                wait_pe1(f"S{hp}")
                if hp:
                    did1(values_out(hp - 1), f"O{hp - 1}")
                dve.wait_ge(alibi_ready, hp + 1)
                did1(maxima(hp, lambda e: alibi[hp % 2][:, e * TRI:(e + 1) * TRI]), f"soft{hp}")
                rest_unit(0, 11 + 2 * hp)
                used(0, 9 + 2 * hp)
                if hp == 0:
                    dve.wait_ge(sums, 4)
                for t in range(TOK):
                    last = stt(out=gates[hp][:, t, :], in0=ps[:, (A, B)[hp % 2][t], :], scalar=rs(T_FFN, t),
                               in1=gbias[:, hp * 512:(hp + 1) * 512], op0=mul, op1=add)
                did1(last, f"gate{hp}")
                wait_act1(f"exp{hp}")
                did1(inverse_sums(hp), f"rinv{hp}")
                wait_pe1(f"PT{hp}")
                did1(probs_T(hp), f"PT{hp}")
                wait_own1(f"rinv{hp}")
                rest_unit(0, 12 + 2 * hp)
            wait_pe1("PV3")
            did1(values_out(3), "O3")
            rest_unit(0, 19)
            wait_act1("oT_hi")
            did1(rest(sT_lo[:, 4:8, :], two_banks(6), sT_hi[:, 4:8, :]), "oT_lo")
            wait_act1("sig3")
            used(0, 17)
            for half in range(2):
                for t in range(TOK):
                    last = nc.vector.tensor_tensor(m_tok[:, t, half * 512:half * 512 + 512], gates[half][:, t, :],
                                                   ps[:, 2 * half + t, :], mul)
            did1(last, "m1")
            rest_unit(0, 20)
            rest_unit(0, 21)
            for half in range(2):
                if half == 0:
                    dve.wait_ge(half_ready, 1)
                    wait_own1("m1")
                else:
                    used(0, 19)
                for t in range(TOK):
                    last = nc.vector.tensor_tensor(PTb[:, 2 * half + t, :], gates[2 + half][:, t, :],
                                                   ps[:, 4 + 2 * half + t, :], mul)
                did1(last, f"m2h{half}")
                wait_own1(f"m2h{half}")
                for t in range(TOK):
                    mq = m_tok[:, t, half * 512:half * 512 + 512]
                    last = nc.vector.tensor_tensor(mq, mq, PTb[:, 2 * half + t, :], add)
                did1(last, f"mh{half}")
            turn_rest(BT, (0, 1, 2, 3), None)
            for c in range(22, 26):
                rest_unit(0, c)

            def post_norm(stat_i, gain, name):
                dve.wait_ge(rstd, rstd_done(stat_i))
                dve.wait_ge(gpost_in, 16)
                for half in range(2):
                    hs = slice(half * 512, half * 512 + 512)
                    for t in range(TOK):
                        last = stt(out=Pb[:, 2 * half + t, :], in0=ps[:, 4 + 2 * half + t, :], scalar=rs(T_MIX, t),
                                   in1=gain[:, hs], op0=mul, op1=mul)
                    did1(last, f"{name}_h{half}")
                    wait_own1(f"{name}_h{half}")
                    for t in range(TOK):
                        nc.vector.tensor_tensor(res[:, t, hs], res[:, t, hs], Pb[:, 2 * half + t, :],
                                                add).then_inc(res_ready, 1)

            post_norm(ST_WOUT, gpost[:, 0:D], "postmix")
            turn_rest(2 * BT, N, colsA[:, C_MLPPRE:C_MLPPRE + KT])
            c0 = B1_UNITS - B1_MLP
            rest_unit(0, c0 + 2)
            rest_unit(0, c0 + 3)

            def squared(jr, j):
                dve.wait_ge(up_relu, jr + j + 1)
                nc.vector.tensor_tensor(sq, relu, relu, mul).then_inc(up_sq, 1)

            def up_rest(jr, j, bank):
                dve.wait_ge(upT_hi, jr + j + 1)
                rest(sT_lo[:, 0:4, :], two_banks(bank), sT_hi[:, 0:4, :]).then_inc(upT_lo, 1)

            squared(0, 0)
            rest_unit(0, c0 + 4)
            up_rest(0, 0, 4)
            rest_unit(0, c0 + 5)
            squared(0, 1)
            rest_unit(0, c0 + 6)
            rest_unit(0, c0 + 7)
            up_rest(0, 1, 2)
            rest_unit(0, c0 + 8)
            with dve.Fori(0, 2) as r:
                for b in range(3):
                    c = c0 + 6 + 4 * b
                    rest_unit(r * 4, c + 3)
                    squared(r * 3, b + 2)
                    rest_unit(r * 4, c + 4)
                    rest_unit(r * 4, c + 5)
                    up_rest(r * 3, b + 2, 2)
                    rest_unit(r * 4, c + 6)
            rest_unit(0, c0 + 33)
            post_norm(ST_MLP, gpost[:, D:2 * D], "postmlp")
            b_dve.closed()

            with dve.Fori(0, LAYERS) as l:
                L3 = l * (LAYER // 3)

                def wait_pe(n):
                    dve.wait_ge(l_pe.sem, l_pe.upto(n, l))

                def wait_act(n):
                    dve.wait_ge(l_act.sem, l_act.upto(n, l))

                def wait_own(n):
                    dve.wait_ge(l_dve.sem, l_dve.upto(n, l))

                def did(ins, n):
                    ins.then_inc(l_dve.sem, l_dve.one(n))

                def onto_res(i, last_unit, base, scale):
                    for half in range(2):
                        if half == 0:
                            dve.wait_ge(half_ready, half_of(l, i))
                        else:
                            used(*last_unit)
                        for t in range(TOK):
                            r = res[:, t, half * 512:half * 512 + 512]
                            stt(out=r, in0=ps[:, base + 2 * half + t, :], scalar=scale(t), in1=r,
                                op0=mul, op1=add).then_inc(res_ready, 1)

                def ffn(which, base):
                    fb = l * (2 * FB)
                    f0 = which * FB
                    turn_rest(turns_before(l, 0 if which == 0 else 5), N, colsL[:, (L_FFN1, L_FFN2)[which]:][:, 0:KT])
                    rest_unit(L3, base + 2)

                    def hidden(jr, j, banks):
                        dve.wait_ge(gate_ready, fb + jr + (f0 + j + 1))
                        for t in range(TOK):
                            last = stt(out=hid[:, t, :], in0=ps[:, banks[t], S:2 * S], scalar=rs(T_FFN, t),
                                       in1=gate_act[:, t, :], op0=mul, op1=mul)
                        last.then_inc(hid_ready, 1)

                    def hid_rest(jr, j, bank=2):
                        dve.wait_ge(hidT_hi, fb + jr + (f0 + j + 1))
                        rest(sT_lo[:, 0:2, :], ps[:, bank, :].rearrange("p (k n) -> p k n", k=2),
                             sT_hi[:, 0:2, :]).then_inc(hidT_lo, 1)

                    rest_unit(L3, base + 3)
                    hidden(0, 0, A)
                    rest_unit(L3, base + 4)
                    hid_rest(0, 0, 4)
                    rest_unit(L3, base + 5)
                    hidden(0, 1, B)
                    rest_unit(L3, base + 6)
                    hid_rest(0, 1)
                    rest_unit(L3, base + 7)
                    with dve.Fori(1, FB - 1) as j:
                        rest_unit(L3 + j, base + 5)
                        hidden(j, 1, A)
                        rest_unit(L3 + j, base + 6)
                        hid_rest(j, 1)
                        rest_unit(L3 + j, base + 7)
                    onto_res((0, 3)[which], (L3, base + FFN - 1), 4, lambda t: 0.5)

                dve.wait_ge(cols_ready, l + 1)
                ffn(0, B1_UNITS)

                m0 = B1_UNITS + FFN

                def unit(i):
                    rest_unit(L3, m0 + i)

                turn_rest(turns_before(l, 1), N, colsL[:, L_MIX:L_MIX + KT])
                unit(2)
                unit(3)
                unit(4)
                unit(5)
                dve.wait_ge(rstd, rstd_done(in_layer(l, ST_MIX)))
                used(L3, m0 + 3)
                did(projected(B, lambda t: k_tok[:, t, :], T_MIX), "k")
                unit(6)
                used(L3, m0 + 4)
                for t in range(TOK):
                    last = stt(out=lf[:, 0, t, :], in0=ps[:, 4 + t, 0:HEADS], scalar=rs(T_MIX, t),
                               in1=colsL[:, L_BF:L_BF + HEADS], op0=mul, op1=add)
                did(last, "f")
                wait_own("f")
                did(stt(out=lf[:, 1], in0=lf[:, 0], scalar=-1.0, in1=lf[:, 0], op0=mul, op1=mx), "fabs")
                unit(7)
                wait_act("fln")
                did(stt(out=lf[:, 4], in0=lf[:, 0], scalar=0.0, in1=lf[:, 3], op0=ALU.min, op1=sub, reverse1=True), "logf")
                unit(8)
                wait_pe("Tk")
                did(nc.vector.tensor_copy(kT, two_banks(4)), "kT")
                unit(9)
                wait_pe("cT")
                did(nc.vector.tensor_copy(cT[:], ps[0:HEADS, 6, 0:S]), "cT")
                unit(10)

                def masked(hp):
                    return maxima(hp, lambda e: mask)

                wait_pe("S0")
                did(nc.vector.memset(uT[:, :, 0:2], 0.0), "pad")
                did(masked(0), "soft0")
                unit(11)
                wait_act("exp0")
                did(inverse_sums(0), "rinv0")
                wait_pe("PT0")
                did(probs_T(0), "PT0")
                unit(12)
                used(L3, m0 + 10)
                wait_act("zc")
                for t in range(TOK):
                    last = stt(out=u_tok[:, t, :], in0=ps[:, A[t], :], scalar=rs(T_MIX, t), in1=zc_tok[:, t, :],
                               op0=mul, op1=mul)
                did(last, "u")
                wait_own("rinv0")
                wait_pe("S1")
                did(values_out(0), "O0")
                did(masked(1), "soft1")
                unit(13)
                wait_act("exp1")
                did(inverse_sums(1), "rinv1")
                wait_pe("PT1")
                did(probs_T(1), "PT1")
                unit(14)
                wait_own("rinv1")
                wait_pe("S2")
                did(values_out(1), "O1")
                did(masked(2), "soft2")
                turn_rest(turns_before(l, 2), (6, 7, 2, 3), colsL[:, L_MEM:L_MEM + KT])
                unit(15)
                wait_act("uT")
                wait_own("pad")
                for tap in range(3):
                    for c in range(4):
                        w = colsL[:, L_WCONV + 4 * tap + c:L_WCONV + 4 * tap + c + 1]
                        src = uT[:, c, tap:tap + S]
                        if tap == 0:
                            last = nc.vector.tensor_scalar(accT[:, c, :], src, w, None, mul)
                        else:
                            last = stt(out=accT[:, c, :], in0=src, scalar=w, in1=accT[:, c, :], op0=mul, op1=add)
                    did(last, f"cv{tap}")
                    wait_own(f"cv{tap}")
                unit(16)
                wait_act("exp2")
                did(inverse_sums(2), "rinv2")
                wait_pe("PT2")
                did(probs_T(2), "PT2")
                used(L3, m0 + 14)
                did(projected(A, lambda t: K_tok[:, t, 0:512], T_MEM), "K0")
                wait_own("rinv2")
                wait_pe("S3")
                did(values_out(2), "O2")
                did(masked(3), "soft3")
                unit(17)
                wait_act("exp3")
                did(inverse_sums(3), "rinv3")
                wait_pe("PT3")
                did(probs_T(3), "PT3")
                wait_pe("Tzb")
                did(nc.vector.tensor_tensor(accT[:, :, :], accT[:, :, :], two_banks(6), mul), "y")
                unit(18)
                wait_act("yc_hi")
                wait_own("y")
                for c in range(4):
                    last = rest(sT_lo[:, c, :], accT[:, c, :], sT_hi[:, c, :], colsL[:, L_CONV + c:L_CONV + c + 1])
                did(last, "ycT_lo")
                wait_pe("PV3")
                wait_own("rinv3")
                did(values_out(3), "O3")
                unit(19)
                wait_act("oT_hi")
                for c in range(4):
                    last = rest(sT_lo[:, 4 + c, :], two_banks(4)[:, c, :], sT_hi[:, 4 + c, :],
                                colsL[:, L_ATT + c:L_ATT + c + 1])
                did(last, "oT_lo")
                unit(20)
                used(L3, m0 + 18)
                did(projected(A, lambda t: Vx[:, t, 0:512], T_MEM), "V0")
                wait_pe("TK0")
                did(nc.vector.tensor_copy(kTx[:, 0:4, :], two_banks(6)), "KT0")
                unit(21)
                wait_pe("TK1")
                did(nc.vector.tensor_copy(kTx[:, 4:8, :], two_banks(6)), "KT1")
                unit(22)
                wait_pe("ssq")
                did(nc.vector.tensor_copy(stat[:, T_CONV, 0:2], ps[:, 0, 0:4:2]), "ssq")
                unit(23)
                unit(24)
                dve.wait_ge(rstd, rstd_done(in_layer(l, ST_CONV)))
                used(L3, m0 + 22)
                for half in range(2):
                    for t in range(TOK):
                        r = res[:, t, half * 512:half * 512 + 512]
                        last = stt(out=r, in0=ps[:, 4 + 2 * half + t, :], scalar=rs(T_CONV, t), in1=r, op0=mul, op1=add)
                did(last, "resconv")
                wait_own("resconv")
                unit(25)
                unit(26)
                onto_res(1, (L3, m0 + 24), 0, lambda t: rs(T_ATT, t))

                turn_rest(turns_before(l, 3), N, colsL[:, L_XAT:L_XAT + KT])
                for i in range(27, 31):
                    unit(i)
                used(L3, m0 + 28)
                did(projected(B, lambda t: xq_tok[:, t, 512:1024], T_XAT), "xq1")
                wait_pe("TX1")
                did(nc.vector.tensor_scalar(xqT[:, 4:8, :], two_banks(6), XDH ** -0.5, None, mul), "xqT1")
                for h in range(XH):
                    wait_pe(f"SX{h}")
                    did(nc.vector.tensor_reduce(xmax[:, 0, 2 * h:2 * h + 2], ps[:, h, :].rearrange("p (t n) -> p t n", t=2),
                                                AX.X, mx), f"xm{h}")
                    wait_own(f"xm{h}")
                    did(nc.vector.tensor_scalar(xmax[:, 1, 2 * h:2 * h + 2], xmax[:, 0, 2 * h:2 * h + 2], -1.0, None, mul),
                        f"xneg{h}")
                wait_act("xexp3")
                did(nc.vector.reciprocal(rinv[:].rearrange("p (t h) -> p t h", t=2)[:, :, 0:XH],
                                         soft[:, 1, :].rearrange("p (t h) -> p t h", t=2)[:, :, 0:XH]), "rinvx")
                for h in (1, 3):
                    wait_pe(f"PX{h}")
                    did(nc.vector.tensor_copy(PTb[:, h, :], ps[:, 4 + h, :]), f"PX{h}")
                wait_own("rinvx")
                for half in range(2):
                    wait_pe(f"OX{half}")
                    for t in range(TOK):
                        o = xq_tok[:, t, half * 512:half * 512 + 512].rearrange("p (e d) -> p e d", e=2)
                        r = rinv[:, 8 * t + 2 * half:8 * t + 2 * half + 2].unsqueeze(2).to_broadcast([P, 2, XDH])
                        last = nc.vector.tensor_tensor(o, ps[:, 2 * half + t, :].rearrange("p (e d) -> p e d", e=2), r, mul)
                    did(last, f"xo{half}")
                turn_rest(turns_before(l, 4), N, None)
                for i in range(31, 35):
                    unit(i)
                onto_res(2, (L3, m0 + 32), 0, lambda t: 1.0)

                ffn(1, B1_UNITS + FFN + MID)
            l_dve.closed()
            dve.wait_ge(rstd, rstd_done(ST_LAYER + LAYERS * NST))
            dve.wait_ge(gfin_in, 32)
            for t in range(TOK):
                stt(out=out_tok[:, t, :], in0=res[:, t, :], scalar=rs(T_XAT, t), in1=gfin[:], op0=mul,
                    op1=mul).then_inc(fin_ready, 1)

        @block.gpsimd
        def _(pool):
            nc.gpsimd.memset(ones[:], 1.0).then_inc(set_ready, 1)
            for i, value in enumerate((1.0 / D, 2.0 / D, EPS, -0.5)):
                nc.gpsimd.memset(consts2[:, i, :], value).then_inc(set_ready, 1)
            pool.wait_ge(set_ready, 5)

            def statistic(i, tile, width):
                total, mean, inv = (stat[:, tile, 2 * i_:2 * i_ + 2] for i_ in range(3))
                nc.gpsimd.tensor_tensor(mean, total, consts2[:, 0 if width == D else 1, :], ALU.mult).then_inc(rstd, 1)
                pool.wait_ge(rstd, rstd_done(i) - 2)
                nc.gpsimd.tensor_tensor(mean, mean, consts2[:, 2, :], ALU.add).then_inc(rstd, 1)
                pool.wait_ge(rstd, rstd_done(i) - 1)
                nc.gpsimd.tensor_tensor(inv, mean, consts2[:, 3, :], ALU.pow).then_inc(rstd, 1)

            pool.wait_ge(sums, 2)
            statistic(ST_X, T_FFN, D)
            pool.wait_ge(sums, 4)
            statistic(ST_MEM, T_MEM, D)
            pool.wait_ge(cst_in, 16)
            for hp in range(PAIRS):
                if hp == 1:
                    pool.wait_ge(b_pe.sem, b_pe.upto("pool_mean"))
                if hp >= 2:
                    pool.wait_ge(b_dve.sem, b_dve.upto(f"soft{hp - 2}"))
                for e in range(2):
                    slope = 2.0 ** (-8.0 * (2 * hp + e + 1) / HEADS)
                    last = nc.gpsimd.tensor_scalar(alibi[hp % 2][:, e * TRI:(e + 1) * TRI], negdist, slope, None, ALU.mult)
                last.then_inc(alibi_ready, 1)
            pool.wait_ge(sums, 6)
            statistic(ST_WOUT, T_MIX, D)
            pool.wait_ge(sums, 8)
            statistic(ST_NORM1, T_FFN, D)
            pool.wait_ge(sums, 10)
            statistic(ST_MLP, T_MIX, D)
            pool.wait_ge(cols_in, 16)
            with pool.Fori(0, LAYERS) as l:
                pool.wait_ge(turn_lo, turns_before(l, 0))
                nc.gpsimd.tensor_copy(colsL[:], colsA[:, bass.ds(l * L_COLS + C_B1, L_COLS)]).then_inc(cols_ready, 1)
                for i, (tile, n_sum, width) in enumerate((
                        (T_FFN, 0, D), (T_MIX, 1, D), (T_ATT, 2, 512), (T_CONV, None, 512), (T_XAT, 3, D), (T_FFN, 4, D))):
                    if n_sum is None:
                        pool.wait_ge(l_dve.sem, l_dve.upto("ssq", l))
                    else:
                        pool.wait_ge(sums, sums_of(l, n_sum))
                    statistic(in_layer(l, i), tile, width)
            pool.wait_ge(sums, sums_of(LAYERS, 0))
            statistic(ST_LAYER + LAYERS * NST, T_XAT, D)


def _wide(w):
    return w.reshape(2, 4, P, 512).transpose(0, 2, 1, 3).reshape(2, P, UNIT)


def _tall(w):
    n = w.shape[0] // (2 * P)
    return w.reshape(n, 2, P, D).transpose(0, 2, 1, 3).reshape(n, P, UNIT)


def _columns(v):
    return v.reshape(-1, P).T


def _stream(a):
    w = a["w_in"][0]
    units = [_wide(w[:, 512 * i:512 * i + 512]) for i in range(8)]
    units += [_tall(a["w_branch_pool"][0]), _tall(a["w_branch_attn"][0]), _tall(a["w_out"][0])]
    up = lambda j: _wide(a["w_up"][0][:, 512 * j:512 * j + 512])
    down = lambda j: _tall(a["w_down"][0][512 * j:512 * j + 512])
    units.append(up(0))
    for j in range(1, B1_FB):
        units += [up(j), down(j - 1)]
    units.append(down(B1_FB - 1))
    for l in range(LAYERS):
        def ffn(gu, dn):
            f = FB * 256
            g = lambda j: _wide(np.concatenate([gu[:, 256 * j:256 * j + 256], gu[:, f + 256 * j:f + 256 * j + 256]], 1))
            d = lambda j: _tall(dn[256 * j:256 * j + 256])
            out = [g(0)]
            for j in range(1, FB):
                out += [g(j), d(j - 1)]
            return out + [d(FB - 1)]
        units += ffn(a["w_ffn1_gu_2"][l], a["w_ffn1_down_2"][l])
        w = a["w_mix_in_2"][l]
        block = lambda i: _wide(w[:, 512 * i:512 * i + 512])
        forget = np.zeros((1, P, UNIT), np.float32)
        forget[0, :, 0:KT * HEADS] = w[:, 3072:].reshape(KT, P, HEADS).transpose(1, 0, 2).reshape(P, KT * HEADS)
        units += [block(3), block(4), forget, block(5), block(1), block(2), block(0)]
        units += [_wide(a["w_xkv_2"][l][:, 512 * i:512 * i + 512]) for i in range(4)]
        units += [_tall(a["w_mix_out_2"][l])]
        units += [_wide(a["w_xq_2"][l][:, 512 * i:512 * i + 512]) for i in range(2)]
        units += [_tall(a["w_xo_2"][l])]
        units += ffn(a["w_ffn2_gu_2"][l], a["w_ffn2_down_2"][l])
    s = np.concatenate(units, 0)
    assert s.shape == (TOTAL, P, UNIT), s.shape
    return s


def _constants():
    q = np.arange(S)
    ok = q[None, :] <= q[:, None]
    dist = np.where(ok, (q[None, :] - q[:, None]).astype(np.float32), np.float32(NEG))
    mask = np.where(ok, np.float32(0), np.float32(NEG))

    def tri(m):
        return np.concatenate([m[0:P, 0:P], m[P:S, :]], 1)

    upto = ok.T[0:P, :].astype(np.float32)
    cst = np.concatenate([np.eye(P, dtype=np.float32), tri(dist), tri(mask), upto], 1)
    mats = []
    for w in POOL_WINDOWS:
        count = np.minimum(q + 1, w).astype(np.float32)
        m = np.where(ok & (q[:, None] - q[None, :] < w), np.float32(1) / count[:, None], np.float32(0))
        m = (m - np.eye(S, dtype=np.float32)).T
        mats.append(np.concatenate([m[0:P, :], m[P:S, P:S]], 1))
    sel = np.zeros((HEADS, HEADS, P), np.float32)
    for h in range(HEADS):
        sel[h, h, :] = 1
    return cst, sel, np.concatenate(mats, 1).astype(np.float32)


def kernel(**a):
    import concourse.bacc as bacc
    from concourse.bass_utils import run_bass_kernel_spmd

    cst, sel, poolmat = _constants()
    a = {k: np.asarray(v) for k, v in a.items()}
    group = [_columns(a["norm_mix_pre"][0]), _columns(a["norm_mlp_pre"][0]), _columns(a["pool_scale"][0])]
    for l in range(LAYERS):
        group += [_columns(a[n][l]) for n in ("g_ffn1_2", "g_mix_2", "g_mem_2", "g_xattn_2", "g_ffn2_2",
                                              "g_conv_out_2", "g_att_out_2")]
        group += [_columns(a["w_conv_2"][l].reshape(-1)), np.broadcast_to(a["b_f_2"][l], (P, HEADS))]
    rows = lambda v: np.broadcast_to(v.reshape(1, -1), (P, v.size))
    arrays = {
        "x": a["x"].reshape(TOK, P, D).transpose(1, 0, 2),
        "mem": a["mem_2"].reshape(TOK, P, D).transpose(1, 0, 2),
        "stream": _stream(a),
        "cols": np.concatenate(group, 1),
        "consts": cst,
        "sel": sel,
        "poolmat": poolmat,
        "poolw": a["pool_w"][0].transpose(1, 0, 2),
        "gate_bias": rows(a["b_gate"][0]),
        "post_gain": rows(np.concatenate([a["norm_mix_post"][0], a["norm_mlp_post"][0]])),
        "final_gain": rows(a["g_final_2"]),
    }
    arrays = {f"{k}_in": np.ascontiguousarray(v) for k, v in arrays.items()}
    nc = bacc.Bacc("TRN2", target_bir_lowering=False, num_devices=1)
    aps = [nc.dram_tensor(k, v.shape, F32, kind="ExternalInput").ap() for k, v in arrays.items()]
    out = nc.dram_tensor("out", (TOK, P, D), F32, kind="ExternalOutput").ap()
    program(nc, *aps, out)
    r = run_bass_kernel_spmd(nc, [arrays], core_ids=[0])
    return r.results[0]["out"].reshape(1, S, D)
```

```python
from contextlib import ExitStack

import numpy as np

import concourse.bass as bass
from concourse import mybir

F32 = mybir.dt.float32
F32R = mybir.dt.float32r
ALU = mybir.AluOpType
ACT = mybir.ActivationFunctionType
AX = mybir.AxisListType

P = 128
D = 1024
S = 256
TOK = S // P
KT = D // P
BT = KT // 2
HEADS, DH = 8, 64
PAIRS = HEADS // 2
XH, XDH = 4, 256
POOL_WINDOWS = (2, 4, 8, 16)
LAYERS = 2
EPS = 1e-6
NEG = -1e30
BIG = 3e38

UNIT = 2048
RING = 3
TRI = 3 * P

B1_IN, B1_BRANCH, B1_OUT = 16, 4, 8 // 2
B1_FB = 8
B1_MLP = 4 * B1_FB
B1_UNITS = B1_IN + B1_BRANCH + B1_OUT + B1_MLP
FB = 11
FFN = 3 * FB
MID = 33
LAYER = 2 * FFN + MID
TOTAL = B1_UNITS + LAYERS * LAYER
AHEAD = TOTAL + 2
assert LAYER % RING == 0 and MID % RING == 0 and FFN % RING == 0

C_MIXPRE, C_MLPPRE, C_PSCALE, C_B1 = 0, 8, 16, 20
L_FFN1, L_MIX, L_MEM, L_XAT, L_FFN2, L_CONV, L_ATT, L_WCONV, L_BF, L_COLS = 0, 8, 16, 24, 32, 40, 44, 48, 60, 68

B1_PE = ["pool_mean", "pool_mix", "Tq", "Tk", "S0", "PT0", "PV0", "S1", "PT1", "PV1", "S2", "PT2",
         "PV2", "S3", "PT3", "PV3", "To"]
B1_ACT = ["p", "q", "ypT_hi", "qT", "v", "exp0", "exp1", "exp2", "exp3",
          "sig0", "sig1", "sig2", "sig3", "oT_hi"]
B1_DVE = ["yT", "ypT_lo", "k", "kT", "soft0", "gate0", "rinv0", "PT0", "O0", "soft1", "gate1", "rinv1", "PT1",
          "O1", "soft2", "gate2", "rinv2", "PT2", "O2", "soft3", "gate3", "rinv3", "PT3", "O3", "oT_lo",
          "m1", "m2q0", "m2q1", "mh0", "m2q2", "m2q3", "mh1", "postmix", "postmlp"]
L_PE = ["Tq", "Tk", "cT", "S0", "PT0", "PV0", "S1", "PT1", "Tu", "PV1", "S2", "PT2", "PV2", "S3", "PT3",
        "Tzb", "PV3", "To", "TK0", "TK1", "ssq", "TX0", "TX1", "SX0", "SX1", "SX2", "SX3",
        "PX0", "PX1", "PX2", "PX3", "OX0", "OX1"]
L_ACT = ["q", "qT", "fexp", "fln", "v", "cT_hi", "zc", "exp0", "exp1", "uT", "zb", "exp2", "exp3", "yc_hi", "ysq", "K1",
         "oT_hi", "V1", "xq0", "xqT0", "xq1", "xexp0", "xexp1", "xexp2", "xexp3", "PX0", "PX2"]
L_DVE = ["k", "f", "fabs", "logf", "kT", "cT", "pad", "soft0", "rinv0", "PT0", "u", "O0", "soft1", "rinv1", "PT1",
         "O1", "soft2", "rinv2", "PT2", "cv0", "K0", "O2", "soft3", "cv1", "rinv3", "PT3", "cv2", "y", "ycT_lo", "O3",
         "oT_lo", "V0", "KT0", "KT1", "ssq", "resconv", "xq1", "xqT1", "xm0", "xneg0", "xm1", "xneg1", "xm2", "xneg2",
         "xm3", "xneg3", "rinvx", "PX1", "PX3", "xo0", "xo1"]

class Steps:

    def __init__(self, sem, names):
        self.sem, self.names, self.at = sem, names, 0
        assert len(set(names)) == len(names), names

    def upto(self, name, layer=0):
        return layer * len(self.names) + self.names.index(name) + 1

    def one(self, name):
        assert self.names[self.at] == name, (self.names[self.at], name)
        self.at += 1
        return 1

    def closed(self):
        assert self.at == len(self.names), self.names[self.at:]


def program(nc, x, mem, stream, cols, consts, sel, poolmat, poolw, gate_bias, post_gain, final_gain, out):
    with ExitStack() as ctx:
        def sb(name, shape, dt=F32):
            return ctx.enter_context(nc.sbuf_tensor(name, shape, dt))

        def sem(name):
            return ctx.enter_context(nc.semaphore(name))

        def tiles2(ap):
            return ap.rearrange("p (k n) -> p k n", k=2)

        res = sb("res", [P, TOK, D])
        xT_hi, xT_lo = sb("xT_hi", [P, KT, S], F32R), sb("xT_lo", [P, KT, S], F32R)
        raw = sb("raw", [P, RING, UNIT])
        w_hi, w_lo = sb("w_hi", [P, RING, UNIT], F32R), sb("w_lo", [P, RING, UNIT], F32R)
        sT_hi, sT_lo = sb("sT_hi", [P, 8, S], F32R), sb("sT_lo", [P, 8, S], F32R)
        cst = sb("cst", [P, P + TRI + TRI + S])
        ident = cst[:, 0:P]
        negdist = cst[:, P:P + TRI]
        mask = cst[:, P + TRI:P + 2 * TRI]
        upto = cst[:, P + 2 * TRI:P + 2 * TRI + S]
        sel_r = sb("sel_r", [P, HEADS, P], F32R)
        ones = sb("ones", [P, 2])
        consts2 = sb("consts2", [P, 4, 2])
        colsA = sb("colsA", [P, C_B1 + LAYERS * L_COLS])
        colsL = sb("colsL", [P, L_COLS])
        gfin = sb("gfin", [P, D])
        scratch = sb("scratch", [P, D])
        stat = sb("stat", [P, 6, 6])
        soft = sb("soft", [P, 2, 16])
        inv_row = sb("inv_row", [P, S])
        part = sb("part", [P, 4])
        xmax = sb("xmax", [P, 2, 8])
        rinv = sb("rinv", [P, 16])
        lf = sb("lf", [P, 4, TOK, HEADS])
        nlf = sb("nlf", [P, TOK, P])
        cT = sb("cT", [P, S], F32R)

        qk_tok = sb("qk_tok", [P, 2, TOK, 512])
        v_tok = sb("v_tok", [P, TOK, 512])
        qkT = sb("qkT", [P, 2, 4, S])
        Pb = sb("Pb", [P, 4, 512])
        PTb = sb("PTb", [P, 4, 512])
        cu = sb("cu", [P, 2, TOK, 512])
        zb_tok = sb("zb_tok", [P, TOK, 512])
        uT = sb("uT", [P, 4, 2 + S])
        accT = sb("accT", [P, 4, S])
        kTx = sb("kTx", [P, KT, S])
        Vx = sb("Vx", [P, TOK, D])

        q_tok, k_tok = qk_tok[:, 0], qk_tok[:, 1]
        qT, kT = qkT[:, 0], qkT[:, 1]
        zc_tok, u_tok = cu[:, 0], cu[:, 1]
        xq_tok = qk_tok[:, :, :, :].rearrange("p a t n -> p (a t n)").rearrange("p (t n) -> p t n", t=TOK)
        xqT = qkT[:, :, :, :].rearrange("p a k n -> p (a k) n")
        K_tok = cu[:, :, :, :].rearrange("p a t n -> p (a t n)").rearrange("p (t n) -> p t n", t=TOK)
        mem_tok = kTx[:, :, :].rearrange("p k n -> p (k n)").rearrange("p (t n) -> p t n", t=TOK)
        o_tok, ysq = q_tok, k_tok.rearrange("p t n -> p (t n)").rearrange("p (c n) -> p c n", c=4)
        gate_scaled, gate_act, up_scaled, hid = (tiles2(Pb[:, i, :]) for i in range(4))
        gates = [None] * 4
        gates[0] = kTx[:, 0:4, :].rearrange("p k n -> p (k n)").rearrange("p (t n) -> p t n", t=TOK)
        gates[1] = kTx[:, 4:8, :].rearrange("p k n -> p (k n)").rearrange("p (t n) -> p t n", t=TOK)
        gates[2] = Vx[:, 0, :].rearrange("p (t n) -> p t n", t=TOK)
        gates[3] = Vx[:, 1, :].rearrange("p (t n) -> p t n", t=TOK)
        gbias = cu[:, :, :, :].rearrange("p a t n -> p (a t n)")
        p_tok = PTb[:, 0:2, :]
        yT = PTb[:, 2:4, :].rearrange("p a n -> p (a n)").rearrange("p (c n) -> p c n", c=4)
        pmat = zb_tok[:, :, :].rearrange("p t n -> p (t n)")
        pmat2 = uT[:, :, :].rearrange("p c n -> p (c n)")
        pw = Pb[:, 0, :].rearrange("p (g n) -> p g n", g=4)
        alibi = [accT[:, :, :].rearrange("p c n -> p (c n)"), pmat]
        m_tok = Pb[:, :, :].rearrange("p a n -> p (a n)").rearrange("p (t n) -> p t n", t=TOK)
        gpost = qk_tok[:, :, :, :].rearrange("p a t n -> p (a t n)")
        relu = Pb[:, 0:2, :]
        sq = Pb[:, 2:4, :].rearrange("p a (k n) -> p (a k) n", k=2)
        sel_in = Vx[:, 0, :].rearrange("p (h n) -> p h n", h=HEADS)
        out_tok = Vx

        ps = ctx.enter_context(nc.psum_tensor("ps", [P, 8, 512], F32))

        unit_landed = [sem(f"unit_landed{s}") for s in range(RING)]
        unit_hi, unit_lo, unit_used = sem("unit_hi"), sem("unit_lo"), sem("unit_used")
        x_in = [sem("x_in0"), sem("x_in1")]
        ident_in, cst_in, cols_in, pool_in, gbias_in, mem_in, gpost_in, gfin_in, out_sem = (
            sem(n) for n in ("ident_in", "cst_in", "cols_in", "pool_in", "gbias_in", "mem_in", "gpost_in", "gfin_in", "out_sem"))
        set_ready = sem("set_ready")
        fin_ready = sem("fin_ready")
        quarter_ready = sem("quarter_ready")
        res_ready = sem("res_ready")
        turn_T = sem("turn_T")
        turn_hi, turn_lo = sem("turn_hi"), sem("turn_lo")
        sums = sem("sums")
        rstd = sem("rstd")
        sel_ready = sem("sel_ready")
        part_sum = sem("part_sum")
        cols_ready = sem("cols_ready")
        gate_done, gate_by_rms, gate_silu, up_by_rms, hid_ready, hid_hi, hid_lo = (
            sem(n) for n in ("gate_done", "gate_by_rms", "gate_silu", "up_by_rms", "hid_ready", "hid_hi", "hid_lo"))
        half_done, relu_ready, sq_ready, sq_hi, sq_lo = (
            sem(n) for n in ("half_done", "relu_ready", "sq_ready", "sq_hi", "sq_lo"))
        inv_T, inv_ready = sem("inv_T"), sem("inv_ready")
        alibi_ready = sem("alibi_ready")
        b_pe, b_act, b_dve = Steps(sem("b_pe"), B1_PE), Steps(sem("b_act"), B1_ACT), Steps(sem("b_dve"), B1_DVE)
        l_pe, l_act, l_dve = Steps(sem("l_pe"), L_PE), Steps(sem("l_act"), L_ACT), Steps(sem("l_dve"), L_DVE)

        ST_X, ST_MEM, ST_WOUT, ST_NORM1, ST_MLP, ST_LAYER = range(6)
        ST_FFN1, ST_MIX, ST_ATT, ST_CONV, ST_XAT, ST_FFN2, NST = range(7)
        T_FFN, T_MEM, T_MIX, T_CONV, T_ATT, T_XAT = range(6)
        SQ_TILE = (0, 0, 4)
        PER_LAYER_RES, PER_LAYER_TURN, PER_LAYER_QUARTERS, PER_LAYER_SUMS = 16, 6 * BT, 15, 10

        def rstd_done(i):
            return 3 * i + 3

        def in_layer(l, i):
            return l * NST + (ST_LAYER + i)

        def rs(tile, t):
            return stat[:, tile, 4 + t:5 + t]

        def res_of(l, i):
            return l * PER_LAYER_RES + (8 + 4 * i + 4)

        def turns_before(l, i):
            return l * PER_LAYER_TURN + (3 + i) * BT

        def quarter_of(l, i, q):
            return l * PER_LAYER_QUARTERS + (12 + 3 * i + q + 1)

        def sums_of(l, i):
            return l * PER_LAYER_SUMS + (14 + 2 * i + 2)

        def tiles_of(bank):
            return ps[:, bank, :].rearrange("p (k n) -> p k n", k=2)

        block = ctx.enter_context(nc.Block())

        def slot(c):
            return c % RING

        def landed(r3, c):
            return r3 * 16 + (c // RING + 1) * 16

        def upto_unit(r3, c):
            return r3 * RING + c + 1

        @block.sync
        def _(sp):
            def load(r3, c):
                if not (isinstance(r3, int) and 3 * r3 + c < RING):
                    sp.wait_ge(unit_lo, upto_unit(r3, c - RING))
                if isinstance(r3, int):
                    src = stream[(3 * r3 + c) % TOTAL]
                else:
                    src = stream[bass.ds(r3 * RING + c, 1)].rearrange("a p n -> p (a n)")
                sp.dma_start(raw[:, slot(c), :], src).then_inc(unit_landed[slot(c)], 16)

            for half in range(2):
                cs = slice(half * 512, half * 512 + 512)
                sp.dma_start(res[:, :, cs], x[:, :, cs]).then_inc(x_in[half], 16)
            for c in range(RING):
                load(0, c)
            whole = (TOTAL - RING) // RING
            with sp.Fori(0, whole) as r:
                for s in range(RING):
                    load(r, RING + s)
            for c in range(RING + whole * RING, AHEAD):
                load(0, c)
            for t in range(TOK):
                sp.wait_ge(fin_ready, t + 1)
                sp.dma_start(out[t], out_tok[:, t, :]).then_inc(out_sem, 16)
            sp.wait_ge(out_sem, 16 * TOK)
            for s in range(RING):
                sp.wait_ge(unit_landed[s], 16 * len(range(s, AHEAD, RING)))

        @block.tensor
        def _(pe):
            def mm(bank_ap, lh, rh, start, stop):
                return nc.tensor.matmul(bank_ap, lh, rh, start=start, stop=stop)

            def wide(r3, c, part, banks, tiles=None):
                pe.wait_ge(unit_lo, upto_unit(r3, c))
                wh = w_hi[:, slot(c), :].rearrange("p (k n) -> p k n", k=4)
                wl = w_lo[:, slot(c), :].rearrange("p (k n) -> p k n", k=4)
                for k in range(4):
                    kk = 4 * part + k
                    if tiles is not None and kk % 2 == 0:
                        pe.wait_ge(turn_lo, tiles + kk // 2 + 1)
                    for t in range(TOK):
                        hi, lo = xT_hi[:, kk, t * P:(t + 1) * P], xT_lo[:, kk, t * P:(t + 1) * P]
                        mm(ps[:, banks[t], :], hi, wh[:, k, :], kk == 0, False)
                        mm(ps[:, banks[t], :], hi, wl[:, k, :], False, False)
                        last = mm(ps[:, banks[t], :], lo, wh[:, k, :], False, kk == 7)
                last.then_inc(unit_used, 1)

            def tall(r3, c, k0, base, start, stop, hi, lo, tiles=None, between=None):
                pe.wait_ge(unit_lo, upto_unit(r3, c))
                wh = w_hi[:, slot(c), :].rearrange("p (k h n) -> p k h n", k=2, h=2)
                wl = w_lo[:, slot(c), :].rearrange("p (k h n) -> p k h n", k=2, h=2)

                def xs(k, t):
                    return hi[:, k0 + k, t * P:(t + 1) * P], lo[:, k0 + k, t * P:(t + 1) * P]

                if tiles is not None:
                    pe.wait_ge(turn_lo, tiles + k0 // 2 + 1)
                if stop:
                    for half in range(2):
                        for t in range(TOK):
                            if between is not None and (half, t) == (1, 0):
                                between()
                            o = ps[:, base + 2 * half + t, :]
                            for k in range(2):
                                xh, xl = xs(k, t)
                                mm(o, xh, wh[:, k, half, :], start and k == 0, False)
                                mm(o, xh, wl[:, k, half, :], False, False)
                                last = mm(o, xl, wh[:, k, half, :], False, k == 1)
                            if (half, t) != (1, 1):
                                last.then_inc(quarter_ready, 1)
                    last.then_inc(unit_used, 1)
                    return
                for k in range(2):
                    if k == 1 and between is not None:
                        between()
                    for t in range(TOK):
                        xh, xl = xs(k, t)
                        for half in range(2):
                            mm(ps[:, base + 2 * half + t, :], xh, wh[:, k, half, :], start and k == 0, False)
                        for half in range(2):
                            mm(ps[:, base + 2 * half + t, :], xh, wl[:, k, half, :], False, False)
                        for half in range(2):
                            last = mm(ps[:, base + 2 * half + t, :], xl, wh[:, k, half, :], False, False)
                last.then_inc(unit_used, 1)

            def flipped(r3, c, part, banks, tiles=None, half_sem=None):
                pe.wait_ge(unit_lo, upto_unit(r3, c))
                wh = w_hi[:, slot(c), :].rearrange("p (k n) -> p k n", k=4)
                wl = w_lo[:, slot(c), :].rearrange("p (k n) -> p k n", k=4)

                def one(k, f):
                    kk, cs = 4 * part + k, slice(f * P, (f + 1) * P)
                    o = ps[:, banks[f // 2], (f % 2) * S:(f % 2) * S + S]
                    mm(o, wh[:, k, cs], xT_hi[:, kk, :], kk == 0 and f % 2 == 0, False)
                    mm(o, wh[:, k, cs], xT_lo[:, kk, :], False, False)
                    return mm(o, wl[:, k, cs], xT_hi[:, kk, :], False, kk == KT - 1 and f % 2 == 1)

                if part == 0:
                    for k in range(4):
                        if tiles is not None and k % 2 == 0:
                            pe.wait_ge(turn_lo, tiles + k // 2 + 1)
                        for f in range(4):
                            last = one(k, f)
                else:
                    if tiles is not None:
                        pe.wait_ge(turn_lo, tiles + BT)
                    for f in range(4):
                        for k in range(4):
                            last = one(k, f)
                        if f == 1:
                            last.then_inc(half_sem, 1)
                last.then_inc(unit_used, 1)

            def inv_turn(stat_i):
                pe.wait_ge(rstd, rstd_done(stat_i))
                for t in range(TOK):
                    last = nc.tensor.transpose(ps[:, 4, t * P:(t + 1) * P], rs(T_FFN, t).to_broadcast([P, P]), ident)
                last.then_inc(inv_T, 1)

            def turn(src, banks, wait=None):
                for k in range(KT):
                    if wait is not None:
                        wait(k)
                    for t in range(TOK):
                        last = nc.tensor.transpose(ps[:, banks[k // 2], (k % 2) * S + t * P:(k % 2) * S + (t + 1) * P],
                                                   src[:, t, k * P:(k + 1) * P], ident)
                    if k % 2 == 1:
                        last.then_inc(turn_T, 1)

            def turn_half(src, banks, k0):
                for k in range(4):
                    for t in range(TOK):
                        last = nc.tensor.transpose(ps[:, banks[k // 2], (k % 2) * S + t * P:(k % 2) * S + (t + 1) * P],
                                                   src[:, t, (k0 + k) * P:(k0 + k + 1) * P], ident)
                return last

            def scores(hp, forget):
                for e in range(2):
                    rows = slice(e * DH, e * DH + DH)
                    for t, (o0, nk) in enumerate(((0, P), (P, S))):
                        o = ps[:, 4 + e, o0:o0 + nk]
                        last = mm(o, qT[rows, hp, t * P:(t + 1) * P], kT[rows, hp, 0:nk], True, not forget)
                        if forget:
                            last = mm(o, sel_r[:, 2 * hp + e, :], cT[:, 0:nk], False, True)
                return last

            def prob_turn(hp):
                for e in range(2):
                    for b in range(3):
                        last = nc.tensor.transpose(ps[:, 4 + e, b * P:(b + 1) * P],
                                                   Pb[:, 2 * (hp % 2) + e, b * P:(b + 1) * P], ident)
                return last

            def values(hp):
                for e in range(2):
                    h = 2 * hp + e
                    pt = PTb[:, 2 * (hp % 2) + e, :]
                    c0 = TRI + e * DH
                    mm(ps[:, 4, c0:c0 + DH], pt[:, 0:P], v_tok[:, 0, h * DH:(h + 1) * DH], True, True)
                    mm(ps[:, 5, c0:c0 + DH], pt[:, P:2 * P], v_tok[:, 0, h * DH:(h + 1) * DH], True, False)
                    last = mm(ps[:, 5, c0:c0 + DH], pt[:, 2 * P:3 * P], v_tok[:, 1, h * DH:(h + 1) * DH], False, True)
                return last

            A, B, N = (0, 1), (2, 3), (4, 5, 6, 7)
            BB = lambda n: b_dve.upto(n)

            pe.wait_ge(ident_in, 16)
            turn(res, N, wait=lambda k: pe.wait_ge(x_in[k // 4], 16))
            wide(0, 0, 0, A, tiles=0)
            wide(0, 1, 1, A, tiles=0)
            wide(0, 2, 0, B)
            pe.wait_ge(b_act.sem, b_act.upto("p"))
            pe.wait_ge(pool_in, 48)
            for g in range(4):
                o = ps[:, 6 + g // 2, (g % 2) * S:(g % 2) * S + S]
                pm = pmat if g < 2 else pmat2
                o0 = (g % 2) * TRI
                mm(o, p_tok[:, 0, g * P:(g + 1) * P], pm[:, o0:o0 + S], True, False)
                last = mm(o[:, P:S], p_tok[:, 1, g * P:(g + 1) * P], pm[:, o0 + S:o0 + TRI], False, True)
            last.then_inc(b_pe.sem, b_pe.one("pool_mean"))
            wide(0, 3, 1, B)
            wide(0, 4, 0, A)
            pe.wait_ge(b_dve.sem, BB("yT"))
            for g in range(4):
                last = mm(ps[:, 4 + g // 2, (g % 2) * S:(g % 2) * S + S], pw[:, g, :], yT[:, g, :], True, True)
            last.then_inc(b_pe.sem, b_pe.one("pool_mix"))
            wide(0, 5, 1, A)
            pe.wait_ge(b_act.sem, b_act.upto("q"))
            wide(0, 6, 0, B)
            turn_half(q_tok, (6, 7), 0).then_inc(b_pe.sem, b_pe.one("Tq"))
            wide(0, 7, 1, B)
            pe.wait_ge(b_dve.sem, BB("k"))
            turn_half(k_tok, (4, 5), 0).then_inc(b_pe.sem, b_pe.one("Tk"))
            for i in range(8):
                hp = i // 2
                if i == 2:
                    pe.wait_ge(b_act.sem, b_act.upto("v"))
                if i in (4, 6):
                    pe.wait_ge(b_dve.sem, BB(f"gate{hp - 2}"))
                wide(0, 8 + i, i % 2, (A, B)[hp % 2])
                if i % 2 == 0:
                    if hp:
                        pe.wait_ge(b_dve.sem, BB(f"PT{hp - 1}"))
                        values(hp - 1).then_inc(b_pe.sem, b_pe.one(f"PV{hp - 1}"))
                    else:
                        pe.wait_ge(b_act.sem, b_act.upto("qT"))
                        pe.wait_ge(b_dve.sem, BB("kT"))
                    scores(hp, False).then_inc(b_pe.sem, b_pe.one(f"S{hp}"))
                else:
                    pe.wait_ge(b_act.sem, b_act.upto(f"exp{hp}"))
                    prob_turn(hp).then_inc(b_pe.sem, b_pe.one(f"PT{hp}"))
            pe.wait_ge(b_dve.sem, BB("gate3"))

            def values3():
                pe.wait_ge(b_dve.sem, BB("PT3"))
                values(3).then_inc(b_pe.sem, b_pe.one("PV3"))

            tall(0, 16, 0, 0, True, False, sT_hi, sT_lo, between=values3)
            pe.wait_ge(b_dve.sem, BB("O3"))
            turn_half(o_tok, (6, 7), 0).then_inc(b_pe.sem, b_pe.one("To"))
            tall(0, 17, 2, 0, False, True, sT_hi, sT_lo)
            pe.wait_ge(b_dve.sem, BB("oT_lo"))
            tall(0, 18, 4, 4, True, False, sT_hi, sT_lo)
            tall(0, 19, 6, 4, False, True, sT_hi, sT_lo)
            turn(m_tok, (0, 1, 2, 3), wait=lambda k: pe.wait_ge(b_dve.sem, BB("mh0" if k < 4 else "mh1")))
            for i in range(4):
                tall(0, 20 + i, 2 * i, 4, i == 0, i == 3, xT_hi, xT_lo, tiles=BT)

            turn(res, N, wait=lambda k: pe.wait_ge(res_ready, 2 if k < 4 else 4))

            def up(r3, c, jr, j, banks, tiles=None):
                if j >= 2:
                    pe.wait_ge(relu_ready, 2 * (jr + j))
                flipped(r3, c, 0, banks, tiles)
                flipped(r3, c + 1, 1, banks, tiles, half_done)

            def down1(r3, c, jr, j, tile, start=False, stop=False):
                pe.wait_ge(sq_lo, jr + j + 1)
                tall(r3, c, tile, 4, start, False, sT_hi, sT_lo)
                tall(r3, c + 1, tile + 2, 4, False, stop, sT_hi, sT_lo)

            c0 = B1_UNITS - B1_MLP
            up(0, c0, 0, 0, A, tiles=2 * BT)
            inv_turn(ST_NORM1)
            up(0, c0 + 2, 0, 1, B)
            down1(0, c0 + 4, 0, 0, 0, start=True)
            with pe.Fori(0, 2) as r:
                for b in range(3):
                    c = c0 + 6 + 4 * b
                    up(r * 4, c, r * 3, b + 2, A)
                    down1(r * 4, c + 2, r * 3, b + 1, SQ_TILE[(b + 2) % 3])
            down1(0, c0 + 30, 0, 7, SQ_TILE[2], stop=True)

            with pe.Fori(0, LAYERS) as l:
                def ffn(which, base):
                    L3 = l * (LAYER // 3)
                    fb = l * (2 * FB)
                    f0 = which * FB
                    before = res_of(l, -1 if which == 0 else 2)
                    turn(res, N, wait=lambda k: pe.wait_ge(res_ready, before - 2 if k < 4 else before))
                    tl = turns_before(l, 0 if which == 0 else 5)

                    def gate_up(r3, c, jr, j, banks, tiles=None):
                        if j >= 2 or not isinstance(jr, int):
                            pe.wait_ge(up_by_rms, fb + jr + (f0 + j))
                        flipped(r3, c, 0, banks, tiles)
                        flipped(r3, c + 1, 1, banks, tiles, gate_done)

                    def down(r3, c, jr, j, start=False, stop=False, k0=0):
                        pe.wait_ge(hid_lo, fb + jr + (f0 + j + 1))
                        tall(r3, c, k0, 4, start, stop, sT_hi, sT_lo)

                    gate_up(L3, base, 0, 0, A, tiles=tl)
                    inv_turn(in_layer(l, (ST_FFN1, ST_FFN2)[which]))
                    gate_up(L3, base + 2, 0, 1, B)
                    down(L3, base + 4, 0, 0, start=True)
                    with pe.Fori(1, FB - 2) as j:
                        gate_up(L3 + j, base + 2, j, 1, A)
                        down(L3 + j, base + 4, j, 0)
                    gate_up(L3, base + FFN - 4, 0, FB - 1, A)
                    down(L3, base + FFN - 2, 0, FB - 2)
                    down(L3, base + FFN - 1, 0, FB - 1, stop=True, k0=2)

                def wait_act(n):
                    pe.wait_ge(l_act.sem, l_act.upto(n, l))

                def wait_dve(n):
                    pe.wait_ge(l_dve.sem, l_dve.upto(n, l))

                ffn(0, B1_UNITS)

                L3 = l * (LAYER // 3)
                m0 = B1_UNITS + FFN
                turn(res, N, wait=lambda k: pe.wait_ge(res_ready, res_of(l, 0) - (2 if k < 4 else 0)))
                tl = turns_before(l, 1)
                wide(L3, m0, 0, A, tiles=tl)
                wide(L3, m0 + 1, 1, A, tiles=tl)
                wide(L3, m0 + 2, 0, B)
                wide(L3, m0 + 3, 1, B)
                pe.wait_ge(unit_lo, upto_unit(L3, m0 + 4))
                fh = w_hi[:, slot(m0 + 4), 0:KT * HEADS].rearrange("p (k n) -> p k n", k=KT)
                fl = w_lo[:, slot(m0 + 4), 0:KT * HEADS].rearrange("p (k n) -> p k n", k=KT)
                for k in range(KT):
                    for t in range(TOK):
                        hi, lo = xT_hi[:, k, t * P:(t + 1) * P], xT_lo[:, k, t * P:(t + 1) * P]
                        mm(ps[:, 4 + t, 0:HEADS], hi, fh[:, k, :], k == 0, False)
                        mm(ps[:, 4 + t, 0:HEADS], hi, fl[:, k, :], False, False)
                        last = mm(ps[:, 4 + t, 0:HEADS], lo, fh[:, k, :], False, k == KT - 1)
                last.then_inc(unit_used, 1)
                wait_act("q")
                wide(L3, m0 + 5, 0, A)
                turn_half(q_tok, (6, 7), 0).then_inc(l_pe.sem, l_pe.one("Tq"))
                wide(L3, m0 + 6, 1, A)
                wait_dve("f")
                turn_half(k_tok, (4, 5), 0).then_inc(l_pe.sem, l_pe.one("Tk"))
                wide(L3, m0 + 7, 0, B)
                wait_act("qT")
                wait_dve("logf")
                mm(ps[:, 6, 0:S], nlf[:, 0, :], upto, True, False)
                mm(ps[:, 6, P:S], nlf[:, 1, :], upto[:, 0:P], False, True).then_inc(l_pe.sem, l_pe.one("cT"))
                wide(L3, m0 + 8, 1, B)
                wait_dve("cT")
                scores(0, True).then_inc(l_pe.sem, l_pe.one("S0"))
                wait_act("v")
                wide(L3, m0 + 9, 0, A)
                wait_act("exp0")
                prob_turn(0).then_inc(l_pe.sem, l_pe.one("PT0"))
                wide(L3, m0 + 10, 1, A)
                wait_dve("PT0")
                values(0).then_inc(l_pe.sem, l_pe.one("PV0"))
                scores(1, True).then_inc(l_pe.sem, l_pe.one("S1"))
                wait_act("zc")
                wide(L3, m0 + 11, 0, B)
                wait_act("exp1")
                prob_turn(1).then_inc(l_pe.sem, l_pe.one("PT1"))
                wait_dve("u")
                turn_half(u_tok, (6, 7), 0).then_inc(l_pe.sem, l_pe.one("Tu"))
                wide(L3, m0 + 12, 1, B)
                wait_dve("PT1")
                values(1).then_inc(l_pe.sem, l_pe.one("PV1"))
                scores(2, True).then_inc(l_pe.sem, l_pe.one("S2"))
                pe.wait_ge(mem_in, l * 16 + 32)

                def mem_wait(k):
                    if k == 0:
                        wait_act("uT")
                    if k == 4:
                        wait_act("zb")
                turn(mem_tok, (6, 7, 2, 3), wait=mem_wait)
                tl = turns_before(l, 2)
                wide(L3, m0 + 13, 0, A, tiles=tl)
                wait_act("exp2")
                prob_turn(2).then_inc(l_pe.sem, l_pe.one("PT2"))
                wide(L3, m0 + 14, 1, A, tiles=tl)
                wait_dve("PT2")
                values(2).then_inc(l_pe.sem, l_pe.one("PV2"))
                scores(3, True).then_inc(l_pe.sem, l_pe.one("S3"))
                wide(L3, m0 + 15, 0, B)
                wait_act("exp3")
                prob_turn(3).then_inc(l_pe.sem, l_pe.one("PT3"))
                turn_half(zb_tok, (6, 7), 0).then_inc(l_pe.sem, l_pe.one("Tzb"))
                wide(L3, m0 + 16, 1, B)
                wait_dve("PT3")
                values(3).then_inc(l_pe.sem, l_pe.one("PV3"))
                wait_dve("K0")
                wide(L3, m0 + 17, 0, A)
                wait_dve("O3")
                turn_half(o_tok, (4, 5), 0).then_inc(l_pe.sem, l_pe.one("To"))
                wide(L3, m0 + 18, 1, A)
                wait_dve("y")
                turn_half(K_tok, (6, 7), 0).then_inc(l_pe.sem, l_pe.one("TK0"))
                wait_act("K1")
                wide(L3, m0 + 19, 0, B)
                wait_dve("KT0")
                turn_half(K_tok, (6, 7), 4).then_inc(l_pe.sem, l_pe.one("TK1"))
                wide(L3, m0 + 20, 1, B)
                wait_act("ysq")
                wait_dve("V0")
                for t in range(TOK):
                    for k in range(4):
                        last = mm(ps[:, 0, 2 * t:2 * t + 2], ysq[:, k, t * P:(t + 1) * P], ones[:, 0:2], k == 0, k == 3)
                last.then_inc(l_pe.sem, l_pe.one("ssq"))
                wait_dve("ycT_lo")
                wait_dve("oT_lo")
                wait_dve("KT1")
                tall(L3, m0 + 21, 0, 4, True, False, sT_hi, sT_lo)
                tall(L3, m0 + 22, 2, 4, False, True, sT_hi, sT_lo)
                wait_dve("ssq")
                wait_act("V1")
                tall(L3, m0 + 23, 4, 0, True, False, sT_hi, sT_lo)
                tall(L3, m0 + 24, 6, 0, False, True, sT_hi, sT_lo)

                turn(res, N, wait=lambda k: pe.wait_ge(res_ready, res_of(l, 1) - (2 if k < 4 else 0)))
                tl = turns_before(l, 3)
                wide(L3, m0 + 25, 0, A, tiles=tl)
                wide(L3, m0 + 26, 1, A, tiles=tl)
                wide(L3, m0 + 27, 0, B)
                wait_act("xq0")
                turn_half(xq_tok, (4, 5), 0).then_inc(l_pe.sem, l_pe.one("TX0"))
                wide(L3, m0 + 28, 1, B)
                wait_dve("xq1")
                wait_act("xq1")
                turn_half(xq_tok, (6, 7), 4).then_inc(l_pe.sem, l_pe.one("TX1"))
                for h in range(XH):
                    if h == 0:
                        wait_act("xqT0")
                    if h == 2:
                        wait_dve("xqT1")
                    for t in range(TOK):
                        for k in range(2):
                            last = mm(ps[:, h, t * S:(t + 1) * S], xqT[:, 2 * h + k, t * P:(t + 1) * P],
                                      kTx[:, 2 * h + k, :], k == 0, k == 1)
                    last.then_inc(l_pe.sem, l_pe.one(f"SX{h}"))
                for h in range(XH):
                    wait_act(f"xexp{h}")
                    for m in range(2):
                        for t in range(TOK):
                            last = nc.tensor.transpose(ps[:, 4 + h, m * S + t * P:m * S + (t + 1) * P],
                                                       Pb[:, h, t * S + m * P:t * S + (m + 1) * P], ident)
                    last.then_inc(l_pe.sem, l_pe.one(f"PX{h}"))
                for half in range(2):
                    for e in range(2):
                        h = 2 * half + e
                        if h % 2 == 0:
                            wait_act(f"PX{h}")
                        else:
                            wait_dve(f"PX{h}")
                        for t in range(TOK):
                            for m in range(2):
                                last = mm(ps[:, 2 * half + t, e * XDH:(e + 1) * XDH],
                                          PTb[:, h, m * S + t * P:m * S + (t + 1) * P],
                                          Vx[:, m, h * XDH:(h + 1) * XDH], m == 0, m == 1)
                    last.then_inc(l_pe.sem, l_pe.one(f"OX{half}"))

                def o_wait(k):
                    if k % 4 == 0:
                        wait_dve(f"xo{k // 4}")
                turn(xq_tok, N, wait=o_wait)
                tl = turns_before(l, 4)
                for i in range(4):
                    tall(L3, m0 + 29 + i, 2 * i, 0, i == 0, i == 3, xT_hi, xT_lo, tiles=tl)

                ffn(1, B1_UNITS + FFN + MID)
            b_pe.closed()
            l_pe.closed()

        @block.scalar
        def _(act):
            copy, square, exp = ACT.Copy, ACT.Square, ACT.Exp

            def round_unit(r3, c):
                act.wait_ge(unit_landed[slot(c)], landed(r3, c))
                if not (isinstance(r3, int) and c < RING):
                    act.wait_ge(unit_used, upto_unit(r3, c - RING))
                nc.scalar.activation(w_hi[:, slot(c), :], raw[:, slot(c), :], copy).then_inc(unit_hi, 1)

            def turn_round(before, banks, gain):
                for b in range(BT):
                    act.wait_ge(turn_T, before + b + 1)
                    if gain is None:
                        last = nc.scalar.activation(xT_hi[:, 2 * b:2 * b + 2, :], tiles_of(banks[b]), copy)
                    else:
                        for k in (2 * b, 2 * b + 1):
                            last = nc.scalar.activation(xT_hi[:, k, :], tiles_of(banks[b])[:, k % 2, :], copy,
                                                        scale=gain[:, k:k + 1])
                    last.then_inc(turn_hi, 1)

            def squares(src, tile, before):
                for t in range(TOK):
                    if t or not isinstance(before, int) or before:
                        act.wait_ge(sums, before + t)
                    ap = src(t)
                    out_ = scratch[:, 0:ap.free_size()]
                    if len(ap.shape) == 3:
                        out_ = out_.rearrange("p (a n) -> p a n", a=ap.shape[1])
                    nc.scalar.activation(out_, ap, square, accum_out=stat[:, tile, t:t + 1]).then_inc(sums, 1)

            def product_squares(i, last_unit, before):
                for q in range(4):
                    if q < 3:
                        act.wait_ge(quarter_ready, 3 * i + q + 1)
                    else:
                        act.wait_ge(unit_used, upto_unit(*last_unit))
                    act.wait_ge(sums, before + q)
                    nc.scalar.activation(scratch[:, 0:512], ps[:, 4 + q, :], square,
                                         accum_out=part[:, q:q + 1]).then_inc(sums, 1)

            def probs(hp):
                for e in range(2):
                    h = 2 * hp + e
                    for t, (o0, nk) in enumerate(((0, P), (P, S))):
                        pr = Pb[:, 2 * (hp % 2) + e, o0:o0 + nk]
                        last = nc.scalar.activation(pr, pr, exp, scale=-1.0, bias=soft[:, 0, 8 * t + h:8 * t + h + 1],
                                                    accum_out=soft[:, 1, 8 * t + h:8 * t + h + 1])
                return last

            A, B, N = (0, 1), (2, 3), (4, 5, 6, 7)
            res_t = lambda t: res[:, t, :]

            def used(r3, c):
                act.wait_ge(unit_used, upto_unit(r3, c))

            def projected(banks, dst, tile):
                for t in range(TOK):
                    last = nc.scalar.activation(dst(t), ps[:, banks[t], :], copy, scale=rs(tile, t))
                return last

            act.dma_start(cst[:, 0:P], consts[:, 0:P]).then_inc(ident_in, 16)
            act.dma_start(colsA[:], cols).then_inc(cols_in, 16)
            act.dma_start(cst[:, P:], consts[:, P:]).then_inc(cst_in, 16)
            act.dma_start(pmat[:, 0:2 * TRI], poolmat[:, 0:2 * TRI]).then_inc(pool_in, 16)
            act.dma_start(pmat2[:, 0:2 * TRI], poolmat[:, 2 * TRI:4 * TRI]).then_inc(pool_in, 16)
            act.dma_start(pw, poolw).then_inc(pool_in, 16)
            act.dma_start(mem_tok, mem).then_inc(mem_in, 16)
            act.dma_start(gbias, gate_bias).then_inc(gbias_in, 16)
            act.dma_start(gfin[:], final_gain).then_inc(gfin_in, 16)
            act.dma_start(sel_in, sel).then_inc(gfin_in, 16)

            def wait_pe1(n):
                act.wait_ge(b_pe.sem, b_pe.upto(n))

            def wait_dve1(n):
                act.wait_ge(b_dve.sem, b_dve.upto(n))

            def did1(ins, n):
                ins.then_inc(b_act.sem, b_act.one(n))

            act.wait_ge(cols_in, 16)
            turn_round(0, N, colsA[:, C_MIXPRE:C_MIXPRE + KT])
            round_unit(0, 0)
            round_unit(0, 1)
            squares(res_t, T_FFN, 0)
            round_unit(0, 2)
            act.wait_ge(mem_in, 16)
            squares(lambda t: mem_tok[:, t, :], T_MEM, 2)
            act.wait_ge(gfin_in, 32)
            nc.scalar.activation(sel_r[:], sel_in, copy).then_inc(sel_ready, 1)
            round_unit(0, 3)
            used(0, 1)
            act.wait_ge(rstd, rstd_done(ST_X))
            did1(projected(A, lambda t: p_tok[:, t, :], T_FFN), "p")
            round_unit(0, 4)
            round_unit(0, 5)
            used(0, 3)
            did1(projected(B, lambda t: q_tok[:, t, :], T_FFN), "q")
            round_unit(0, 6)
            wait_pe1("pool_mix")
            for g in range(4):
                last = nc.scalar.activation(sT_hi[:, g, :], ps[:, 4 + g // 2, (g % 2) * S:(g % 2) * S + S], copy,
                                            scale=colsA[:, C_PSCALE + g:C_PSCALE + g + 1])
            did1(last, "ypT_hi")
            round_unit(0, 7)
            round_unit(0, 8)
            wait_pe1("Tq")
            did1(nc.scalar.activation(qT, ps[:, 6:8, :].rearrange("p b (k n) -> p (b k) n", k=2), copy, scale=DH ** -0.5), "qT")
            round_unit(0, 9)
            used(0, 7)
            did1(projected(B, lambda t: v_tok[:, t, :], T_FFN), "v")
            round_unit(0, 10)
            for hp in range(PAIRS):
                round_unit(0, 11 + 2 * hp)
                wait_dve1(f"soft{hp}")
                did1(probs(hp), f"exp{hp}")
                round_unit(0, 12 + 2 * hp)
            for i in range(4):
                wait_dve1(f"gate{i}")
                did1(nc.scalar.activation(gates[i], gates[i], ACT.Sigmoid), f"sig{i}")
            wait_pe1("To")
            did1(nc.scalar.activation(sT_hi[:, 4:8, :], ps[:, 6:8, :].rearrange("p b (k n) -> p (b k) n", k=2), copy), "oT_hi")
            act.dma_start(gpost, post_gain).then_inc(gpost_in, 16)
            round_unit(0, 19)
            round_unit(0, 20)
            round_unit(0, 21)
            turn_round(BT, (0, 1, 2, 3), None)
            round_unit(0, 22)
            round_unit(0, 23)
            round_unit(0, 24)
            round_unit(0, 25)
            product_squares(2, (0, 23), 4)
            turn_round(2 * BT, N, colsA[:, C_MLPPRE:C_MLPPRE + KT])
            c0 = B1_UNITS - B1_MLP
            round_unit(0, c0 + 2)
            squares(res_t, T_FFN, 8)

            def sq_round(jr, j, tile):
                act.wait_ge(sq_ready, jr + j + 1)
                nc.scalar.activation(sT_hi[:, tile:tile + 4, :], sq, copy).then_inc(sq_hi, 1)

            round_unit(0, c0 + 3)
            round_unit(0, c0 + 4)
            sq_round(0, 0, 0)
            round_unit(0, c0 + 5)
            round_unit(0, c0 + 6)
            round_unit(0, c0 + 7)
            sq_round(0, 1, 4)
            round_unit(0, c0 + 8)
            with act.Fori(0, 2) as r:
                for b in range(3):
                    c = c0 + 6 + 4 * b
                    round_unit(r * 4, c + 3)
                    round_unit(r * 4, c + 4)
                    if b != 1:
                        sq_round(r * 3, b + 2, SQ_TILE[b])
                    round_unit(r * 4, c + 5)
                    if b == 1:
                        used(r * 4, c + 3)
                        sq_round(r * 3, b + 2, SQ_TILE[b])
                    round_unit(r * 4, c + 6)
            round_unit(0, c0 + 33)
            product_squares(3, (0, c0 + 31), 10)
            b_act.closed()

            with act.Fori(0, LAYERS) as l:
                L3 = l * (LAYER // 3)

                def wait_pe(n):
                    act.wait_ge(l_pe.sem, l_pe.upto(n, l))

                def wait_dve(n):
                    act.wait_ge(l_dve.sem, l_dve.upto(n, l))

                def did(ins, n):
                    ins.then_inc(l_act.sem, l_act.one(n))

                def ffn(which, base):
                    fb = l * (2 * FB)
                    f0 = which * FB
                    if which == 0:
                        act.wait_ge(cols_ready, l + 1)
                    g = colsL[:, (L_FFN1, L_FFN2)[which]:][:, 0:KT]
                    turn_round(turns_before(l, 0 if which == 0 else 5), N, g)
                    round_unit(L3, base + 2)
                    squares(res_t, T_FFN, sums_of(l, (0, 4)[which]) - 2)

                    def gate(jr, j):
                        act.wait_ge(gate_by_rms, fb + jr + (f0 + j + 1))
                        nc.scalar.activation(gate_act, gate_scaled, ACT.Silu).then_inc(gate_silu, 1)

                    def hid_round(jr, j, k0=0):
                        act.wait_ge(hid_ready, fb + jr + (f0 + j + 1))
                        nc.scalar.activation(sT_hi[:, k0:k0 + 2, :], hid, copy).then_inc(hid_hi, 1)

                    round_unit(L3, base + 3)
                    round_unit(L3, base + 4)
                    gate(0, 0)
                    hid_round(0, 0)
                    round_unit(L3, base + 5)
                    gate(0, 1)
                    round_unit(L3, base + 6)
                    used(L3, base + 4)
                    hid_round(0, 1)
                    round_unit(L3, base + 7)
                    with act.Fori(1, FB - 2) as j:
                        round_unit(L3 + j, base + 5)
                        gate(j, 1)
                        round_unit(L3 + j, base + 6)
                        used(L3 + j, base + 4)
                        hid_round(j, 1)
                        round_unit(L3 + j, base + 7)
                    round_unit(L3, base + FFN - 1)
                    gate(0, FB - 1)
                    hid_round(0, FB - 1, k0=2)
                    round_unit(L3, base + FFN)
                    round_unit(L3, base + FFN + 1)

                act.wait_ge(b_dve.sem, b_dve.upto("postmlp"))
                act.dma_start(mem_tok, mem).then_inc(mem_in, 16)
                ffn(0, B1_UNITS)

                m0 = B1_UNITS + FFN

                def unit(i):
                    round_unit(L3, m0 + i)

                turn_round(turns_before(l, 1), N, colsL[:, L_MIX:L_MIX + KT])
                unit(2)
                squares(res_t, T_MIX, sums_of(l, 1) - 2)
                unit(3)
                act.wait_ge(rstd, rstd_done(in_layer(l, ST_MIX)))
                used(L3, m0 + 1)
                did(projected(A, lambda t: q_tok[:, t, :], T_MIX), "q")
                unit(4)
                unit(5)
                unit(6)
                unit(7)
                wait_pe("Tq")
                did(nc.scalar.activation(qT, ps[:, 6:8, :].rearrange("p b (k n) -> p (b k) n", k=2), copy, scale=DH ** -0.5), "qT")
                wait_dve("fabs")
                did(nc.scalar.activation(lf[:, 2], lf[:, 1], exp, scale=-1.0), "fexp")
                act.wait_ge(l_act.sem, l_act.upto("fexp", l))
                did(nc.scalar.activation(lf[:, 3], lf[:, 2], ACT.Ln, bias=1.0), "fln")
                unit(8)
                used(L3, m0 + 6)
                did(projected(A, lambda t: v_tok[:, t, :], T_MIX), "v")
                unit(9)
                wait_pe("cT")
                did(nc.scalar.activation(cT[:], ps[:, 6, 0:S], copy), "cT_hi")
                unit(10)
                used(L3, m0 + 8)
                did(projected(B, lambda t: zc_tok[:, t, :], T_MIX), "zc")
                unit(11)
                wait_dve("soft0")
                did(probs(0), "exp0")
                unit(12)
                unit(13)
                wait_dve("soft1")
                did(probs(1), "exp1")
                unit(14)
                wait_pe("Tu")
                did(nc.scalar.activation(uT[:, :, 2:2 + S], ps[:, 6:8, :].rearrange("p b (k n) -> p (b k) n", k=2), copy), "uT")
                used(L3, m0 + 12)
                did(projected(B, lambda t: zb_tok[:, t, :], T_MIX), "zb")
                turn_round(turns_before(l, 2), (6, 7, 2, 3), colsL[:, L_MEM:L_MEM + KT])
                wait_dve("soft2")
                did(probs(2), "exp2")
                unit(15)
                unit(16)
                unit(17)
                wait_dve("soft3")
                did(probs(3), "exp3")
                unit(18)
                wait_dve("y")
                for c in range(4):
                    last = nc.scalar.activation(sT_hi[:, c, :], accT[:, c, :], copy, scale=colsL[:, L_CONV + c:L_CONV + c + 1])
                did(last, "yc_hi")
                did(nc.scalar.activation(ysq, accT[:, :, :], square), "ysq")
                used(L3, m0 + 16)
                did(projected(B, lambda t: K_tok[:, t, 512:1024], T_MEM), "K1")
                unit(19)
                wait_pe("To")
                for c in range(4):
                    last = nc.scalar.activation(sT_hi[:, 4 + c, :], ps[:, 4 + c // 2, (c % 2) * S:(c % 2) * S + S], copy,
                                                scale=colsL[:, L_ATT + c:L_ATT + c + 1])
                did(last, "oT_hi")
                squares(lambda t: o_tok[:, t, :], T_ATT, sums_of(l, 2) - 2)
                unit(20)
                unit(21)
                unit(22)
                used(L3, m0 + 20)
                did(projected(B, lambda t: Vx[:, t, 512:1024], T_MEM), "V1")
                for i in range(23, 27):
                    unit(i)

                turn_round(turns_before(l, 3), N, colsL[:, L_XAT:L_XAT + KT])
                unit(27)
                squares(res_t, T_XAT, sums_of(l, 3) - 2)
                unit(28)
                act.wait_ge(rstd, rstd_done(in_layer(l, ST_XAT)))
                used(L3, m0 + 26)
                did(projected(A, lambda t: xq_tok[:, t, 0:512], T_XAT), "xq0")
                unit(29)
                wait_pe("TX0")
                did(nc.scalar.activation(xqT[:, 0:4, :], ps[:, 4:6, :].rearrange("p b (k n) -> p (b k) n", k=2), copy,
                                         scale=XDH ** -0.5), "xqT0")
                unit(30)
                used(L3, m0 + 28)
                did(nc.scalar.activation(xq_tok[:, 0, 512:1024], ps[:, 2, :], copy, scale=rs(T_XAT, 0)), "xq1")
                for h in range(XH):
                    wait_dve(f"xneg{h}")
                    for t in range(TOK):
                        last = nc.scalar.activation(Pb[:, h, t * S:(t + 1) * S], ps[:, h, t * S:(t + 1) * S], exp,
                                                    bias=xmax[:, 1, 2 * h + t:2 * h + t + 1],
                                                    accum_out=soft[:, 1, 8 * t + h:8 * t + h + 1])
                    did(last, f"xexp{h}")
                for h in (0, 2):
                    wait_pe(f"PX{h}")
                    did(nc.scalar.activation(PTb[:, h, :], ps[:, 4 + h, :], copy), f"PX{h}")
                turn_round(turns_before(l, 4), N, None)
                for i in range(31, 35):
                    unit(i)

                ffn(1, B1_UNITS + FFN + MID)
            l_act.closed()
            act.wait_ge(res_ready, res_of(LAYERS, -1))
            squares(res_t, T_XAT, sums_of(LAYERS, 0) - 2)

        @block.vector
        def _(dve):
            sub, mul, add, mx = ALU.subtract, ALU.mult, ALU.add, ALU.max
            stt = nc.vector.scalar_tensor_tensor

            def rest_unit(r3, c):
                dve.wait_ge(unit_hi, upto_unit(r3, c))
                nc.vector.tensor_tensor(w_lo[:, slot(c), :], raw[:, slot(c), :], w_hi[:, slot(c), :].bitcast(F32),
                                        sub).then_inc(unit_lo, 1)

            def rest(dst, src, hi, gain=None):
                if gain is None:
                    return nc.vector.tensor_tensor(dst, src, hi.bitcast(F32), sub)
                return stt(out=dst, in0=src, scalar=gain, in1=hi.bitcast(F32), op0=mul, op1=sub)

            def turn_rest(before, banks, gain):
                for b in range(BT):
                    dve.wait_ge(turn_hi, before + b + 1)
                    if gain is None:
                        last = rest(xT_lo[:, 2 * b:2 * b + 2, :], tiles_of(banks[b]), xT_hi[:, 2 * b:2 * b + 2, :])
                    else:
                        for k in (2 * b, 2 * b + 1):
                            last = rest(xT_lo[:, k, :], tiles_of(banks[b])[:, k % 2, :], xT_hi[:, k, :], gain[:, k:k + 1])
                    last.then_inc(turn_lo, 1)

            def used(r3, c):
                dve.wait_ge(unit_used, upto_unit(r3, c))

            def projected(banks, dst, tile):
                for t in range(TOK):
                    last = nc.vector.tensor_scalar(dst(t), ps[:, banks[t], :], rs(tile, t), None, mul)
                return last

            def two_banks(b):
                return ps[:, b:b + 2, :].rearrange("p b (k n) -> p (b k) n", k=2)

            def maxima(hp, bias):
                for e in range(2):
                    h = 2 * hp + e
                    for t, (o0, nk) in enumerate(((0, P), (P, S))):
                        last = nc.vector.tensor_tensor_reduce(
                            out=Pb[:, 2 * (hp % 2) + e, o0:o0 + nk], in0=ps[:, 4 + e, o0:o0 + nk],
                            in1=bias(e)[:, o0:o0 + nk], scale=-1.0, scalar=BIG, op0=add, op1=ALU.min,
                            accum_out=soft[:, 0, 8 * t + h:8 * t + h + 1])
                return last

            def pair(ap, hp):
                return ap.rearrange("p (t h) -> p t h", t=2)[:, :, 2 * hp:2 * hp + 2]

            def inverse_sums(hp):
                return nc.vector.reciprocal(pair(rinv[:], hp), pair(soft[:, 1, :], hp))

            def probs_T(hp):
                a = 2 * (hp % 2)
                return nc.vector.tensor_copy(PTb[:, a:a + 2, 0:TRI], ps[:, 4:6, 0:TRI])

            def values_out(hp):
                for t in range(TOK):
                    o = o_tok[:, t, hp * P:(hp + 1) * P].rearrange("p (e d) -> p e d", e=2)
                    r = rinv[:, 8 * t + 2 * hp:8 * t + 2 * hp + 2].unsqueeze(2).to_broadcast([P, 2, DH])
                    last = nc.vector.tensor_tensor(o, ps[:, 4 + t, TRI:512].rearrange("p (e d) -> p e d", e=2), r, mul)
                return last

            A, B, N = (0, 1), (2, 3), (4, 5, 6, 7)

            def wait_pe1(n):
                dve.wait_ge(b_pe.sem, b_pe.upto(n))

            def wait_act1(n):
                dve.wait_ge(b_act.sem, b_act.upto(n))

            def wait_own1(n):
                dve.wait_ge(b_dve.sem, b_dve.upto(n))

            def did1(ins, n):
                ins.then_inc(b_dve.sem, b_dve.one(n))

            turn_rest(0, N, colsA[:, C_MIXPRE:C_MIXPRE + KT])
            for c in range(6):
                rest_unit(0, c)
            wait_pe1("pool_mean")
            did1(nc.vector.tensor_copy(yT, two_banks(6)), "yT")
            rest_unit(0, 6)
            wait_act1("ypT_hi")
            for g in range(4):
                last = rest(sT_lo[:, g, :], two_banks(4)[:, g, :], sT_hi[:, g, :], colsA[:, C_PSCALE + g:C_PSCALE + g + 1])
            did1(last, "ypT_lo")
            rest_unit(0, 7)
            used(0, 5)
            did1(projected(A, lambda t: k_tok[:, t, :], T_FFN), "k")
            rest_unit(0, 8)
            rest_unit(0, 9)
            wait_pe1("Tk")
            did1(nc.vector.tensor_copy(kT, two_banks(4)), "kT")
            rest_unit(0, 10)
            dve.wait_ge(gbias_in, 16)
            for hp in range(PAIRS):
                wait_pe1(f"S{hp}")
                if hp:
                    did1(values_out(hp - 1), f"O{hp - 1}")
                dve.wait_ge(alibi_ready, hp + 1)
                did1(maxima(hp, lambda e: alibi[hp % 2][:, e * TRI:(e + 1) * TRI]), f"soft{hp}")
                rest_unit(0, 11 + 2 * hp)
                used(0, 9 + 2 * hp)
                if hp == 0:
                    dve.wait_ge(sums, 4)
                for t in range(TOK):
                    last = stt(out=gates[hp][:, t, :], in0=ps[:, (A, B)[hp % 2][t], :], scalar=rs(T_FFN, t),
                               in1=gbias[:, hp * 512:(hp + 1) * 512], op0=mul, op1=add)
                did1(last, f"gate{hp}")
                wait_act1(f"exp{hp}")
                did1(inverse_sums(hp), f"rinv{hp}")
                wait_pe1(f"PT{hp}")
                did1(probs_T(hp), f"PT{hp}")
                wait_own1(f"rinv{hp}")
                rest_unit(0, 12 + 2 * hp)
            wait_pe1("PV3")
            did1(values_out(3), "O3")
            wait_act1("oT_hi")
            did1(rest(sT_lo[:, 4:8, :], two_banks(6), sT_hi[:, 4:8, :]), "oT_lo")
            rest_unit(0, 19)
            wait_act1("sig3")
            used(0, 17)
            for half in range(2):
                for t in range(TOK):
                    last = nc.vector.tensor_tensor(m_tok[:, t, half * 512:half * 512 + 512], gates[half][:, t, :],
                                                   ps[:, 2 * half + t, :], mul)
            did1(last, "m1")
            rest_unit(0, 20)
            rest_unit(0, 21)
            wait_own1("m1")
            for q in range(4):
                half, t = divmod(q, TOK)
                if q < 3:
                    dve.wait_ge(quarter_ready, 3 + q + 1)
                else:
                    used(0, 19)
                did1(nc.vector.tensor_tensor(PTb[:, q, :], gates[2 + half][:, t, :], ps[:, 4 + q, :], mul), f"m2q{q}")
                if t == 1:
                    for t in range(TOK):
                        wait_own1(f"m2q{2 * half + t}")
                        mq = m_tok[:, t, half * 512:half * 512 + 512]
                        last = nc.vector.tensor_tensor(mq, mq, PTb[:, 2 * half + t, :], add)
                    did1(last, f"mh{half}")
            turn_rest(BT, (0, 1, 2, 3), None)
            for c in range(22, 26):
                rest_unit(0, c)

            def post_norm(stat_i, gain, name, before):
                dve.wait_ge(gpost_in, 16)
                for q in range(4):
                    half, t = divmod(q, TOK)
                    dve.wait_ge(sums, before + q + 1)
                    last = nc.vector.tensor_tensor(Pb[:, q, :], ps[:, 4 + q, :], gain[:, half * 512:half * 512 + 512], mul)
                did1(last, name)
                dve.wait_ge(rstd, rstd_done(stat_i))
                wait_own1(name)
                for q in range(4):
                    half, t = divmod(q, TOK)
                    r = res[:, t, half * 512:half * 512 + 512]
                    stt(out=r, in0=Pb[:, q, :], scalar=rs(T_MIX, t), in1=r, op0=mul, op1=add).then_inc(res_ready, 1)

            post_norm(ST_WOUT, gpost[:, 0:D], "postmix", 4)
            turn_rest(2 * BT, N, colsA[:, C_MLPPRE:C_MLPPRE + KT])
            c0 = B1_UNITS - B1_MLP
            rest_unit(0, c0 + 2)
            rest_unit(0, c0 + 3)

            def inv_copy(n):
                dve.wait_ge(inv_T, n)
                nc.vector.tensor_copy(inv_row[:], ps[:, 4, 0:S]).then_inc(inv_ready, 1)
                dve.wait_ge(inv_ready, n)

            inv_both = inv_row[:, :].unsqueeze(1).to_broadcast([P, 2, S])

            def squared(r3, c, jr, j, banks):
                if j:
                    dve.wait_ge(sq_lo, jr + j)
                for half in range(2):
                    if half == 0:
                        dve.wait_ge(half_done, jr + j + 1)
                    else:
                        used(r3, c)
                    stt(out=tiles2(relu[:, half, :]), in0=tiles_of(banks[half]), scalar=0.0, in1=inv_both, op0=mx,
                        op1=mul).then_inc(relu_ready, 1)
                dve.wait_ge(relu_ready, 2 * (jr + j + 1))
                r = relu.rearrange("p a (k n) -> p (a k) n", k=2)
                nc.vector.tensor_tensor(sq, r, r, mul).then_inc(sq_ready, 1)

            def sq_rest(jr, j, tile):
                dve.wait_ge(sq_hi, jr + j + 1)
                rest(sT_lo[:, tile:tile + 4, :], sq, sT_hi[:, tile:tile + 4, :]).then_inc(sq_lo, 1)

            inv_copy(1)
            squared(0, c0 + 1, 0, 0, A)
            rest_unit(0, c0 + 4)
            sq_rest(0, 0, 0)
            rest_unit(0, c0 + 5)
            squared(0, c0 + 3, 0, 1, B)
            rest_unit(0, c0 + 6)
            rest_unit(0, c0 + 7)
            sq_rest(0, 1, 4)
            rest_unit(0, c0 + 8)
            with dve.Fori(0, 2) as r:
                for b in range(3):
                    c = c0 + 6 + 4 * b
                    rest_unit(r * 4, c + 3)
                    squared(r * 4, c + 1, r * 3, b + 2, A)
                    rest_unit(r * 4, c + 4)
                    if b != 1:
                        sq_rest(r * 3, b + 2, SQ_TILE[b])
                    rest_unit(r * 4, c + 5)
                    if b == 1:
                        sq_rest(r * 3, b + 2, SQ_TILE[b])
                    rest_unit(r * 4, c + 6)
            rest_unit(0, c0 + 33)
            post_norm(ST_MLP, gpost[:, D:2 * D], "postmlp", 10)
            b_dve.closed()

            with dve.Fori(0, LAYERS) as l:
                L3 = l * (LAYER // 3)

                def wait_pe(n):
                    dve.wait_ge(l_pe.sem, l_pe.upto(n, l))

                def wait_act(n):
                    dve.wait_ge(l_act.sem, l_act.upto(n, l))

                def wait_own(n):
                    dve.wait_ge(l_dve.sem, l_dve.upto(n, l))

                def did(ins, n):
                    ins.then_inc(l_dve.sem, l_dve.one(n))

                def onto_res(i, last_unit, base, scale):
                    for q in range(4):
                        half, t = divmod(q, TOK)
                        if q < 3:
                            dve.wait_ge(quarter_ready, quarter_of(l, i, q))
                        else:
                            used(*last_unit)
                        r = res[:, t, half * 512:half * 512 + 512]
                        stt(out=r, in0=ps[:, base + q, :], scalar=scale(t), in1=r, op0=mul, op1=add).then_inc(res_ready, 1)

                def ffn(which, base):
                    fb = l * (2 * FB)
                    f0 = which * FB
                    turn_rest(turns_before(l, 0 if which == 0 else 5), N, colsL[:, (L_FFN1, L_FFN2)[which]:][:, 0:KT])
                    rest_unit(L3, base + 2)

                    def hidden(r3, c, jr, j, banks):
                        n = fb + jr + (f0 + j + 1)
                        dve.wait_ge(gate_done, n)
                        nc.vector.tensor_tensor(gate_scaled, tiles_of(banks[0]), inv_both, mul).then_inc(gate_by_rms, 1)
                        used(r3, c)
                        nc.vector.tensor_tensor(up_scaled, tiles_of(banks[1]), inv_both, mul).then_inc(up_by_rms, 1)
                        if j or not isinstance(jr, int):
                            dve.wait_ge(hid_lo, fb + jr + (f0 + j))
                        dve.wait_ge(up_by_rms, n)
                        dve.wait_ge(gate_silu, n)
                        nc.vector.tensor_tensor(hid, up_scaled, gate_act, mul).then_inc(hid_ready, 1)

                    def hid_rest(jr, j, k0=0):
                        dve.wait_ge(hid_hi, fb + jr + (f0 + j + 1))
                        rest(sT_lo[:, k0:k0 + 2, :], hid, sT_hi[:, k0:k0 + 2, :]).then_inc(hid_lo, 1)

                    rest_unit(L3, base + 3)
                    inv_copy(l * 2 + (2 + which))
                    rest_unit(L3, base + 4)
                    hidden(L3, base + 1, 0, 0, A)
                    hid_rest(0, 0)
                    rest_unit(L3, base + 5)
                    hidden(L3, base + 3, 0, 1, B)
                    rest_unit(L3, base + 6)
                    hid_rest(0, 1)
                    rest_unit(L3, base + 7)
                    with dve.Fori(1, FB - 2) as j:
                        rest_unit(L3 + j, base + 5)
                        hidden(L3 + j, base + 3, j, 1, A)
                        rest_unit(L3 + j, base + 6)
                        hid_rest(j, 1)
                        rest_unit(L3 + j, base + 7)
                    rest_unit(L3, base + FFN - 1)
                    hidden(L3, base + FFN - 3, 0, FB - 1, A)
                    hid_rest(0, FB - 1, k0=2)
                    rest_unit(L3, base + FFN)
                    rest_unit(L3, base + FFN + 1)
                    onto_res((0, 4)[which], (L3, base + FFN - 1), 4, lambda t: 0.5)

                dve.wait_ge(cols_ready, l + 1)
                ffn(0, B1_UNITS)

                m0 = B1_UNITS + FFN

                def unit(i):
                    rest_unit(L3, m0 + i)

                turn_rest(turns_before(l, 1), N, colsL[:, L_MIX:L_MIX + KT])
                unit(2)
                unit(3)
                unit(4)
                unit(5)
                dve.wait_ge(rstd, rstd_done(in_layer(l, ST_MIX)))
                used(L3, m0 + 3)
                did(projected(B, lambda t: k_tok[:, t, :], T_MIX), "k")
                unit(6)
                used(L3, m0 + 4)
                for t in range(TOK):
                    last = stt(out=lf[:, 0, t, :], in0=ps[:, 4 + t, 0:HEADS], scalar=rs(T_MIX, t),
                               in1=colsL[:, L_BF:L_BF + HEADS], op0=mul, op1=add)
                did(last, "f")
                wait_own("f")
                did(stt(out=lf[:, 1], in0=lf[:, 0], scalar=-1.0, in1=lf[:, 0], op0=mul, op1=mx), "fabs")
                unit(7)
                wait_act("fln")
                for c in (0, 32):
                    last = stt(out=nlf[:, :, c:c + HEADS], in0=lf[:, 0], scalar=0.0, in1=lf[:, 3], op0=ALU.min, op1=sub,
                               reverse1=True)
                did(last, "logf")
                unit(8)
                wait_pe("Tk")
                did(nc.vector.tensor_copy(kT, two_banks(4)), "kT")
                unit(9)
                wait_act("cT_hi")
                did(nc.vector.tensor_tensor(cT[32:64, :], ps[32:64, 6, 0:S], cT[32:64, :].bitcast(F32), sub), "cT")
                unit(10)

                def masked(hp):
                    return maxima(hp, lambda e: mask)

                wait_pe("S0")
                did(nc.vector.memset(uT[:, :, 0:2], 0.0), "pad")
                did(masked(0), "soft0")
                unit(11)
                wait_act("exp0")
                did(inverse_sums(0), "rinv0")
                wait_pe("PT0")
                did(probs_T(0), "PT0")
                unit(12)
                used(L3, m0 + 10)
                wait_act("zc")
                for t in range(TOK):
                    last = stt(out=u_tok[:, t, :], in0=ps[:, A[t], :], scalar=rs(T_MIX, t), in1=zc_tok[:, t, :],
                               op0=mul, op1=mul)
                did(last, "u")
                wait_own("rinv0")
                wait_pe("S1")
                did(values_out(0), "O0")
                did(masked(1), "soft1")
                unit(13)
                wait_act("exp1")
                did(inverse_sums(1), "rinv1")
                wait_pe("PT1")
                did(probs_T(1), "PT1")
                unit(14)
                wait_own("rinv1")
                wait_pe("S2")
                did(values_out(1), "O1")
                did(masked(2), "soft2")
                turn_rest(turns_before(l, 2), (6, 7, 2, 3), colsL[:, L_MEM:L_MEM + KT])
                unit(15)

                def conv(tap):
                    for c in range(4):
                        w = colsL[:, L_WCONV + 4 * tap + c:L_WCONV + 4 * tap + c + 1]
                        src = uT[:, c, tap:tap + S]
                        if tap == 0:
                            last = nc.vector.tensor_scalar(accT[:, c, :], src, w, None, mul)
                        else:
                            last = stt(out=accT[:, c, :], in0=src, scalar=w, in1=accT[:, c, :], op0=mul, op1=add)
                    return last

                wait_act("exp2")
                did(inverse_sums(2), "rinv2")
                wait_pe("PT2")
                did(probs_T(2), "PT2")
                unit(16)
                wait_act("uT")
                wait_own("pad")
                did(conv(0), "cv0")
                used(L3, m0 + 14)
                did(projected(A, lambda t: K_tok[:, t, 0:512], T_MEM), "K0")
                wait_own("rinv2")
                wait_pe("S3")
                did(values_out(2), "O2")
                did(masked(3), "soft3")
                unit(17)
                wait_own("cv0")
                did(conv(1), "cv1")
                wait_act("exp3")
                did(inverse_sums(3), "rinv3")
                wait_pe("PT3")
                did(probs_T(3), "PT3")
                wait_own("cv1")
                did(conv(2), "cv2")
                wait_own("cv2")
                wait_pe("Tzb")
                did(nc.vector.tensor_tensor(accT[:, :, :], accT[:, :, :], two_banks(6), mul), "y")
                unit(18)
                wait_act("yc_hi")
                wait_own("y")
                for c in range(4):
                    last = rest(sT_lo[:, c, :], accT[:, c, :], sT_hi[:, c, :], colsL[:, L_CONV + c:L_CONV + c + 1])
                did(last, "ycT_lo")
                wait_pe("PV3")
                wait_own("rinv3")
                did(values_out(3), "O3")
                unit(19)
                wait_act("oT_hi")
                for c in range(4):
                    last = rest(sT_lo[:, 4 + c, :], two_banks(4)[:, c, :], sT_hi[:, 4 + c, :],
                                colsL[:, L_ATT + c:L_ATT + c + 1])
                did(last, "oT_lo")
                unit(20)
                used(L3, m0 + 18)
                did(projected(A, lambda t: Vx[:, t, 0:512], T_MEM), "V0")
                wait_pe("TK0")
                did(nc.vector.tensor_copy(kTx[:, 0:4, :], two_banks(6)), "KT0")
                unit(21)
                wait_pe("TK1")
                did(nc.vector.tensor_copy(kTx[:, 4:8, :], two_banks(6)), "KT1")
                unit(22)
                wait_pe("ssq")
                did(nc.vector.tensor_copy(stat[:, T_CONV, 0:2], ps[:, 0, 0:4:2]), "ssq")
                unit(23)
                unit(24)
                dve.wait_ge(rstd, rstd_done(in_layer(l, ST_CONV)))
                used(L3, m0 + 22)
                for half in range(2):
                    for t in range(TOK):
                        r = res[:, t, half * 512:half * 512 + 512]
                        last = stt(out=r, in0=ps[:, 4 + 2 * half + t, :], scalar=rs(T_CONV, t), in1=r, op0=mul, op1=add)
                did(last, "resconv")
                wait_own("resconv")
                unit(25)
                unit(26)
                onto_res(2, (L3, m0 + 24), 0, lambda t: rs(T_ATT, t))

                turn_rest(turns_before(l, 3), N, colsL[:, L_XAT:L_XAT + KT])
                for i in range(27, 31):
                    unit(i)
                used(L3, m0 + 28)
                did(nc.vector.tensor_scalar(xq_tok[:, 1, 512:1024], ps[:, 3, :], rs(T_XAT, 1), None, mul), "xq1")
                wait_pe("TX1")
                did(nc.vector.tensor_scalar(xqT[:, 4:8, :], two_banks(6), XDH ** -0.5, None, mul), "xqT1")
                for h in range(XH):
                    wait_pe(f"SX{h}")
                    did(nc.vector.tensor_reduce(xmax[:, 0, 2 * h:2 * h + 2], ps[:, h, :].rearrange("p (t n) -> p t n", t=2),
                                                AX.X, mx), f"xm{h}")
                    wait_own(f"xm{h}")
                    did(nc.vector.tensor_scalar(xmax[:, 1, 2 * h:2 * h + 2], xmax[:, 0, 2 * h:2 * h + 2], -1.0, None, mul),
                        f"xneg{h}")
                wait_act("xexp3")
                did(nc.vector.reciprocal(rinv[:].rearrange("p (t h) -> p t h", t=2)[:, :, 0:XH],
                                         soft[:, 1, :].rearrange("p (t h) -> p t h", t=2)[:, :, 0:XH]), "rinvx")
                for h in (1, 3):
                    wait_pe(f"PX{h}")
                    did(nc.vector.tensor_copy(PTb[:, h, :], ps[:, 4 + h, :]), f"PX{h}")
                wait_own("rinvx")
                for half in range(2):
                    wait_pe(f"OX{half}")
                    for t in range(TOK):
                        o = xq_tok[:, t, half * 512:half * 512 + 512].rearrange("p (e d) -> p e d", e=2)
                        r = rinv[:, 8 * t + 2 * half:8 * t + 2 * half + 2].unsqueeze(2).to_broadcast([P, 2, XDH])
                        last = nc.vector.tensor_tensor(o, ps[:, 2 * half + t, :].rearrange("p (e d) -> p e d", e=2), r, mul)
                    did(last, f"xo{half}")
                turn_rest(turns_before(l, 4), N, None)
                for i in range(31, 35):
                    unit(i)
                onto_res(3, (L3, m0 + 32), 0, lambda t: 1.0)

                ffn(1, B1_UNITS + FFN + MID)
            l_dve.closed()
            dve.wait_ge(rstd, rstd_done(ST_LAYER + LAYERS * NST))
            dve.wait_ge(gfin_in, 32)
            for t in range(TOK):
                stt(out=out_tok[:, t, :], in0=res[:, t, :], scalar=rs(T_XAT, t), in1=gfin[:], op0=mul,
                    op1=mul).then_inc(fin_ready, 1)

        @block.gpsimd
        def _(pool):
            nc.gpsimd.memset(ones[:], 1.0).then_inc(set_ready, 1)
            nc.gpsimd.memset(nlf[:], 0.0).then_inc(set_ready, 1)
            for i, value in enumerate((1.0 / D, 2.0 / D, EPS, -0.5)):
                nc.gpsimd.memset(consts2[:, i, :], value).then_inc(set_ready, 1)
            pool.wait_ge(set_ready, 6)

            def statistic(i, tile, width):
                total, mean, inv = (stat[:, tile, 2 * i_:2 * i_ + 2] for i_ in range(3))
                nc.gpsimd.tensor_tensor(mean, total, consts2[:, 0 if width == D else 1, :], ALU.mult).then_inc(rstd, 1)
                pool.wait_ge(rstd, rstd_done(i) - 2)
                nc.gpsimd.tensor_tensor(mean, mean, consts2[:, 2, :], ALU.add).then_inc(rstd, 1)
                pool.wait_ge(rstd, rstd_done(i) - 1)
                nc.gpsimd.tensor_tensor(inv, mean, consts2[:, 3, :], ALU.pow).then_inc(rstd, 1)

            pool.wait_ge(sums, 2)
            statistic(ST_X, T_FFN, D)
            pool.wait_ge(sums, 4)
            statistic(ST_MEM, T_MEM, D)
            pool.wait_ge(cst_in, 16)
            for hp in range(PAIRS):
                if hp == 1:
                    pool.wait_ge(b_pe.sem, b_pe.upto("pool_mean"))
                if hp >= 2:
                    pool.wait_ge(b_dve.sem, b_dve.upto(f"soft{hp - 2}"))
                for e in range(2):
                    slope = 2.0 ** (-8.0 * (2 * hp + e + 1) / HEADS)
                    last = nc.gpsimd.tensor_scalar(alibi[hp % 2][:, e * TRI:(e + 1) * TRI], negdist, slope, None, ALU.mult)
                last.then_inc(alibi_ready, 1)
            for i, n_sums, tile in ((ST_WOUT, 8, T_MIX), (ST_NORM1, 10, T_FFN), (ST_MLP, 14, T_MIX)):
                pool.wait_ge(sums, n_sums)
                if i != ST_NORM1:
                    nc.gpsimd.tensor_tensor(stat[:, T_MIX, 0:2], part[:, 0:2], part[:, 2:4], ALU.add).then_inc(part_sum, 1)
                    pool.wait_ge(part_sum, 1 if i == ST_WOUT else 2)
                statistic(i, tile, D)
            pool.wait_ge(cols_in, 16)
            with pool.Fori(0, LAYERS) as l:
                pool.wait_ge(turn_lo, turns_before(l, 0))
                nc.gpsimd.tensor_copy(colsL[:], colsA[:, bass.ds(l * L_COLS + C_B1, L_COLS)]).then_inc(cols_ready, 1)
                for i, (tile, n_sum, width) in enumerate((
                        (T_FFN, 0, D), (T_MIX, 1, D), (T_ATT, 2, 512), (T_CONV, None, 512), (T_XAT, 3, D), (T_FFN, 4, D))):
                    if n_sum is None:
                        pool.wait_ge(l_dve.sem, l_dve.upto("ssq", l))
                    else:
                        pool.wait_ge(sums, sums_of(l, n_sum))
                    statistic(in_layer(l, i), tile, width)
            pool.wait_ge(sums, sums_of(LAYERS, 0))
            statistic(ST_LAYER + LAYERS * NST, T_XAT, D)


def _wide(w):
    return w.reshape(2, 4, P, 512).transpose(0, 2, 1, 3).reshape(2, P, UNIT)


def _tall(w):
    n = w.shape[0] // (2 * P)
    return w.reshape(n, 2, P, D).transpose(0, 2, 1, 3).reshape(n, P, UNIT)


def _columns(v):
    return v.reshape(-1, P).T


def _stream(a):
    w = a["w_in"][0]
    units = [_wide(w[:, 512 * i:512 * i + 512]) for i in range(8)]
    units += [_tall(a["w_branch_pool"][0]), _tall(a["w_branch_attn"][0]), _tall(a["w_out"][0])]
    up = lambda j: _wide(a["w_up"][0][:, 512 * j:512 * j + 512])
    down = lambda j: _tall(a["w_down"][0][512 * j:512 * j + 512])
    units.append(up(0))
    for j in range(1, B1_FB):
        units += [up(j), down(j - 1)]
    units.append(down(B1_FB - 1))
    for l in range(LAYERS):
        def ffn(gu, dn):
            f = FB * 256
            g = lambda j: _wide(np.concatenate([gu[:, 256 * j:256 * j + 256], gu[:, f + 256 * j:f + 256 * j + 256]], 1))
            d = lambda j: _tall(dn[256 * j:256 * j + 256])
            out = [g(0)]
            for j in range(1, FB):
                out += [g(j), d(j - 1)]
            return out + [d(FB - 1)]
        units += ffn(a["w_ffn1_gu_2"][l], a["w_ffn1_down_2"][l])
        w = a["w_mix_in_2"][l]
        block = lambda i: _wide(w[:, 512 * i:512 * i + 512])
        forget = np.zeros((1, P, UNIT), np.float32)
        forget[0, :, 0:KT * HEADS] = w[:, 3072:].reshape(KT, P, HEADS).transpose(1, 0, 2).reshape(P, KT * HEADS)
        units += [block(3), block(4), forget, block(5), block(1), block(2), block(0)]
        units += [_wide(a["w_xkv_2"][l][:, 512 * i:512 * i + 512]) for i in range(4)]
        units += [_tall(a["w_mix_out_2"][l])]
        units += [_wide(a["w_xq_2"][l][:, 512 * i:512 * i + 512]) for i in range(2)]
        units += [_tall(a["w_xo_2"][l])]
        units += ffn(a["w_ffn2_gu_2"][l], a["w_ffn2_down_2"][l])
    s = np.concatenate(units, 0)
    assert s.shape == (TOTAL, P, UNIT), s.shape
    return s


def _constants():
    q = np.arange(S)
    ok = q[None, :] <= q[:, None]
    dist = np.where(ok, (q[None, :] - q[:, None]).astype(np.float32), np.float32(NEG))
    mask = np.where(ok, np.float32(0), np.float32(NEG))

    def tri(m):
        return np.concatenate([m[0:P, 0:P], m[P:S, :]], 1)

    upto = ok.T[0:P, :].astype(np.float32)
    cst = np.concatenate([np.eye(P, dtype=np.float32), tri(dist), tri(mask), upto], 1)
    mats = []
    for w in POOL_WINDOWS:
        count = np.minimum(q + 1, w).astype(np.float32)
        m = np.where(ok & (q[:, None] - q[None, :] < w), np.float32(1) / count[:, None], np.float32(0))
        m = (m - np.eye(S, dtype=np.float32)).T
        mats.append(np.concatenate([m[0:P, :], m[P:S, P:S]], 1))
    sel = np.zeros((P, HEADS, P), np.float32)
    for h in range(HEADS):
        sel[h, h, :] = sel[32 + h, h, :] = 1
    return cst, sel, np.concatenate(mats, 1).astype(np.float32)


def kernel(**a):
    import concourse.bacc as bacc
    from concourse.bass_utils import run_bass_kernel_spmd

    cst, sel, poolmat = _constants()
    a = {k: np.asarray(v) for k, v in a.items()}
    group = [_columns(a["norm_mix_pre"][0]), _columns(a["norm_mlp_pre"][0]), _columns(a["pool_scale"][0])]
    for l in range(LAYERS):
        group += [_columns(a[n][l]) for n in ("g_ffn1_2", "g_mix_2", "g_mem_2", "g_xattn_2", "g_ffn2_2",
                                              "g_conv_out_2", "g_att_out_2")]
        group += [_columns(a["w_conv_2"][l].reshape(-1)), np.broadcast_to(a["b_f_2"][l], (P, HEADS))]
    rows = lambda v: np.broadcast_to(v.reshape(1, -1), (P, v.size))
    arrays = {
        "x": a["x"].reshape(TOK, P, D).transpose(1, 0, 2),
        "mem": a["mem_2"].reshape(TOK, P, D).transpose(1, 0, 2),
        "stream": _stream(a),
        "cols": np.concatenate(group, 1),
        "consts": cst,
        "sel": sel,
        "poolmat": poolmat,
        "poolw": a["pool_w"][0].transpose(1, 0, 2),
        "gate_bias": rows(a["b_gate"][0]),
        "post_gain": rows(np.concatenate([a["norm_mix_post"][0], a["norm_mlp_post"][0]])),
        "final_gain": rows(a["g_final_2"]),
    }
    arrays = {f"{k}_in": np.ascontiguousarray(v) for k, v in arrays.items()}
    nc = bacc.Bacc("TRN2", target_bir_lowering=False, num_devices=1)
    aps = [nc.dram_tensor(k, v.shape, F32, kind="ExternalInput").ap() for k, v in arrays.items()]
    out = nc.dram_tensor("out", (TOK, P, D), F32, kind="ExternalOutput").ap()
    program(nc, *aps, out)
    r = run_bass_kernel_spmd(nc, [arrays], core_ids=[0])
    return r.results[0]["out"].reshape(1, S, D)
```

```python
from contextlib import ExitStack

import numpy as np

import concourse.bass as bass
from concourse import mybir

F32 = mybir.dt.float32
F32R = mybir.dt.float32r
ALU = mybir.AluOpType
ACT = mybir.ActivationFunctionType
AX = mybir.AxisListType

P = 128
D = 1024
S = 256
TOK = S // P
KT = D // P
BT = KT // 2
HEADS, DH = 8, 64
PAIRS = HEADS // 2
XH, XDH = 4, 256
POOL_WINDOWS = (2, 4, 8, 16)
LAYERS = 2
EPS = 1e-6
NEG = -1e30
BIG = 3e38

F_COLS = KT * 2 * HEADS
WARM_X, WARM_FIRST, WARM_NORM = 3, 3, 7
UNIT = 2048
RING = 3
TRI = 3 * P

B1_IN, B1_BRANCH, B1_OUT = 16, 4, 8 // 2
B1_FB = 8
B1_MLP = 4 * B1_FB
B1_UNITS = B1_IN + B1_BRANCH + B1_OUT + B1_MLP
FB = 11
FFN = 3 * FB
MID = 33
LAYER = 2 * FFN + MID
TOTAL = B1_UNITS + LAYERS * LAYER
AHEAD = TOTAL + 2
assert LAYER % RING == 0 and MID % RING == 0 and FFN % RING == 0

C_MIXPRE, C_MLPPRE, C_PSCALE, C_B1 = 0, 8, 16, 20
L_FFN1, L_MIX, L_MEM, L_XAT, L_FFN2, L_CONV, L_ATT, L_WCONV, L_BF, L_COLS = 0, 8, 16, 24, 32, 40, 44, 48, 60, 68

B1_PE = ["pool_mean", "pool_mix", "S0", "PT0", "PV0", "S1", "PT1", "PV1", "S2", "PT2",
         "PV2", "S3", "PT3", "PV3", "To"]
B1_ACT = ["p", "ypT_hi", "v", "exp0", "exp1", "exp2", "exp3",
          "sig0", "sig1", "sig2", "sig3", "oT_hi"]
B1_DVE = ["yT", "qT", "ypT_lo", "kT", "soft0", "gate0", "rinv0", "PT0", "O0", "soft1", "gate1", "rinv1", "PT1",
          "O1", "soft2", "gate2", "rinv2", "PT2", "O2", "soft3", "gate3", "rinv3", "PT3", "O3", "oT_lo",
          "m1", "m2q0", "m2q1", "mh0", "m2q2", "m2q3", "mh1", "postmix", "postmlp"]
L_PE = ["cT", "S0", "PT0", "PV0", "S1", "PT1", "PV1", "S2", "PT2", "PV2", "S3", "PT3", "PV3", "To", "ssq",
        "XQ2", "SX0", "SX1", "SX2", "SX3", "PX0", "PX1", "PX2", "PX3", "OX0", "OX1"]
L_ACT = ["fexp", "fln", "v", "cT_hi", "zc", "exp0", "exp1", "zb", "exp2", "exp3", "yc_hi", "ysq",
         "oT_hi", "V1", "xqT0", "xexp0", "xexp1", "xexp2", "xexp3", "PX0", "PX2"]
L_DVE = ["inv_sq", "qT", "kT", "f_lo", "f", "fabs", "logf", "cT", "pad", "soft0", "rinv0", "PT0", "zcs", "u", "O0", "soft1",
         "rinv1", "PT1", "O1", "soft2", "rinv2", "PT2", "cv0", "KT0", "O2", "soft3", "zbs", "cv1", "rinv3", "PT3",
         "cv2", "y", "ycT_lo", "O3", "KT1", "oT_lo", "ysum", "V0", "ssq", "resconv", "xqT1", "xqT2",
         "xm0", "xneg0", "xm1", "xneg1", "xm2", "xneg2", "xm3", "xneg3", "rinvx", "PX1", "PX3", "xo0", "xo1"]

class Steps:

    def __init__(self, sem, names):
        self.sem, self.names, self.at = sem, names, 0
        assert len(set(names)) == len(names), names

    def upto(self, name, layer=0):
        return layer * len(self.names) + self.names.index(name) + 1

    def one(self, name):
        assert self.names[self.at] == name, (self.names[self.at], name)
        self.at += 1
        return 1

    def closed(self):
        assert self.at == len(self.names), self.names[self.at:]


def program(nc, x, mem, stream, cols, consts, sel, poolmat, poolw, gate_bias, post_gain, final_gain, out):
    with ExitStack() as ctx:
        def sb(name, shape, dt=F32):
            return ctx.enter_context(nc.sbuf_tensor(name, shape, dt))

        def sem(name):
            return ctx.enter_context(nc.semaphore(name))

        def tiles2(ap):
            return ap.rearrange("p (k n) -> p k n", k=2)

        res = sb("res", [P, TOK, D])
        xT_hi, xT_lo = sb("xT_hi", [P, KT, S], F32R), sb("xT_lo", [P, KT, S], F32R)
        raw = sb("raw", [P, RING, UNIT])
        w_hi, w_lo = sb("w_hi", [P, RING, UNIT], F32R), sb("w_lo", [P, RING, UNIT], F32R)
        sT_hi, sT_lo = sb("sT_hi", [P, 8, S], F32R), sb("sT_lo", [P, 8, S], F32R)
        cst = sb("cst", [P, P + TRI + TRI + S])
        ident = cst[:, 0:P]
        negdist = cst[:, P:P + TRI]
        mask = cst[:, P + TRI:P + 2 * TRI]
        upto = cst[:, P + 2 * TRI:P + 2 * TRI + S]
        sel_r = sb("sel_r", [P, HEADS, P], F32R)
        ones = sb("ones", [P, 2])
        consts2 = sb("consts2", [P, 4, 2])
        colsA = sb("colsA", [P, C_B1 + LAYERS * L_COLS])
        colsL = sb("colsL", [P, L_COLS])
        gfin = sb("gfin", [P, D])
        scratch = sb("scratch", [P, D])
        stat = sb("stat", [P, 6, 6])
        soft = sb("soft", [P, 2, 16])
        inv_row = sb("inv_row", [P, S])
        inv_sq, inv_mem = sb("inv_sq", [P, S]), sb("inv_mem", [P, S])
        part = sb("part", [P, 4])
        xmax = sb("xmax", [P, 2, 8])
        rinv = sb("rinv", [P, 16])
        lf = sb("lf", [P, 5, TOK, HEADS])
        nlf = sb("nlf", [P, TOK, P])
        cT = sb("cT", [P, S], F32R)

        qk_tok = sb("qk_tok", [P, 2, TOK, 512])
        v_tok = sb("v_tok", [P, TOK, 512])
        qkT = sb("qkT", [P, 2, 4, S])
        Pb = sb("Pb", [P, 4, 512])
        PTb = sb("PTb", [P, 4, 512])
        cu = sb("cu", [P, 2, TOK, 512])
        zb_tok = sb("zb_tok", [P, TOK, 512])
        uT = sb("uT", [P, 4, 2 + S])
        accT = sb("accT", [P, 4, S])
        kTx = sb("kTx", [P, KT, S])
        Vx = sb("Vx", [P, TOK, D])

        q_tok, k_tok = qk_tok[:, 0], qk_tok[:, 1]
        qT, kT = qkT[:, 0], qkT[:, 1]
        zcT = cu[:, 0].rearrange("p t n -> p (t n)").rearrange("p (c n) -> p c n", c=4)
        ysum = zcT[:, 0, :]
        zbT = zb_tok[:, :, :].rearrange("p t n -> p (t n)").rearrange("p (c n) -> p c n", c=4)
        xq_tok = qk_tok[:, :, :, :].rearrange("p a t n -> p (a t n)").rearrange("p (t n) -> p t n", t=TOK)
        xqT = qkT[:, :, :, :].rearrange("p a k n -> p (a k) n")
        mem_tok = kTx[:, :, :].rearrange("p k n -> p (k n)").rearrange("p (t n) -> p t n", t=TOK)
        o_tok, ysq = q_tok, k_tok.rearrange("p t n -> p (t n)").rearrange("p (c n) -> p c n", c=4)
        gate_scaled, gate_act, up_scaled, hid = (tiles2(Pb[:, i, :]) for i in range(4))
        gates = [None] * 4
        gates[0] = kTx[:, 0:4, :].rearrange("p k n -> p (k n)").rearrange("p (t n) -> p t n", t=TOK)
        gates[1] = kTx[:, 4:8, :].rearrange("p k n -> p (k n)").rearrange("p (t n) -> p t n", t=TOK)
        gates[2] = Vx[:, 0, :].rearrange("p (t n) -> p t n", t=TOK)
        gates[3] = Vx[:, 1, :].rearrange("p (t n) -> p t n", t=TOK)
        gbias = cu[:, :, :, :].rearrange("p a t n -> p (a t n)")
        p_tok = PTb[:, 0:2, :]
        yT = PTb[:, 2:4, :].rearrange("p a n -> p (a n)").rearrange("p (c n) -> p c n", c=4)
        pmat = zb_tok[:, :, :].rearrange("p t n -> p (t n)")
        pmat2 = uT[:, :, :].rearrange("p c n -> p (c n)")
        pw = Pb[:, 0, :].rearrange("p (g n) -> p g n", g=4)
        alibi = [accT[:, :, :].rearrange("p c n -> p (c n)"), pmat]
        m_tok = Pb[:, :, :].rearrange("p a n -> p (a n)").rearrange("p (t n) -> p t n", t=TOK)
        gpost = qk_tok[:, :, :, :].rearrange("p a t n -> p (a t n)")
        relu = Pb[:, 0:2, :]
        sq = Pb[:, 2:4, :].rearrange("p a (k n) -> p (a k) n", k=2)
        sel_in = Vx[:, 0, :].rearrange("p (h n) -> p h n", h=HEADS)
        out_tok = Vx

        ps = ctx.enter_context(nc.psum_tensor("ps", [P, 8, 512], F32))

        unit_landed = [sem(f"unit_landed{s}") for s in range(RING)]
        unit_hi, unit_lo, unit_used = sem("unit_hi"), sem("unit_lo"), sem("unit_used")
        x_in = [sem("x_in0"), sem("x_in1")]
        ident_in, cst_in, cols_in, pool_in, gbias_in, mem_in, gpost_in, gfin_in, out_sem = (
            sem(n) for n in ("ident_in", "cst_in", "cols_in", "pool_in", "gbias_in", "mem_in", "gpost_in", "gfin_in", "out_sem"))
        sel_in_sbuf = sem("sel_in_sbuf")
        table_ready = sem("table_ready")
        set_ready = sem("set_ready")
        fin_gain = sem("fin_gain")
        fin_ready = [sem("fin_ready0"), sem("fin_ready1")]
        first_hi, first_lo = sem("first_hi"), sem("first_lo")
        quarter_ready = sem("quarter_ready")
        res_ready = sem("res_ready")
        turn_T = sem("turn_T")
        turn_hi, turn_lo = sem("turn_hi"), sem("turn_lo")
        sums = sem("sums")
        rstd = sem("rstd")
        sel_ready = sem("sel_ready")
        part_sum = sem("part_sum")
        cols_ready = sem("cols_ready")
        gate_done, gate_by_rms, gate_silu, up_by_rms, hid_ready, hid_hi, hid_lo = (
            sem(n) for n in ("gate_done", "gate_by_rms", "gate_silu", "up_by_rms", "hid_ready", "hid_hi", "hid_lo"))
        half_done, relu_ready, sq_ready, sq_hi, sq_lo = (
            sem(n) for n in ("half_done", "relu_ready", "sq_ready", "sq_hi", "sq_lo"))
        inv_T, inv_ready = sem("inv_T"), sem("inv_ready")
        alibi_ready = sem("alibi_ready")
        b_pe, b_act, b_dve = Steps(sem("b_pe"), B1_PE), Steps(sem("b_act"), B1_ACT), Steps(sem("b_dve"), B1_DVE)
        l_pe, l_act, l_dve = Steps(sem("l_pe"), L_PE), Steps(sem("l_act"), L_ACT), Steps(sem("l_dve"), L_DVE)

        ST_X, ST_MEM, ST_WOUT, ST_NORM1, ST_MLP, ST_LAYER = range(6)
        ST_FFN1, ST_MIX, ST_ATT, ST_CONV, ST_XAT, ST_FFN2, NST = range(7)
        T_FFN, T_MEM, T_MIX, T_CONV, T_ATT, T_XAT = range(6)
        SQ_TILE = (0, 0, 4)
        PER_LAYER_RES, PER_LAYER_TURN, PER_LAYER_QUARTERS, PER_LAYER_SUMS = 16, 6 * BT, 15, 10

        def rstd_done(i):
            return 3 * i + 3

        def in_layer(l, i):
            return l * NST + (ST_LAYER + i)

        def rs(tile, t):
            return stat[:, tile, 4 + t:5 + t]

        def res_of(l, i):
            return l * PER_LAYER_RES + (8 + 4 * i + 4)

        def turns_before(l, i):
            return l * PER_LAYER_TURN + (3 + i) * BT

        def quarter_of(l, i, q):
            return l * PER_LAYER_QUARTERS + (12 + 3 * i + q + 1)

        def sums_of(l, i):
            return l * PER_LAYER_SUMS + (14 + 2 * i + 2)

        def tiles_of(bank):
            return ps[:, bank, :].rearrange("p (k n) -> p k n", k=2)

        def two_banks(b):
            return ps[:, b:b + 2, :].rearrange("p b (k n) -> p (b k) n", k=2)

        block = ctx.enter_context(nc.Block())

        def slot(c):
            return c % RING

        def landed(r3, c):
            return r3 * 16 + (c // RING + 1) * 16

        def upto_unit(r3, c):
            return r3 * RING + c + 1

        @block.sync
        def _(sp):
            def load(r3, c):
                if not (isinstance(r3, int) and 3 * r3 + c < RING):
                    sp.wait_ge(unit_lo, upto_unit(r3, c - RING))
                if isinstance(r3, int):
                    src = stream[(3 * r3 + c) % TOTAL]
                else:
                    src = stream[bass.ds(r3 * RING + c, 1)].rearrange("a p n -> p (a n)")
                sp.dma_start(raw[:, slot(c), :], src).then_inc(unit_landed[slot(c)], 16)

            for half in range(2):
                cs = slice(half * 512, half * 512 + 512)
                sp.dma_start(res[:, :, cs], x[:, :, cs]).then_inc(x_in[half], 16)
            for c in range(RING):
                load(0, c)
            sp.dma_start(pmat[:, 0:2 * TRI], poolmat[:, 0:2 * TRI]).then_inc(pool_in, 16)
            load(0, RING)
            sp.dma_start(pmat2[:, 0:2 * TRI], poolmat[:, 2 * TRI:4 * TRI]).then_inc(pool_in, 16)
            sp.dma_start(pw, poolw).then_inc(pool_in, 16)
            sp.dma_start(cst[:, P:], consts[:, P:]).then_inc(cst_in, 16)
            sp.dma_start(mem_tok, mem).then_inc(mem_in, 16)
            load(0, RING + 1)
            sp.dma_start(sel_in, sel).then_inc(sel_in_sbuf, 16)
            load(0, RING + 2)
            sp.dma_start(gbias, gate_bias).then_inc(gbias_in, 16)
            sp.dma_start(gfin[:], final_gain).then_inc(gfin_in, 16)
            whole = (TOTAL - RING) // RING
            with sp.Fori(1, whole) as r:
                for s in range(RING):
                    load(r, RING + s)
            for c in range(RING + whole * RING, AHEAD):
                load(0, c)
            for t in range(TOK):
                sp.wait_ge(fin_ready[t], 1)
                sp.dma_start(out[t], out_tok[:, t, :]).then_inc(out_sem, 16)
            sp.wait_ge(out_sem, 16 * TOK)
            for s in range(RING):
                sp.wait_ge(unit_landed[s], 16 * len(range(s, AHEAD, RING)))

        @block.tensor
        def _(pe):
            def mm(bank_ap, lh, rh, start, stop):
                return nc.tensor.matmul(bank_ap, lh, rh, start=start, stop=stop)

            def warm(n):
                for _ in range(n):
                    mm(ps[:, 0, 0:S], nlf[:, 0, :], nlf[:, :, :].rearrange("p t n -> p (t n)"), True, True)

            def wide(r3, c, part, banks, tiles=None, first=False):
                if not first:
                    pe.wait_ge(unit_lo, upto_unit(r3, c))
                wh = w_hi[:, slot(c), :].rearrange("p (k n) -> p k n", k=4)
                wl = w_lo[:, slot(c), :].rearrange("p (k n) -> p k n", k=4)
                if first:
                    def one_pass(k, x_, w):
                        for t in range(TOK):
                            last = mm(ps[:, banks[t], :], x_[:, k, t * P:(t + 1) * P], w[:, k, :], w is wh and k == 0
                                      and x_ is xT_hi, False)
                        return last

                    for k in range(4):
                        if k < 3:
                            pe.wait_ge(first_hi, k + 1)
                        else:
                            pe.wait_ge(unit_hi, 1)
                        one_pass(k, xT_hi, wh)
                    for k in range(4):
                        pe.wait_ge(turn_lo, k // 2 + 1)
                        one_pass(k, xT_lo, wh)
                    for k in range(4):
                        if k < 3:
                            pe.wait_ge(first_lo, k + 1)
                        else:
                            pe.wait_ge(unit_lo, 1)
                        last = one_pass(k, xT_hi, wl)
                    last.then_inc(unit_used, 1)
                    return
                for k in range(4):
                    kk = 4 * part + k
                    if tiles is not None and kk % 2 == 0:
                        pe.wait_ge(turn_lo, tiles + kk // 2 + 1)
                    for t in range(TOK):
                        hi, lo = xT_hi[:, kk, t * P:(t + 1) * P], xT_lo[:, kk, t * P:(t + 1) * P]
                        mm(ps[:, banks[t], :], hi, wh[:, k, :], kk == 0, False)
                        mm(ps[:, banks[t], :], hi, wl[:, k, :], False, False)
                        last = mm(ps[:, banks[t], :], lo, wh[:, k, :], False, kk == 7)
                last.then_inc(unit_used, 1)

            def tall(r3, c, k0, base, start, stop, hi, lo, tiles=None, between=None):
                pe.wait_ge(unit_lo, upto_unit(r3, c))
                wh = w_hi[:, slot(c), :].rearrange("p (k h n) -> p k h n", k=2, h=2)
                wl = w_lo[:, slot(c), :].rearrange("p (k h n) -> p k h n", k=2, h=2)

                def xs(k, t):
                    return hi[:, k0 + k, t * P:(t + 1) * P], lo[:, k0 + k, t * P:(t + 1) * P]

                if tiles is not None:
                    pe.wait_ge(turn_lo, tiles + k0 // 2 + 1)
                if stop:
                    for half in range(2):
                        for t in range(TOK):
                            if between is not None and (half, t) == (1, 0):
                                between()
                            o = ps[:, base + 2 * half + t, :]
                            for k in range(2):
                                xh, xl = xs(k, t)
                                mm(o, xh, wh[:, k, half, :], start and k == 0, False)
                                mm(o, xh, wl[:, k, half, :], False, False)
                                last = mm(o, xl, wh[:, k, half, :], False, k == 1)
                            if (half, t) != (1, 1):
                                last.then_inc(quarter_ready, 1)
                    last.then_inc(unit_used, 1)
                    return
                for k in range(2):
                    if k == 1 and between is not None:
                        between()
                    for t in range(TOK):
                        xh, xl = xs(k, t)
                        for half in range(2):
                            mm(ps[:, base + 2 * half + t, :], xh, wh[:, k, half, :], start and k == 0, False)
                        for half in range(2):
                            mm(ps[:, base + 2 * half + t, :], xh, wl[:, k, half, :], False, False)
                        for half in range(2):
                            last = mm(ps[:, base + 2 * half + t, :], xl, wh[:, k, half, :], False, False)
                last.then_inc(unit_used, 1)

            def flipped(r3, c, part, banks, tiles=None, half_sem=None):
                pe.wait_ge(unit_lo, upto_unit(r3, c))
                wh = w_hi[:, slot(c), :].rearrange("p (k n) -> p k n", k=4)
                wl = w_lo[:, slot(c), :].rearrange("p (k n) -> p k n", k=4)

                def tile(f):
                    return slice(f * P, (f + 1) * P)

                def out(f):
                    return ps[:, banks[f // 2], (f % 2) * S:(f % 2) * S + S]

                def hi_passes(k, f):
                    kk = 4 * part + k
                    mm(out(f), wh[:, k, tile(f)], xT_hi[:, kk, :], kk == 0 and f % 2 == 0, False)
                    return mm(out(f), wl[:, k, tile(f)], xT_hi[:, kk, :], False, kk == KT - 1 and f % 2 == 1)

                def one(k, f):
                    kk = 4 * part + k
                    if kk == 0:
                        hi_passes(k, f)
                        return mm(out(f), wh[:, k, tile(f)], xT_lo[:, kk, :], False, False)
                    mm(out(f), wh[:, k, tile(f)], xT_lo[:, kk, :], False, False)
                    return hi_passes(k, f)

                if part == 0:
                    for k in range(4):
                        if tiles is None:
                            for f in range(4):
                                last = one(k, f)
                        elif k % 2 == 0:
                            pe.wait_ge(turn_hi, tiles + k // 2 + 1)
                            for k_ in (k, k + 1):
                                for f in range(4):
                                    hi_passes(k_, f)
                            pe.wait_ge(turn_lo, tiles + k // 2 + 1)
                            for k_ in (k, k + 1):
                                for f in range(4):
                                    last = mm(out(f), wh[:, k_, tile(f)], xT_lo[:, k_, :], False, False)
                else:
                    if tiles is not None:
                        pe.wait_ge(turn_lo, tiles + BT)
                    for f in range(4):
                        for k in range(4):
                            last = one(k, f)
                        if f == 1 and half_sem is not None:
                            last.then_inc(half_sem, 1)
                last.then_inc(unit_used, 1)

            def inv_turn(stat_i, tile=T_FFN, bank=4):
                pe.wait_ge(rstd, rstd_done(stat_i))
                for t in range(TOK):
                    last = nc.tensor.transpose(ps[:, bank, t * P:(t + 1) * P],
                                               rs(tile, t).to_broadcast([P, P]), ident)
                last.then_inc(inv_T, 1)

            def turn(src, banks, wait=None):
                for k in range(KT):
                    if wait is not None:
                        wait(k)
                    for t in range(TOK):
                        last = nc.tensor.transpose(ps[:, banks[k // 2], (k % 2) * S + t * P:(k % 2) * S + (t + 1) * P],
                                                   src[:, t, k * P:(k + 1) * P], ident)
                    if k % 2 == 1:
                        last.then_inc(turn_T, 1)

            def turn_half(src, banks, k0):
                for k in range(4):
                    for t in range(TOK):
                        last = nc.tensor.transpose(ps[:, banks[k // 2], (k % 2) * S + t * P:(k % 2) * S + (t + 1) * P],
                                                   src[:, t, (k0 + k) * P:(k0 + k + 1) * P], ident)
                return last

            def scores(hp, forget):
                for e in range(2):
                    rows = slice(e * DH, e * DH + DH)
                    for t, (o0, nk) in enumerate(((0, P), (P, S))):
                        o = ps[:, 4 + e, o0:o0 + nk]
                        last = mm(o, qT[rows, hp, t * P:(t + 1) * P], kT[rows, hp, 0:nk], True, not forget)
                        if forget:
                            last = mm(o, sel_r[:, 2 * hp + e, :], cT[:, 0:nk], False, True)
                return last

            def prob_turn(hp):
                for e in range(2):
                    for b in range(3):
                        last = nc.tensor.transpose(ps[:, 4 + e, b * P:(b + 1) * P],
                                                   Pb[:, 2 * (hp % 2) + e, b * P:(b + 1) * P], ident)
                return last

            def values(hp):
                for e in range(2):
                    h = 2 * hp + e
                    pt = PTb[:, 2 * (hp % 2) + e, :]
                    c0 = TRI + e * DH
                    mm(ps[:, 4, c0:c0 + DH], pt[:, 0:P], v_tok[:, 0, h * DH:(h + 1) * DH], True, True)
                    mm(ps[:, 5, c0:c0 + DH], pt[:, P:2 * P], v_tok[:, 0, h * DH:(h + 1) * DH], True, False)
                    last = mm(ps[:, 5, c0:c0 + DH], pt[:, 2 * P:3 * P], v_tok[:, 1, h * DH:(h + 1) * DH], False, True)
                return last

            A, B, N = (0, 1), (2, 3), (4, 5, 6, 7)
            BB = lambda n: b_dve.upto(n)

            pe.wait_ge(set_ready, 2)
            warm(WARM_X)
            pe.wait_ge(ident_in, 16)
            turn(res, N, wait=lambda k: pe.wait_ge(x_in[k // 4], 16))
            warm(WARM_FIRST)
            wide(0, 0, 0, A, tiles=0, first=True)
            wide(0, 1, 1, A, tiles=0)
            inv_turn(ST_X)
            flipped(0, 2, 0, B)
            pe.wait_ge(b_act.sem, b_act.upto("p"))
            pe.wait_ge(pool_in, 48)
            for g in range(4):
                o = ps[:, 6 + g // 2, (g % 2) * S:(g % 2) * S + S]
                pm = pmat if g < 2 else pmat2
                o0 = (g % 2) * TRI
                mm(o, p_tok[:, 0, g * P:(g + 1) * P], pm[:, o0:o0 + S], True, False)
                last = mm(o[:, P:S], p_tok[:, 1, g * P:(g + 1) * P], pm[:, o0 + S:o0 + TRI], False, True)
            last.then_inc(b_pe.sem, b_pe.one("pool_mean"))
            flipped(0, 3, 1, B)
            flipped(0, 4, 0, A)
            pe.wait_ge(b_dve.sem, BB("yT"))
            for g in range(4):
                last = mm(ps[:, 4 + g // 2, (g % 2) * S:(g % 2) * S + S], pw[:, g, :], yT[:, g, :], True, True)
            last.then_inc(b_pe.sem, b_pe.one("pool_mix"))
            flipped(0, 5, 1, A)
            pe.wait_ge(b_dve.sem, BB("qT"))
            wide(0, 6, 0, B)
            wide(0, 7, 1, B)
            for i in range(8):
                hp = i // 2
                if i == 2:
                    pe.wait_ge(b_act.sem, b_act.upto("v"))
                if i == 0:
                    pe.wait_ge(b_dve.sem, BB("kT"))
                if i in (4, 6):
                    pe.wait_ge(b_dve.sem, BB(f"gate{hp - 2}"))
                wide(0, 8 + i, i % 2, (A, B)[hp % 2])
                if i % 2 == 0:
                    if hp:
                        pe.wait_ge(b_dve.sem, BB(f"PT{hp - 1}"))
                        values(hp - 1).then_inc(b_pe.sem, b_pe.one(f"PV{hp - 1}"))
                    scores(hp, False).then_inc(b_pe.sem, b_pe.one(f"S{hp}"))
                else:
                    pe.wait_ge(b_act.sem, b_act.upto(f"exp{hp}"))
                    prob_turn(hp).then_inc(b_pe.sem, b_pe.one(f"PT{hp}"))
            pe.wait_ge(b_dve.sem, BB("gate3"))

            def values3():
                pe.wait_ge(b_dve.sem, BB("PT3"))
                values(3).then_inc(b_pe.sem, b_pe.one("PV3"))

            tall(0, 16, 0, 0, True, False, sT_hi, sT_lo, between=values3)
            pe.wait_ge(b_dve.sem, BB("O3"))
            turn_half(o_tok, (6, 7), 0).then_inc(b_pe.sem, b_pe.one("To"))
            tall(0, 17, 2, 0, False, True, sT_hi, sT_lo)
            pe.wait_ge(b_dve.sem, BB("oT_lo"))
            tall(0, 18, 4, 4, True, False, sT_hi, sT_lo)
            tall(0, 19, 6, 4, False, True, sT_hi, sT_lo)
            turn(m_tok, (0, 1, 2, 3), wait=lambda k: pe.wait_ge(b_dve.sem, BB("mh0" if k < 4 else "mh1")))
            for i in range(4):
                tall(0, 20 + i, 2 * i, 4, i == 0, i == 3, xT_hi, xT_lo, tiles=BT)

            warm(WARM_NORM)
            turn(res, N, wait=lambda k: pe.wait_ge(res_ready, 2 if k < 4 else 4))

            def up(r3, c, jr, j, banks, tiles=None):
                if j >= 2:
                    pe.wait_ge(relu_ready, 2 * (jr + j))
                flipped(r3, c, 0, banks, tiles)
                flipped(r3, c + 1, 1, banks, tiles, half_done)

            def down1(r3, c, jr, j, tile, start=False, stop=False):
                pe.wait_ge(sq_lo, jr + j + 1)
                tall(r3, c, tile, 4, start, False, sT_hi, sT_lo)
                tall(r3, c + 1, tile + 2, 4, False, stop, sT_hi, sT_lo)

            c0 = B1_UNITS - B1_MLP
            up(0, c0, 0, 0, A, tiles=2 * BT)
            inv_turn(ST_NORM1)
            inv_turn(ST_MEM, T_MEM, 5)
            up(0, c0 + 2, 0, 1, B)
            down1(0, c0 + 4, 0, 0, 0, start=True)
            with pe.Fori(0, 2) as r:
                for b in range(3):
                    c = c0 + 6 + 4 * b
                    up(r * 4, c, r * 3, b + 2, A)
                    down1(r * 4, c + 2, r * 3, b + 1, SQ_TILE[(b + 2) % 3])
            down1(0, c0 + 30, 0, 7, SQ_TILE[2], stop=True)
            warm(WARM_NORM)

            with pe.Fori(0, LAYERS) as l:
                def ffn(which, base):
                    L3 = l * (LAYER // 3)
                    fb = l * (2 * FB)
                    f0 = which * FB
                    before = res_of(l, -1 if which == 0 else 2)
                    turn(res, N, wait=lambda k: pe.wait_ge(res_ready, before - 2 if k < 4 else before))
                    tl = turns_before(l, 0 if which == 0 else 5)

                    def gate_up(r3, c, jr, j, banks, tiles=None):
                        if j >= 2 or not isinstance(jr, int):
                            pe.wait_ge(up_by_rms, fb + jr + (f0 + j))
                        flipped(r3, c, 0, banks, tiles)
                        flipped(r3, c + 1, 1, banks, tiles, gate_done)

                    def down(r3, c, jr, j, start=False, stop=False, k0=0):
                        pe.wait_ge(hid_lo, fb + jr + (f0 + j + 1))
                        tall(r3, c, k0, 4, start, stop, sT_hi, sT_lo)

                    gate_up(L3, base, 0, 0, A, tiles=tl)
                    inv_turn(in_layer(l, (ST_FFN1, ST_FFN2)[which]))
                    gate_up(L3, base + 2, 0, 1, B)
                    down(L3, base + 4, 0, 0, start=True)
                    with pe.Fori(1, FB - 2) as j:
                        gate_up(L3 + j, base + 2, j, 1, A)
                        down(L3 + j, base + 4, j, 0)
                    gate_up(L3, base + FFN - 4, 0, FB - 1, A)
                    down(L3, base + FFN - 2, 0, FB - 2)
                    down(L3, base + FFN - 1, 0, FB - 1, stop=True, k0=2)

                def wait_act(n):
                    pe.wait_ge(l_act.sem, l_act.upto(n, l))

                def wait_dve(n):
                    pe.wait_ge(l_dve.sem, l_dve.upto(n, l))

                ffn(0, B1_UNITS)

                L3 = l * (LAYER // 3)
                m0 = B1_UNITS + FFN
                turn(res, N, wait=lambda k: pe.wait_ge(res_ready, res_of(l, 0) - (2 if k < 4 else 0)))
                tl = turns_before(l, 1)
                flipped(L3, m0, 0, A, tiles=tl)
                flipped(L3, m0 + 1, 1, A, tiles=tl)
                inv_turn(in_layer(l, ST_MIX), T_MIX, 6)
                flipped(L3, m0 + 2, 0, B)
                flipped(L3, m0 + 3, 1, B)
                pe.wait_ge(unit_lo, upto_unit(L3, m0 + 4))
                fw = w_hi[:, slot(m0 + 4), 0:F_COLS].rearrange("p (k n) -> p k n", k=KT)
                for k in range(KT):
                    for t in range(TOK):

                        def hi_pass(o=ps[:, 4 + t, 0:2 * HEADS], x_=xT_hi[:, k, t * P:(t + 1) * P]):
                            return mm(o, x_, fw[:, k, :], k == 0, k == KT - 1)

                        if k < KT - 1:
                            hi_pass()
                        last = mm(ps[:, 4 + t, 0:HEADS], xT_lo[:, k, t * P:(t + 1) * P], fw[:, k, 0:HEADS], False, False)
                        if k == KT - 1:
                            last = hi_pass()
                last.then_inc(unit_used, 1)
                wait_dve("qT")
                wide(L3, m0 + 5, 0, A)
                wide(L3, m0 + 6, 1, A)
                wait_dve("kT")
                flipped(L3, m0 + 7, 0, B)
                wait_dve("logf")
                mm(ps[:, 6, 0:S], nlf[:, 0, :], upto, True, False)
                mm(ps[:, 6, P:S], nlf[:, 1, :], upto[:, 0:P], False, True).then_inc(l_pe.sem, l_pe.one("cT"))
                flipped(L3, m0 + 8, 1, B)
                wait_dve("cT")
                scores(0, True).then_inc(l_pe.sem, l_pe.one("S0"))
                wait_act("v")
                flipped(L3, m0 + 9, 0, A)
                wait_act("exp0")
                prob_turn(0).then_inc(l_pe.sem, l_pe.one("PT0"))
                flipped(L3, m0 + 10, 1, A)
                wait_dve("PT0")
                values(0).then_inc(l_pe.sem, l_pe.one("PV0"))
                scores(1, True).then_inc(l_pe.sem, l_pe.one("S1"))
                wait_act("zc")
                flipped(L3, m0 + 11, 0, B)
                wait_act("exp1")
                prob_turn(1).then_inc(l_pe.sem, l_pe.one("PT1"))
                flipped(L3, m0 + 12, 1, B)
                wait_dve("PT1")
                values(1).then_inc(l_pe.sem, l_pe.one("PV1"))
                scores(2, True).then_inc(l_pe.sem, l_pe.one("S2"))
                pe.wait_ge(mem_in, l * 16 + 32)

                def mem_wait(k):
                    if k == 4:
                        wait_act("zb")
                turn(mem_tok, (6, 7, 2, 3), wait=mem_wait)
                tl = turns_before(l, 2)
                wait_dve("u")
                flipped(L3, m0 + 13, 0, A, tiles=tl)
                wait_act("exp2")
                prob_turn(2).then_inc(l_pe.sem, l_pe.one("PT2"))
                flipped(L3, m0 + 14, 1, A, tiles=tl)
                wait_dve("PT2")
                values(2).then_inc(l_pe.sem, l_pe.one("PV2"))
                scores(3, True).then_inc(l_pe.sem, l_pe.one("S3"))
                flipped(L3, m0 + 15, 0, B)
                wait_act("exp3")
                prob_turn(3).then_inc(l_pe.sem, l_pe.one("PT3"))
                flipped(L3, m0 + 16, 1, B)
                wait_dve("PT3")
                values(3).then_inc(l_pe.sem, l_pe.one("PV3"))
                wait_dve("KT0")
                wide(L3, m0 + 17, 0, A)
                wait_dve("O3")
                turn_half(o_tok, (4, 5), 0).then_inc(l_pe.sem, l_pe.one("To"))
                wide(L3, m0 + 18, 1, A)
                wait_dve("KT1")
                wide(L3, m0 + 19, 0, B)
                wide(L3, m0 + 20, 1, B)
                wait_dve("V0")
                for t in range(TOK):
                    last = mm(ps[:, 0, 2 * t:2 * t + 2], ysum[:, t * P:(t + 1) * P], ones[:, 0:2], True, True)
                last.then_inc(l_pe.sem, l_pe.one("ssq"))
                wait_dve("ycT_lo")
                wait_dve("oT_lo")
                tall(L3, m0 + 21, 0, 4, True, False, sT_hi, sT_lo)
                tall(L3, m0 + 22, 2, 4, False, True, sT_hi, sT_lo)
                wait_dve("ssq")
                wait_act("V1")
                tall(L3, m0 + 23, 4, 0, True, False, sT_hi, sT_lo)
                tall(L3, m0 + 24, 6, 0, False, True, sT_hi, sT_lo)

                turn(res, N, wait=lambda k: pe.wait_ge(res_ready, res_of(l, 1) - (2 if k < 4 else 0)))
                tl = turns_before(l, 3)
                flipped(L3, m0 + 25, 0, A, tiles=tl)
                flipped(L3, m0 + 26, 1, A, tiles=tl)
                flipped(L3, m0 + 27, 0, B)
                l_pe.one("XQ2")
                flipped(L3, m0 + 28, 1, B, half_sem=l_pe.sem)
                for h in range(XH):
                    if h == 0:
                        wait_act("xqT0")
                    elif h > 1:
                        wait_dve(f"xqT{h - 1}")
                    for t in range(TOK):
                        for k in range(2):
                            last = mm(ps[:, h, t * S:(t + 1) * S], xqT[:, 2 * h + k, t * P:(t + 1) * P],
                                      kTx[:, 2 * h + k, :], k == 0, k == 1)
                    last.then_inc(l_pe.sem, l_pe.one(f"SX{h}"))
                for h in range(XH):
                    wait_act(f"xexp{h}")
                    for m in range(2):
                        for t in range(TOK):
                            last = nc.tensor.transpose(ps[:, 4 + h, m * S + t * P:m * S + (t + 1) * P],
                                                       Pb[:, h, t * S + m * P:t * S + (m + 1) * P], ident)
                    last.then_inc(l_pe.sem, l_pe.one(f"PX{h}"))
                for half in range(2):
                    for e in range(2):
                        h = 2 * half + e
                        if h % 2 == 0:
                            wait_act(f"PX{h}")
                        else:
                            wait_dve(f"PX{h}")
                        for t in range(TOK):
                            for m in range(2):
                                last = mm(ps[:, 2 * half + t, e * XDH:(e + 1) * XDH],
                                          PTb[:, h, m * S + t * P:m * S + (t + 1) * P],
                                          Vx[:, m, h * XDH:(h + 1) * XDH], m == 0, m == 1)
                    last.then_inc(l_pe.sem, l_pe.one(f"OX{half}"))

                def o_wait(k):
                    if k % 4 == 0:
                        wait_dve(f"xo{k // 4}")
                turn(xq_tok, N, wait=o_wait)
                tl = turns_before(l, 4)
                for i in range(4):
                    tall(L3, m0 + 29 + i, 2 * i, 0, i == 0, i == 3, xT_hi, xT_lo, tiles=tl)

                ffn(1, B1_UNITS + FFN + MID)
            b_pe.closed()
            l_pe.closed()

        @block.scalar
        def _(act):
            copy, square, exp = ACT.Copy, ACT.Square, ACT.Exp

            def round_unit(r3, c, width=UNIT):
                act.wait_ge(unit_landed[slot(c)], landed(r3, c))
                if not (isinstance(r3, int) and c < RING):
                    act.wait_ge(unit_used, upto_unit(r3, c - RING))
                nc.scalar.activation(w_hi[:, slot(c), 0:width], raw[:, slot(c), 0:width], copy).then_inc(unit_hi, 1)

            def turn_round(before, banks, gain):
                for b in range(BT):
                    act.wait_ge(turn_T, before + b + 1)
                    if gain is None:
                        last = nc.scalar.activation(xT_hi[:, 2 * b:2 * b + 2, :], tiles_of(banks[b]), copy)
                    else:
                        for k in (2 * b, 2 * b + 1):
                            last = nc.scalar.activation(xT_hi[:, k, :], tiles_of(banks[b])[:, k % 2, :], copy,
                                                        scale=gain[:, k:k + 1])
                    last.then_inc(turn_hi, 1)

            def squares(src, tile, before):
                for t in range(TOK):
                    if t or not isinstance(before, int) or before:
                        act.wait_ge(sums, before + t)
                    ap = src(t)
                    out_ = scratch[:, 0:ap.free_size()]
                    if len(ap.shape) == 3:
                        out_ = out_.rearrange("p (a n) -> p a n", a=ap.shape[1])
                    nc.scalar.activation(out_, ap, square, accum_out=stat[:, tile, t:t + 1]).then_inc(sums, 1)

            def product_squares(i, last_unit, before):
                for q in range(4):
                    if q < 3:
                        act.wait_ge(quarter_ready, 3 * i + q + 1)
                    else:
                        act.wait_ge(unit_used, upto_unit(*last_unit))
                    act.wait_ge(sums, before + q)
                    nc.scalar.activation(scratch[:, 0:512], ps[:, 4 + q, :], square,
                                         accum_out=part[:, q:q + 1]).then_inc(sums, 1)

            def probs(hp):
                for e in range(2):
                    h = 2 * hp + e
                    for t, (o0, nk) in enumerate(((0, P), (P, S))):
                        pr = Pb[:, 2 * (hp % 2) + e, o0:o0 + nk]
                        last = nc.scalar.activation(pr, pr, exp, scale=-1.0, bias=soft[:, 0, 8 * t + h:8 * t + h + 1],
                                                    accum_out=soft[:, 1, 8 * t + h:8 * t + h + 1])
                return last

            A, B, N = (0, 1), (2, 3), (4, 5, 6, 7)
            res_t = lambda t: res[:, t, :]

            def used(r3, c):
                act.wait_ge(unit_used, upto_unit(r3, c))

            def projected(banks, dst, tile):
                for t in range(TOK):
                    last = nc.scalar.activation(dst(t), ps[:, banks[t], :], copy, scale=rs(tile, t))
                return last

            act.dma_start(cst[:, 0:P], consts[:, 0:P]).then_inc(ident_in, 16)
            act.dma_start(colsA[:], cols).then_inc(cols_in, 16)
            def wait_pe1(n):
                act.wait_ge(b_pe.sem, b_pe.upto(n))

            def wait_dve1(n):
                act.wait_ge(b_dve.sem, b_dve.upto(n))

            def did1(ins, n):
                ins.then_inc(b_act.sem, b_act.one(n))

            act.wait_ge(set_ready, 1)
            nc.scalar.activation(scratch[:, 0:2], ones[:], copy).then_inc(table_ready, 1)
            act.wait_ge(cols_in, 16)
            turn_round(0, N, colsA[:, C_MIXPRE:C_MIXPRE + KT])
            act.wait_ge(unit_landed[0], 16)
            for k in range(4):
                nc.scalar.activation(w_hi[:, 0, k * 512:(k + 1) * 512], raw[:, 0, k * 512:(k + 1) * 512],
                                     copy).then_inc(first_hi if k < 3 else unit_hi, 1)
            round_unit(0, 1)
            act.wait_ge(table_ready, 1)
            squares(res_t, T_FFN, 0)
            round_unit(0, 2)
            round_unit(0, 3)
            used(0, 1)
            act.wait_ge(rstd, rstd_done(ST_X))
            did1(projected(A, lambda t: p_tok[:, t, :], T_FFN), "p")
            round_unit(0, 4)
            round_unit(0, 5)
            round_unit(0, 6)
            act.wait_ge(mem_in, 16)
            squares(lambda t: mem_tok[:, t, :], T_MEM, 2)
            act.wait_ge(sel_in_sbuf, 16)
            nc.scalar.activation(sel_r[:], sel_in, copy).then_inc(sel_ready, 1)
            wait_pe1("pool_mix")
            for g in range(4):
                last = nc.scalar.activation(sT_hi[:, g, :], ps[:, 4 + g // 2, (g % 2) * S:(g % 2) * S + S], copy,
                                            scale=colsA[:, C_PSCALE + g:C_PSCALE + g + 1])
            did1(last, "ypT_hi")
            round_unit(0, 7)
            round_unit(0, 8)
            round_unit(0, 9)
            used(0, 7)
            did1(projected(B, lambda t: v_tok[:, t, :], T_FFN), "v")
            round_unit(0, 10)
            for hp in range(PAIRS):
                round_unit(0, 11 + 2 * hp)
                wait_dve1(f"soft{hp}")
                did1(probs(hp), f"exp{hp}")
                round_unit(0, 12 + 2 * hp)
            for i in range(4):
                wait_dve1(f"gate{i}")
                did1(nc.scalar.activation(gates[i], gates[i], ACT.Sigmoid), f"sig{i}")
            wait_pe1("To")
            did1(nc.scalar.activation(sT_hi[:, 4:8, :], ps[:, 6:8, :].rearrange("p b (k n) -> p (b k) n", k=2), copy), "oT_hi")
            act.dma_start(gpost, post_gain).then_inc(gpost_in, 16)
            round_unit(0, 19)
            round_unit(0, 20)
            round_unit(0, 21)
            turn_round(BT, (0, 1, 2, 3), None)
            round_unit(0, 22)
            round_unit(0, 23)
            round_unit(0, 24)
            round_unit(0, 25)
            product_squares(2, (0, 23), 4)
            turn_round(2 * BT, N, colsA[:, C_MLPPRE:C_MLPPRE + KT])
            c0 = B1_UNITS - B1_MLP
            round_unit(0, c0 + 2)
            squares(res_t, T_FFN, 8)

            def sq_round(jr, j, tile):
                act.wait_ge(sq_ready, jr + j + 1)
                nc.scalar.activation(sT_hi[:, tile:tile + 4, :], sq, copy).then_inc(sq_hi, 1)

            round_unit(0, c0 + 3)
            round_unit(0, c0 + 4)
            sq_round(0, 0, 0)
            round_unit(0, c0 + 5)
            round_unit(0, c0 + 6)
            round_unit(0, c0 + 7)
            sq_round(0, 1, 4)
            round_unit(0, c0 + 8)
            with act.Fori(0, 2) as r:
                for b in range(3):
                    c = c0 + 6 + 4 * b
                    round_unit(r * 4, c + 3)
                    round_unit(r * 4, c + 4)
                    if b != 1:
                        sq_round(r * 3, b + 2, SQ_TILE[b])
                    round_unit(r * 4, c + 5)
                    if b == 1:
                        used(r * 4, c + 3)
                        sq_round(r * 3, b + 2, SQ_TILE[b])
                    round_unit(r * 4, c + 6)
            round_unit(0, c0 + 33)
            product_squares(3, (0, c0 + 31), 10)
            b_act.closed()

            with act.Fori(0, LAYERS) as l:
                L3 = l * (LAYER // 3)

                def wait_pe(n):
                    act.wait_ge(l_pe.sem, l_pe.upto(n, l))

                def wait_dve(n):
                    act.wait_ge(l_dve.sem, l_dve.upto(n, l))

                def did(ins, n):
                    ins.then_inc(l_act.sem, l_act.one(n))

                def ffn(which, base):
                    fb = l * (2 * FB)
                    f0 = which * FB
                    if which == 0:
                        act.wait_ge(cols_ready, l + 1)
                    g = colsL[:, (L_FFN1, L_FFN2)[which]:][:, 0:KT]
                    turn_round(turns_before(l, 0 if which == 0 else 5), N, g)
                    round_unit(L3, base + 2)
                    squares(res_t, T_FFN, sums_of(l, (0, 4)[which]) - 2)

                    def gate(jr, j):
                        act.wait_ge(gate_by_rms, fb + jr + (f0 + j + 1))
                        nc.scalar.activation(gate_act, gate_scaled, ACT.Silu).then_inc(gate_silu, 1)

                    def hid_round(jr, j, k0=0):
                        act.wait_ge(hid_ready, fb + jr + (f0 + j + 1))
                        nc.scalar.activation(sT_hi[:, k0:k0 + 2, :], hid, copy).then_inc(hid_hi, 1)

                    round_unit(L3, base + 3)
                    round_unit(L3, base + 4)
                    gate(0, 0)
                    hid_round(0, 0)
                    round_unit(L3, base + 5)
                    gate(0, 1)
                    round_unit(L3, base + 6)
                    used(L3, base + 4)
                    hid_round(0, 1)
                    round_unit(L3, base + 7)
                    with act.Fori(1, FB - 2) as j:
                        round_unit(L3 + j, base + 5)
                        gate(j, 1)
                        round_unit(L3 + j, base + 6)
                        used(L3 + j, base + 4)
                        hid_round(j, 1)
                        round_unit(L3 + j, base + 7)
                    round_unit(L3, base + FFN - 1)
                    gate(0, FB - 1)
                    hid_round(0, FB - 1, k0=2)
                    round_unit(L3, base + FFN)
                    round_unit(L3, base + FFN + 1)

                act.wait_ge(b_dve.sem, b_dve.upto("postmlp"))
                act.dma_start(mem_tok, mem).then_inc(mem_in, 16)
                ffn(0, B1_UNITS)

                m0 = B1_UNITS + FFN

                def unit(i):
                    round_unit(L3, m0 + i)

                turn_round(turns_before(l, 1), N, colsL[:, L_MIX:L_MIX + KT])
                unit(2)
                squares(res_t, T_MIX, sums_of(l, 1) - 2)
                unit(3)
                round_unit(L3, m0 + 4, F_COLS)
                unit(5)
                unit(6)
                unit(7)
                wait_dve("fabs")
                did(nc.scalar.activation(lf[:, 2], lf[:, 1], exp, scale=-1.0), "fexp")
                act.wait_ge(l_act.sem, l_act.upto("fexp", l))
                did(nc.scalar.activation(lf[:, 3], lf[:, 2], ACT.Ln, bias=1.0), "fln")
                unit(8)
                used(L3, m0 + 6)
                did(projected(A, lambda t: v_tok[:, t, :], T_MIX), "v")
                unit(9)
                wait_pe("cT")
                did(nc.scalar.activation(cT[:], ps[:, 6, 0:S], copy), "cT_hi")
                unit(10)
                used(L3, m0 + 8)
                did(nc.scalar.activation(zcT, two_banks(2), copy), "zc")
                unit(11)
                wait_dve("soft0")
                did(probs(0), "exp0")
                unit(12)
                unit(13)
                wait_dve("soft1")
                did(probs(1), "exp1")
                unit(14)
                used(L3, m0 + 12)
                did(nc.scalar.activation(zbT, two_banks(2), copy), "zb")
                turn_round(turns_before(l, 2), (6, 7, 2, 3), colsL[:, L_MEM:L_MEM + KT])
                wait_dve("soft2")
                did(probs(2), "exp2")
                unit(15)
                unit(16)
                unit(17)
                wait_dve("soft3")
                did(probs(3), "exp3")
                unit(18)
                wait_dve("y")
                for c in range(4):
                    last = nc.scalar.activation(sT_hi[:, c, :], accT[:, c, :], copy, scale=colsL[:, L_CONV + c:L_CONV + c + 1])
                did(last, "yc_hi")
                did(nc.scalar.activation(ysq, accT[:, :, :], square), "ysq")
                unit(19)
                wait_pe("To")
                for c in range(4):
                    last = nc.scalar.activation(sT_hi[:, 4 + c, :], ps[:, 4 + c // 2, (c % 2) * S:(c % 2) * S + S], copy,
                                                scale=colsL[:, L_ATT + c:L_ATT + c + 1])
                did(last, "oT_hi")
                squares(lambda t: o_tok[:, t, :], T_ATT, sums_of(l, 2) - 2)
                unit(20)
                unit(21)
                unit(22)
                used(L3, m0 + 20)
                did(projected(B, lambda t: Vx[:, t, 512:1024], T_MEM), "V1")
                for i in range(23, 27):
                    unit(i)

                turn_round(turns_before(l, 3), N, colsL[:, L_XAT:L_XAT + KT])
                unit(27)
                squares(res_t, T_XAT, sums_of(l, 3) - 2)
                unit(28)
                used(L3, m0 + 26)
                did(nc.scalar.activation(xqT[:, 0:4, :], two_banks(0), copy, scale=XDH ** -0.5), "xqT0")
                unit(29)
                unit(30)
                act.wait_ge(rstd, rstd_done(in_layer(l, ST_XAT)))
                for h in range(XH):
                    wait_dve(f"xneg{h}")
                    for t in range(TOK):
                        last = nc.scalar.activation(Pb[:, h, t * S:(t + 1) * S], ps[:, h, t * S:(t + 1) * S], exp,
                                                    scale=rs(T_XAT, t), bias=xmax[:, 1, 2 * h + t:2 * h + t + 1],
                                                    accum_out=soft[:, 1, 8 * t + h:8 * t + h + 1])
                    did(last, f"xexp{h}")
                for h in (0, 2):
                    wait_pe(f"PX{h}")
                    did(nc.scalar.activation(PTb[:, h, :], ps[:, 4 + h, :], copy), f"PX{h}")
                turn_round(turns_before(l, 4), N, None)
                for i in range(31, 35):
                    unit(i)

                ffn(1, B1_UNITS + FFN + MID)
            l_act.closed()
            for t in range(TOK):
                act.wait_ge(res_ready, res_of(LAYERS, -1) - 1 + t)
                act.wait_ge(sums, sums_of(LAYERS, 0) - 2 + t)
                nc.scalar.activation(scratch[:], res[:, t, :], square, accum_out=stat[:, T_XAT, t:t + 1]).then_inc(sums, 1)
            act.wait_ge(fin_gain, 1)
            act.wait_ge(rstd, rstd_done(ST_LAYER + LAYERS * NST))
            nc.scalar.activation(out_tok[:, 0, :], out_tok[:, 0, :], copy, scale=rs(T_XAT, 0)).then_inc(fin_ready[0], 1)

        @block.vector
        def _(dve):
            sub, mul, add, mx = ALU.subtract, ALU.mult, ALU.add, ALU.max
            stt = nc.vector.scalar_tensor_tensor

            def rest_unit(r3, c):
                dve.wait_ge(unit_hi, upto_unit(r3, c))
                nc.vector.tensor_tensor(w_lo[:, slot(c), :], raw[:, slot(c), :], w_hi[:, slot(c), :].bitcast(F32),
                                        sub).then_inc(unit_lo, 1)

            def rest(dst, src, hi, gain=None):
                if gain is None:
                    return nc.vector.tensor_tensor(dst, src, hi.bitcast(F32), sub)
                return stt(out=dst, in0=src, scalar=gain, in1=hi.bitcast(F32), op0=mul, op1=sub)

            def turn_rest(before, banks, gain):
                for b in range(BT):
                    dve.wait_ge(turn_hi, before + b + 1)
                    if gain is None:
                        last = rest(xT_lo[:, 2 * b:2 * b + 2, :], tiles_of(banks[b]), xT_hi[:, 2 * b:2 * b + 2, :])
                    else:
                        for k in (2 * b, 2 * b + 1):
                            last = rest(xT_lo[:, k, :], tiles_of(banks[b])[:, k % 2, :], xT_hi[:, k, :], gain[:, k:k + 1])
                    last.then_inc(turn_lo, 1)

            def used(r3, c):
                dve.wait_ge(unit_used, upto_unit(r3, c))

            def projected(banks, dst, tile):
                for t in range(TOK):
                    last = nc.vector.tensor_scalar(dst(t), ps[:, banks[t], :], rs(tile, t), None, mul)
                return last

            def maxima(hp, bias):
                for e in range(2):
                    h = 2 * hp + e
                    for t, (o0, nk) in enumerate(((0, P), (P, S))):
                        last = nc.vector.tensor_tensor_reduce(
                            out=Pb[:, 2 * (hp % 2) + e, o0:o0 + nk], in0=ps[:, 4 + e, o0:o0 + nk],
                            in1=bias(e)[:, o0:o0 + nk], scale=-1.0, scalar=BIG, op0=add, op1=ALU.min,
                            accum_out=soft[:, 0, 8 * t + h:8 * t + h + 1])
                return last

            def pair(ap, hp):
                return ap.rearrange("p (t h) -> p t h", t=2)[:, :, 2 * hp:2 * hp + 2]

            def inverse_sums(hp):
                return nc.vector.reciprocal(pair(rinv[:], hp), pair(soft[:, 1, :], hp))

            def probs_T(hp):
                a = 2 * (hp % 2)
                return nc.vector.tensor_copy(PTb[:, a:a + 2, 0:TRI], ps[:, 4:6, 0:TRI])

            def values_out(hp):
                for t in range(TOK):
                    o = o_tok[:, t, hp * P:(hp + 1) * P].rearrange("p (e d) -> p e d", e=2)
                    r = rinv[:, 8 * t + 2 * hp:8 * t + 2 * hp + 2].unsqueeze(2).to_broadcast([P, 2, DH])
                    last = nc.vector.tensor_tensor(o, ps[:, 4 + t, TRI:512].rearrange("p (e d) -> p e d", e=2), r, mul)
                return last

            A, B, N = (0, 1), (2, 3), (4, 5, 6, 7)

            def wait_pe1(n):
                dve.wait_ge(b_pe.sem, b_pe.upto(n))

            def wait_act1(n):
                dve.wait_ge(b_act.sem, b_act.upto(n))

            def wait_own1(n):
                dve.wait_ge(b_dve.sem, b_dve.upto(n))

            def did1(ins, n):
                ins.then_inc(b_dve.sem, b_dve.one(n))

            def inv_copy(n, bank=4):
                dve.wait_ge(inv_T, n)
                nc.vector.tensor_copy(inv_row[:], ps[:, bank, 0:S]).then_inc(inv_ready, 1)
                dve.wait_ge(inv_ready, n)

            def over(row, n):
                return row[:, :].unsqueeze(1).to_broadcast([P, n, S])

            inv_both = over(inv_row, 2)

            turn_rest(0, N, colsA[:, C_MIXPRE:C_MIXPRE + KT])
            for k in range(4):
                if k < 3:
                    dve.wait_ge(first_hi, k + 1)
                else:
                    dve.wait_ge(unit_hi, 1)
                cs = slice(k * 512, (k + 1) * 512)
                nc.vector.tensor_tensor(w_lo[:, 0, cs], raw[:, 0, cs], w_hi[:, 0, cs].bitcast(F32),
                                        sub).then_inc(first_lo if k < 3 else unit_lo, 1)
            for c in range(1, 4):
                rest_unit(0, c)
            inv_copy(1)
            rest_unit(0, 4)
            rest_unit(0, 5)
            wait_pe1("pool_mean")
            did1(nc.vector.tensor_copy(yT, two_banks(6)), "yT")
            used(0, 3)
            did1(stt(out=qT, in0=two_banks(2), scalar=DH ** -0.5, in1=over(inv_row, 4), op0=mul, op1=mul), "qT")
            rest_unit(0, 6)
            wait_act1("ypT_hi")
            for g in range(4):
                last = rest(sT_lo[:, g, :], two_banks(4)[:, g, :], sT_hi[:, g, :], colsA[:, C_PSCALE + g:C_PSCALE + g + 1])
            did1(last, "ypT_lo")
            rest_unit(0, 7)
            used(0, 5)
            did1(nc.vector.tensor_tensor(kT, two_banks(0), over(inv_row, 4), mul), "kT")
            rest_unit(0, 8)
            rest_unit(0, 9)
            rest_unit(0, 10)
            dve.wait_ge(gbias_in, 16)
            for hp in range(PAIRS):
                wait_pe1(f"S{hp}")
                if hp:
                    did1(values_out(hp - 1), f"O{hp - 1}")
                dve.wait_ge(alibi_ready, hp + 1)
                did1(maxima(hp, lambda e: alibi[hp % 2][:, e * TRI:(e + 1) * TRI]), f"soft{hp}")
                rest_unit(0, 11 + 2 * hp)
                used(0, 9 + 2 * hp)
                if hp == 0:
                    dve.wait_ge(sums, 4)
                for t in range(TOK):
                    last = stt(out=gates[hp][:, t, :], in0=ps[:, (A, B)[hp % 2][t], :], scalar=rs(T_FFN, t),
                               in1=gbias[:, hp * 512:(hp + 1) * 512], op0=mul, op1=add)
                did1(last, f"gate{hp}")
                wait_act1(f"exp{hp}")
                did1(inverse_sums(hp), f"rinv{hp}")
                wait_pe1(f"PT{hp}")
                did1(probs_T(hp), f"PT{hp}")
                wait_own1(f"rinv{hp}")
                rest_unit(0, 12 + 2 * hp)
            wait_pe1("PV3")
            did1(values_out(3), "O3")
            wait_act1("oT_hi")
            did1(rest(sT_lo[:, 4:8, :], two_banks(6), sT_hi[:, 4:8, :]), "oT_lo")
            rest_unit(0, 19)
            wait_act1("sig3")
            used(0, 17)
            for half in range(2):
                for t in range(TOK):
                    last = nc.vector.tensor_tensor(m_tok[:, t, half * 512:half * 512 + 512], gates[half][:, t, :],
                                                   ps[:, 2 * half + t, :], mul)
            did1(last, "m1")
            rest_unit(0, 20)
            wait_own1("m1")
            for q in range(4):
                half, t = divmod(q, TOK)
                if q < 3:
                    dve.wait_ge(quarter_ready, 3 + q + 1)
                else:
                    used(0, 19)
                did1(nc.vector.tensor_tensor(PTb[:, q, :], gates[2 + half][:, t, :], ps[:, 4 + q, :], mul), f"m2q{q}")
                wait_own1(f"m2q{q}")
                mq = m_tok[:, t, half * 512:half * 512 + 512]
                last = nc.vector.tensor_tensor(mq, mq, PTb[:, q, :], add)
                if t == 1:
                    did1(last, f"mh{half}")
            turn_rest(BT, (0, 1, 2, 3), None)
            for c in range(21, 25):
                rest_unit(0, c)

            def post_norm(stat_i, gain, name, before):
                dve.wait_ge(gpost_in, 16)
                for q in range(4):
                    half, t = divmod(q, TOK)
                    dve.wait_ge(sums, before + q + 1)
                    last = nc.vector.tensor_tensor(Pb[:, q, :], ps[:, 4 + q, :], gain[:, half * 512:half * 512 + 512], mul)
                did1(last, name)
                dve.wait_ge(rstd, rstd_done(stat_i))
                wait_own1(name)
                for q in range(4):
                    half, t = divmod(q, TOK)
                    r = res[:, t, half * 512:half * 512 + 512]
                    stt(out=r, in0=Pb[:, q, :], scalar=rs(T_MIX, t), in1=r, op0=mul, op1=add).then_inc(res_ready, 1)

            post_norm(ST_WOUT, gpost[:, 0:D], "postmix", 4)
            turn_rest(2 * BT, N, colsA[:, C_MLPPRE:C_MLPPRE + KT])
            c0 = B1_UNITS - B1_MLP
            rest_unit(0, c0 + 1)
            rest_unit(0, c0 + 2)
            rest_unit(0, c0 + 3)

            def squared(r3, c, jr, j, banks):
                if j:
                    dve.wait_ge(sq_lo, jr + j)
                for half in range(2):
                    if half == 0:
                        dve.wait_ge(half_done, jr + j + 1)
                    else:
                        used(r3, c)
                    stt(out=tiles2(relu[:, half, :]), in0=tiles_of(banks[half]), scalar=0.0, in1=inv_both, op0=mx,
                        op1=mul).then_inc(relu_ready, 1)
                dve.wait_ge(relu_ready, 2 * (jr + j + 1))
                r = relu.rearrange("p a (k n) -> p (a k) n", k=2)
                nc.vector.tensor_tensor(sq, r, r, mul).then_inc(sq_ready, 1)

            def sq_rest(jr, j, tile):
                dve.wait_ge(sq_hi, jr + j + 1)
                rest(sT_lo[:, tile:tile + 4, :], sq, sT_hi[:, tile:tile + 4, :]).then_inc(sq_lo, 1)

            inv_copy(2)
            dve.wait_ge(inv_T, 3)
            nc.vector.tensor_copy(inv_mem[:], ps[:, 5, 0:S]).then_inc(inv_ready, 1)
            squared(0, c0 + 1, 0, 0, A)
            rest_unit(0, c0 + 4)
            sq_rest(0, 0, 0)
            rest_unit(0, c0 + 5)
            squared(0, c0 + 3, 0, 1, B)
            rest_unit(0, c0 + 6)
            rest_unit(0, c0 + 7)
            sq_rest(0, 1, 4)
            rest_unit(0, c0 + 8)
            with dve.Fori(0, 2) as r:
                for b in range(3):
                    c = c0 + 6 + 4 * b
                    rest_unit(r * 4, c + 3)
                    squared(r * 4, c + 1, r * 3, b + 2, A)
                    rest_unit(r * 4, c + 4)
                    if b != 1:
                        sq_rest(r * 3, b + 2, SQ_TILE[b])
                    rest_unit(r * 4, c + 5)
                    if b == 1:
                        sq_rest(r * 3, b + 2, SQ_TILE[b])
                    rest_unit(r * 4, c + 6)
            post_norm(ST_MLP, gpost[:, D:2 * D], "postmlp", 10)
            b_dve.closed()

            with dve.Fori(0, LAYERS) as l:
                L3 = l * (LAYER // 3)

                def wait_pe(n):
                    dve.wait_ge(l_pe.sem, l_pe.upto(n, l))

                def wait_act(n):
                    dve.wait_ge(l_act.sem, l_act.upto(n, l))

                def wait_own(n):
                    dve.wait_ge(l_dve.sem, l_dve.upto(n, l))

                def did(ins, n):
                    ins.then_inc(l_dve.sem, l_dve.one(n))

                def onto_res(i, last_unit, base, scale):
                    for q in range(4):
                        half, t = divmod(q, TOK)
                        if q < 3:
                            dve.wait_ge(quarter_ready, quarter_of(l, i, q))
                        else:
                            used(*last_unit)
                        r = res[:, t, half * 512:half * 512 + 512]
                        stt(out=r, in0=ps[:, base + q, :], scalar=scale(t), in1=r, op0=mul, op1=add).then_inc(res_ready, 1)

                def ffn(which, base):
                    fb = l * (2 * FB)
                    f0 = which * FB
                    turn_rest(turns_before(l, 0 if which == 0 else 5), N, colsL[:, (L_FFN1, L_FFN2)[which]:][:, 0:KT])
                    rest_unit(L3, base + 1)
                    rest_unit(L3, base + 2)

                    def hidden(r3, c, jr, j, banks):
                        n = fb + jr + (f0 + j + 1)
                        dve.wait_ge(gate_done, n)
                        nc.vector.tensor_tensor(gate_scaled, tiles_of(banks[0]), inv_both, mul).then_inc(gate_by_rms, 1)
                        used(r3, c)
                        nc.vector.tensor_tensor(up_scaled, tiles_of(banks[1]), inv_both, mul).then_inc(up_by_rms, 1)
                        if j or not isinstance(jr, int):
                            dve.wait_ge(hid_lo, fb + jr + (f0 + j))
                        dve.wait_ge(up_by_rms, n)
                        dve.wait_ge(gate_silu, n)
                        nc.vector.tensor_tensor(hid, up_scaled, gate_act, mul).then_inc(hid_ready, 1)

                    def hid_rest(jr, j, k0=0):
                        dve.wait_ge(hid_hi, fb + jr + (f0 + j + 1))
                        rest(sT_lo[:, k0:k0 + 2, :], hid, sT_hi[:, k0:k0 + 2, :]).then_inc(hid_lo, 1)

                    rest_unit(L3, base + 3)
                    inv_copy(l * 3 + (4, 6)[which])
                    rest_unit(L3, base + 4)
                    hidden(L3, base + 1, 0, 0, A)
                    hid_rest(0, 0)
                    rest_unit(L3, base + 5)
                    hidden(L3, base + 3, 0, 1, B)
                    rest_unit(L3, base + 6)
                    hid_rest(0, 1)
                    rest_unit(L3, base + 7)
                    with dve.Fori(1, FB - 2) as j:
                        rest_unit(L3 + j, base + 5)
                        hidden(L3 + j, base + 3, j, 1, A)
                        rest_unit(L3 + j, base + 6)
                        hid_rest(j, 1)
                        rest_unit(L3 + j, base + 7)
                    rest_unit(L3, base + FFN - 1)
                    hidden(L3, base + FFN - 3, 0, FB - 1, A)
                    hid_rest(0, FB - 1, k0=2)
                    rest_unit(L3, base + FFN)
                    onto_res((0, 4)[which], (L3, base + FFN - 1), 4, lambda t: 0.5)

                dve.wait_ge(cols_ready, l + 1)
                ffn(0, B1_UNITS)

                m0 = B1_UNITS + FFN

                def unit(i):
                    rest_unit(L3, m0 + i)

                turn_rest(turns_before(l, 1), N, colsL[:, L_MIX:L_MIX + KT])
                unit(1)
                unit(2)
                unit(3)
                inv_copy(l * 3 + 5, 6)
                did(nc.vector.tensor_tensor(inv_sq[:], inv_row[:], inv_row[:], mul), "inv_sq")
                used(L3, m0 + 1)
                did(stt(out=qT, in0=two_banks(0), scalar=DH ** -0.5, in1=over(inv_row, 4), op0=mul, op1=mul), "qT")
                dve.wait_ge(unit_hi, upto_unit(L3, m0 + 4))
                fw = w_hi[:, slot(m0 + 4), 0:F_COLS].rearrange("p (k n) -> p k n", k=KT)[:, :, HEADS:]
                fr = raw[:, slot(m0 + 4), 0:F_COLS].rearrange("p (k n) -> p k n", k=KT)[:, :, HEADS:]
                nc.vector.tensor_tensor(fw, fr, fw.bitcast(F32), sub).then_inc(unit_lo, 1)
                unit(5)
                used(L3, m0 + 3)
                did(nc.vector.tensor_tensor(kT, two_banks(2), over(inv_row, 4), mul), "kT")
                unit(6)
                used(L3, m0 + 4)
                for t in range(TOK):
                    last = stt(out=lf[:, 4, t, :], in0=ps[:, 4 + t, HEADS:2 * HEADS], scalar=rs(T_MIX, t),
                               in1=colsL[:, L_BF:L_BF + HEADS], op0=mul, op1=add)
                did(last, "f_lo")
                wait_own("f_lo")
                for t in range(TOK):
                    last = stt(out=lf[:, 0, t, :], in0=ps[:, 4 + t, 0:HEADS], scalar=rs(T_MIX, t), in1=lf[:, 4, t, :],
                               op0=mul, op1=add)
                did(last, "f")
                wait_own("f")
                did(stt(out=lf[:, 1], in0=lf[:, 0], scalar=-1.0, in1=lf[:, 0], op0=mul, op1=mx), "fabs")
                unit(7)
                wait_act("fln")
                for c in (0, 32):
                    last = stt(out=nlf[:, :, c:c + HEADS], in0=lf[:, 0], scalar=0.0, in1=lf[:, 3], op0=ALU.min, op1=sub,
                               reverse1=True)
                did(last, "logf")
                unit(8)
                unit(9)
                wait_act("cT_hi")
                did(nc.vector.tensor_tensor(cT[32:64, :], ps[32:64, 6, 0:S], cT[32:64, :].bitcast(F32), sub), "cT")
                unit(10)

                def masked(hp):
                    return maxima(hp, lambda e: mask)

                wait_pe("S0")
                did(nc.vector.memset(uT[:, :, 0:2], 0.0), "pad")
                did(masked(0), "soft0")
                unit(11)
                wait_act("exp0")
                did(inverse_sums(0), "rinv0")
                wait_pe("PT0")
                did(probs_T(0), "PT0")
                unit(12)
                wait_act("zc")
                wait_own("inv_sq")
                did(nc.vector.tensor_tensor(zcT, zcT, over(inv_sq, 4), mul), "zcs")
                used(L3, m0 + 10)
                wait_own("zcs")
                did(nc.vector.tensor_tensor(uT[:, :, 2:2 + S], two_banks(0), zcT, mul), "u")
                wait_own("rinv0")
                wait_pe("S1")
                did(values_out(0), "O0")
                did(masked(1), "soft1")
                unit(13)
                wait_act("exp1")
                did(inverse_sums(1), "rinv1")
                wait_pe("PT1")
                did(probs_T(1), "PT1")
                unit(14)
                wait_own("rinv1")
                wait_pe("S2")
                did(values_out(1), "O1")
                did(masked(2), "soft2")
                turn_rest(turns_before(l, 2), (6, 7, 2, 3), colsL[:, L_MEM:L_MEM + KT])
                unit(15)

                def conv(tap):
                    for c in range(4):
                        w = colsL[:, L_WCONV + 4 * tap + c:L_WCONV + 4 * tap + c + 1]
                        src = uT[:, c, tap:tap + S]
                        if tap == 0:
                            last = nc.vector.tensor_scalar(accT[:, c, :], src, w, None, mul)
                        else:
                            last = stt(out=accT[:, c, :], in0=src, scalar=w, in1=accT[:, c, :], op0=mul, op1=add)
                    return last

                wait_act("exp2")
                did(inverse_sums(2), "rinv2")
                wait_pe("PT2")
                did(probs_T(2), "PT2")
                unit(16)
                wait_own("u")
                did(conv(0), "cv0")
                used(L3, m0 + 14)
                did(nc.vector.tensor_tensor(kTx[:, 0:4, :], two_banks(0), over(inv_mem, 4), mul), "KT0")
                wait_own("rinv2")
                wait_pe("S3")
                did(values_out(2), "O2")
                did(masked(3), "soft3")
                unit(17)
                wait_act("zb")
                did(nc.vector.tensor_tensor(zbT, zbT, over(inv_row, 4), mul), "zbs")
                wait_own("cv0")
                did(conv(1), "cv1")
                wait_act("exp3")
                did(inverse_sums(3), "rinv3")
                wait_pe("PT3")
                did(probs_T(3), "PT3")
                wait_own("cv1")
                did(conv(2), "cv2")
                wait_own("cv2")
                did(nc.vector.tensor_tensor(accT[:, :, :], accT[:, :, :], zbT, mul), "y")
                unit(18)
                wait_act("yc_hi")
                wait_own("y")
                for c in range(4):
                    last = rest(sT_lo[:, c, :], accT[:, c, :], sT_hi[:, c, :], colsL[:, L_CONV + c:L_CONV + c + 1])
                did(last, "ycT_lo")
                wait_pe("PV3")
                wait_own("rinv3")
                did(values_out(3), "O3")
                used(L3, m0 + 16)
                did(nc.vector.tensor_tensor(kTx[:, 4:8, :], two_banks(2), over(inv_mem, 4), mul), "KT1")
                unit(19)
                wait_act("oT_hi")
                for c in range(4):
                    last = rest(sT_lo[:, 4 + c, :], two_banks(4)[:, c, :], sT_hi[:, 4 + c, :],
                                colsL[:, L_ATT + c:L_ATT + c + 1])
                did(last, "oT_lo")
                wait_act("ysq")
                did(nc.vector.tensor_reduce(ysum, ysq.rearrange("p c n -> p n c"), AX.X, add), "ysum")
                unit(20)
                used(L3, m0 + 18)
                did(projected(A, lambda t: Vx[:, t, 0:512], T_MEM), "V0")
                unit(21)
                unit(22)
                wait_pe("ssq")
                did(nc.vector.tensor_copy(stat[:, T_CONV, 0:2], ps[:, 0, 0:4:2]), "ssq")
                unit(23)
                unit(24)
                dve.wait_ge(rstd, rstd_done(in_layer(l, ST_CONV)))
                used(L3, m0 + 22)
                for half in range(2):
                    for t in range(TOK):
                        r = res[:, t, half * 512:half * 512 + 512]
                        last = stt(out=r, in0=ps[:, 4 + 2 * half + t, :], scalar=rs(T_CONV, t), in1=r, op0=mul, op1=add)
                did(last, "resconv")
                wait_own("resconv")
                unit(25)
                onto_res(2, (L3, m0 + 24), 0, lambda t: rs(T_ATT, t))

                turn_rest(turns_before(l, 3), N, colsL[:, L_XAT:L_XAT + KT])
                for i in range(26, 31):
                    unit(i)
                wait_pe("XQ2")
                did(nc.vector.tensor_scalar(xqT[:, 4:6, :], tiles_of(2), XDH ** -0.5, None, mul), "xqT1")
                used(L3, m0 + 28)
                did(nc.vector.tensor_scalar(xqT[:, 6:8, :], tiles_of(3), XDH ** -0.5, None, mul), "xqT2")
                dve.wait_ge(rstd, rstd_done(in_layer(l, ST_XAT)))
                for h in range(XH):
                    wait_pe(f"SX{h}")
                    did(nc.vector.tensor_reduce(xmax[:, 0, 2 * h:2 * h + 2], ps[:, h, :].rearrange("p (t n) -> p t n", t=2),
                                                AX.X, mx), f"xm{h}")
                    wait_own(f"xm{h}")
                    did(stt(out=xmax[:, 1, 2 * h:2 * h + 2], in0=xmax[:, 0, 2 * h:2 * h + 2], scalar=-1.0,
                            in1=stat[:, T_XAT, 4:6], op0=mul, op1=mul), f"xneg{h}")
                wait_act("xexp3")
                did(nc.vector.reciprocal(rinv[:].rearrange("p (t h) -> p t h", t=2)[:, :, 0:XH],
                                         soft[:, 1, :].rearrange("p (t h) -> p t h", t=2)[:, :, 0:XH]), "rinvx")
                for h in (1, 3):
                    wait_pe(f"PX{h}")
                    did(nc.vector.tensor_copy(PTb[:, h, :], ps[:, 4 + h, :]), f"PX{h}")
                wait_own("rinvx")
                for half in range(2):
                    wait_pe(f"OX{half}")
                    for t in range(TOK):
                        o = xq_tok[:, t, half * 512:half * 512 + 512].rearrange("p (e d) -> p e d", e=2)
                        r = rinv[:, 8 * t + 2 * half:8 * t + 2 * half + 2].unsqueeze(2).to_broadcast([P, 2, XDH])
                        last = nc.vector.tensor_tensor(o, ps[:, 2 * half + t, :].rearrange("p (e d) -> p e d", e=2), r, mul)
                    did(last, f"xo{half}")
                turn_rest(turns_before(l, 4), N, None)
                for i in range(31, 34):
                    unit(i)
                onto_res(3, (L3, m0 + 32), 0, lambda t: 1.0)

                ffn(1, B1_UNITS + FFN + MID)
            l_dve.closed()
            dve.wait_ge(gfin_in, 16)
            for t in range(TOK):
                dve.wait_ge(res_ready, res_of(LAYERS, -1) - 1 + t)
                nc.vector.tensor_tensor(out_tok[:, t, :], res[:, t, :], gfin[:], mul).then_inc(fin_gain, 1)
            dve.wait_ge(fin_gain, 2)
            dve.wait_ge(rstd, rstd_done(ST_LAYER + LAYERS * NST))
            nc.vector.tensor_scalar(out_tok[:, 1, :], out_tok[:, 1, :], rs(T_XAT, 1), None, mul).then_inc(fin_ready[1], 1)

        @block.gpsimd
        def _(pool):
            nc.gpsimd.memset(ones[:], 1.0).then_inc(set_ready, 1)
            nc.gpsimd.memset(nlf[:], 0.0).then_inc(set_ready, 1)
            for i, value in enumerate((1.0 / D, 2.0 / D, EPS, -0.5)):
                nc.gpsimd.memset(consts2[:, i, :], value).then_inc(set_ready, 1)
            pool.wait_ge(set_ready, 6)

            def statistic(i, tile, width):
                total, mean, inv = (stat[:, tile, 2 * i_:2 * i_ + 2] for i_ in range(3))
                nc.gpsimd.tensor_tensor(mean, total, consts2[:, 0 if width == D else 1, :], ALU.mult).then_inc(rstd, 1)
                pool.wait_ge(rstd, rstd_done(i) - 2)
                nc.gpsimd.tensor_tensor(mean, mean, consts2[:, 2, :], ALU.add).then_inc(rstd, 1)
                pool.wait_ge(rstd, rstd_done(i) - 1)
                nc.gpsimd.tensor_tensor(inv, mean, consts2[:, 3, :], ALU.pow).then_inc(rstd, 1)

            pool.wait_ge(sums, 2)
            statistic(ST_X, T_FFN, D)
            pool.wait_ge(sums, 4)
            statistic(ST_MEM, T_MEM, D)
            pool.wait_ge(cst_in, 16)
            for hp in range(PAIRS):
                if hp == 1:
                    pool.wait_ge(b_pe.sem, b_pe.upto("pool_mean"))
                if hp >= 2:
                    pool.wait_ge(b_dve.sem, b_dve.upto(f"soft{hp - 2}"))
                for e in range(2):
                    slope = 2.0 ** (-8.0 * (2 * hp + e + 1) / HEADS)
                    last = nc.gpsimd.tensor_scalar(alibi[hp % 2][:, e * TRI:(e + 1) * TRI], negdist, slope, None, ALU.mult)
                last.then_inc(alibi_ready, 1)
            for i, n_sums, tile in ((ST_WOUT, 8, T_MIX), (ST_NORM1, 10, T_FFN), (ST_MLP, 14, T_MIX)):
                pool.wait_ge(sums, n_sums)
                if i != ST_NORM1:
                    nc.gpsimd.tensor_tensor(stat[:, T_MIX, 0:2], part[:, 0:2], part[:, 2:4], ALU.add).then_inc(part_sum, 1)
                    pool.wait_ge(part_sum, 1 if i == ST_WOUT else 2)
                statistic(i, tile, D)
            pool.wait_ge(cols_in, 16)
            with pool.Fori(0, LAYERS) as l:
                pool.wait_ge(turn_lo, turns_before(l, 0))
                nc.gpsimd.tensor_copy(colsL[:], colsA[:, bass.ds(l * L_COLS + C_B1, L_COLS)]).then_inc(cols_ready, 1)
                for i, (tile, n_sum, width) in enumerate((
                        (T_FFN, 0, D), (T_MIX, 1, D), (T_ATT, 2, 512), (T_CONV, None, 512), (T_XAT, 3, D), (T_FFN, 4, D))):
                    if n_sum is None:
                        pool.wait_ge(l_dve.sem, l_dve.upto("ssq", l))
                    else:
                        pool.wait_ge(sums, sums_of(l, n_sum))
                    statistic(in_layer(l, i), tile, width)
            pool.wait_ge(sums, sums_of(LAYERS, 0))
            statistic(ST_LAYER + LAYERS * NST, T_XAT, D)


def _wide(w):
    return w.reshape(2, 4, P, 512).transpose(0, 2, 1, 3).reshape(2, P, UNIT)


def _tall(w):
    n = w.shape[0] // (2 * P)
    return w.reshape(n, 2, P, D).transpose(0, 2, 1, 3).reshape(n, P, UNIT)


def _columns(v):
    return v.reshape(-1, P).T


def _stream(a):
    w = a["w_in"][0]
    units = [_wide(w[:, 512 * i:512 * i + 512]) for i in range(8)]
    units += [_tall(a["w_branch_pool"][0]), _tall(a["w_branch_attn"][0]), _tall(a["w_out"][0])]
    up = lambda j: _wide(a["w_up"][0][:, 512 * j:512 * j + 512])
    down = lambda j: _tall(a["w_down"][0][512 * j:512 * j + 512])
    units.append(up(0))
    for j in range(1, B1_FB):
        units += [up(j), down(j - 1)]
    units.append(down(B1_FB - 1))
    for l in range(LAYERS):
        def ffn(gu, dn):
            f = FB * 256
            g = lambda j: _wide(np.concatenate([gu[:, 256 * j:256 * j + 256], gu[:, f + 256 * j:f + 256 * j + 256]], 1))
            d = lambda j: _tall(dn[256 * j:256 * j + 256])
            out = [g(0)]
            for j in range(1, FB):
                out += [g(j), d(j - 1)]
            return out + [d(FB - 1)]
        units += ffn(a["w_ffn1_gu_2"][l], a["w_ffn1_down_2"][l])
        w = a["w_mix_in_2"][l]
        block = lambda i: _wide(w[:, 512 * i:512 * i + 512])
        forget = np.zeros((1, P, UNIT), np.float32)
        fw = w[:, 3072:].reshape(KT, P, HEADS).transpose(1, 0, 2)
        forget[0, :, 0:F_COLS] = np.concatenate([fw, fw], 2).reshape(P, F_COLS)
        units += [block(3), block(4), forget, block(5), block(1), block(2), block(0)]
        units += [_wide(a["w_xkv_2"][l][:, 512 * i:512 * i + 512]) for i in range(4)]
        units += [_tall(a["w_mix_out_2"][l])]
        units += [_wide(a["w_xq_2"][l][:, 512 * i:512 * i + 512]) for i in range(2)]
        units += [_tall(a["w_xo_2"][l])]
        units += ffn(a["w_ffn2_gu_2"][l], a["w_ffn2_down_2"][l])
    s = np.concatenate(units, 0)
    assert s.shape == (TOTAL, P, UNIT), s.shape
    return s


def _constants():
    q = np.arange(S)
    ok = q[None, :] <= q[:, None]
    dist = np.where(ok, (q[None, :] - q[:, None]).astype(np.float32), np.float32(NEG))
    mask = np.where(ok, np.float32(0), np.float32(NEG))

    def tri(m):
        return np.concatenate([m[0:P, 0:P], m[P:S, :]], 1)

    upto = ok.T[0:P, :].astype(np.float32)
    cst = np.concatenate([np.eye(P, dtype=np.float32), tri(dist), tri(mask), upto], 1)
    mats = []
    for w in POOL_WINDOWS:
        count = np.minimum(q + 1, w).astype(np.float32)
        m = np.where(ok & (q[:, None] - q[None, :] < w), np.float32(1) / count[:, None], np.float32(0))
        m = (m - np.eye(S, dtype=np.float32)).T
        mats.append(np.concatenate([m[0:P, :], m[P:S, P:S]], 1))
    sel = np.zeros((P, HEADS, P), np.float32)
    for h in range(HEADS):
        sel[h, h, :] = sel[32 + h, h, :] = 1
    return cst, sel, np.concatenate(mats, 1).astype(np.float32)


def kernel(**a):
    import concourse.bacc as bacc
    from concourse.bass_utils import run_bass_kernel_spmd

    cst, sel, poolmat = _constants()
    a = {k: np.asarray(v) for k, v in a.items()}
    group = [_columns(a["norm_mix_pre"][0]), _columns(a["norm_mlp_pre"][0]), _columns(a["pool_scale"][0])]
    for l in range(LAYERS):
        group += [_columns(a[n][l]) for n in ("g_ffn1_2", "g_mix_2", "g_mem_2", "g_xattn_2", "g_ffn2_2",
                                              "g_conv_out_2", "g_att_out_2")]
        group += [_columns(a["w_conv_2"][l].reshape(-1)), np.broadcast_to(a["b_f_2"][l], (P, HEADS))]
    rows = lambda v: np.broadcast_to(v.reshape(1, -1), (P, v.size))
    arrays = {
        "x": a["x"].reshape(TOK, P, D).transpose(1, 0, 2),
        "mem": a["mem_2"].reshape(TOK, P, D).transpose(1, 0, 2),
        "stream": _stream(a),
        "cols": np.concatenate(group, 1),
        "consts": cst,
        "sel": sel,
        "poolmat": poolmat,
        "poolw": a["pool_w"][0].transpose(1, 0, 2),
        "gate_bias": rows(a["b_gate"][0]),
        "post_gain": rows(np.concatenate([a["norm_mix_post"][0], a["norm_mlp_post"][0]])),
        "final_gain": rows(a["g_final_2"]),
    }
    arrays = {f"{k}_in": np.ascontiguousarray(v) for k, v in arrays.items()}
    nc = bacc.Bacc("TRN2", target_bir_lowering=False, num_devices=1)
    aps = [nc.dram_tensor(k, v.shape, F32, kind="ExternalInput").ap() for k, v in arrays.items()]
    out = nc.dram_tensor("out", (TOK, P, D), F32, kind="ExternalOutput").ap()
    program(nc, *aps, out)
    r = run_bass_kernel_spmd(nc, [arrays], core_ids=[0])
    return r.results[0]["out"].reshape(1, S, D)
```
